# Optimizing a Trainium2 kernel written in Bass

```python
import math
import jax, jax.numpy as jnp
from jax import lax
import numpy as np
import jax
import jax.numpy as jnp

D_MODEL = 1024
BATCH = 1
SEQ = 256
DEPTH = 1

HEAD_DIM = 64
DIL_GROUPS = ((128, 1), (512, 4), (2048, 16))
A_HEADS_PER_GROUP = 4
A_HEADS = A_HEADS_PER_GROUP * len(DIL_GROUPS)
A_OUT = A_HEADS_PER_GROUP * HEAD_DIM
B_HEADS = 4
B_V_DIM = 2 * HEAD_DIM
B_OUT = B_HEADS * B_V_DIM
C_HEADS = 4
C_OUT = C_HEADS * HEAD_DIM
IDX_HEADS = 8
IDX_DIM = 64
TOPK_MAX = 256
D_FF = 2816
NUM_BUCKETS = 32
MAX_DISTANCE = 2048
BIAS_HEADS = A_HEADS + B_HEADS + C_HEADS
Q_BLOCK = 128
RMS_EPS = 1e-6

A_QKV_COLS = 3 * A_HEADS * HEAD_DIM
B_QK_COLS = 4 * B_HEADS * HEAD_DIM
B_V_COLS = B_HEADS * B_V_DIM
C_COLS = C_HEADS * HEAD_DIM + 2 * HEAD_DIM
IDX_COLS = IDX_HEADS * IDX_DIM + IDX_DIM + IDX_HEADS
GATE_COLS = 3 * D_MODEL
N_IN = A_QKV_COLS + B_QK_COLS + B_V_COLS + C_COLS + IDX_COLS + GATE_COLS
SPLIT_POINTS = [A_QKV_COLS,
                A_QKV_COLS + B_QK_COLS,
                A_QKV_COLS + B_QK_COLS + B_V_COLS,
                A_QKV_COLS + B_QK_COLS + B_V_COLS + C_COLS,
                A_QKV_COLS + B_QK_COLS + B_V_COLS + C_COLS + IDX_COLS]


def rms_norm(x, g):
    xf = x.astype(jnp.float32)
    y = xf * lax.rsqrt(jnp.mean(xf * xf, axis=-1, keepdims=True) + RMS_EPS)
    return (y * g.astype(jnp.float32)).astype(x.dtype)

def swiglu(x, w_gate, w_up, w_down):
    return (jax.nn.silu(x @ w_gate) * (x @ w_up)) @ w_down

def rel_bucket(dist):
    n = jnp.maximum(dist, 0)
    max_exact = NUM_BUCKETS // 2
    nf = jnp.maximum(n, 1).astype(jnp.float32)
    large = max_exact + (jnp.log(nf / max_exact) / math.log(MAX_DISTANCE / max_exact)
                         * (NUM_BUCKETS - max_exact)).astype(jnp.int32)
    large = jnp.minimum(large, NUM_BUCKETS - 1)
    return jnp.where(n < max_exact, n, large)

def dilated_window_group(q, k, v, window, dilation, bias_table):
    b, t, h, dh = q.shape
    n = t // dilation
    wn = window // dilation
    nb = -(-n // wn)
    pad = nb * wn - n

    def to_sub(z):
        z = z.reshape(b, n, dilation, h, dh).transpose(0, 2, 1, 3, 4)
        return jnp.pad(z, ((0, 0), (0, 0), (0, pad), (0, 0), (0, 0)))

    qs, ks, vs = to_sub(q), to_sub(k), to_sub(v)
    qb = qs.reshape(b, dilation, nb, wn, h, dh)

    def band(z):
        zp = jnp.pad(z, ((0, 0), (0, 0), (wn, 0), (0, 0), (0, 0))).reshape(b, dilation, nb + 1, wn, h, dh)
        return jnp.concatenate([zp[:, :, :-1], zp[:, :, 1:]], axis=3)

    kb, vb = band(ks), band(vs)
    logits = jnp.einsum('brnqhe,brnkhe->brnhqk', qb, kb).astype(jnp.float32) * (dh ** -0.5)
    a = jnp.arange(wn)[:, None]
    c = jnp.arange(2 * wn)[None, :]
    sub_dist = wn + a - c
    bias = bias_table[rel_bucket(sub_dist * dilation)].astype(jnp.float32)
    logits = logits + bias.transpose(2, 0, 1)
    key_pos = (jnp.arange(nb)[:, None] - 1) * wn + c
    mask = ((sub_dist >= 0) & (sub_dist <= wn))[None] & (key_pos >= 0)[:, None, :]
    logits = jnp.where(mask[:, None], logits, -jnp.inf)
    m = jnp.max(logits, axis=-1)
    p = jnp.exp(logits - m[..., None])
    s = jnp.sum(p, axis=-1)
    o = jnp.einsum('brnhqk,brnkhe->brnqhe', p, vb.astype(jnp.float32))

    def from_sub(z):
        z = z.reshape((b, dilation, nb * wn) + z.shape[4:])[:, :, :n]
        z = jnp.moveaxis(z, 1, 2)
        return z.reshape((b, t) + z.shape[3:])

    return from_sub(o), from_sub(jnp.swapaxes(m, 3, 4)), from_sub(jnp.swapaxes(s, 3, 4))

def dilated_attention(q, k, v, bias_table):
    outs = []
    for g, (w, d) in enumerate(DIL_GROUPS):
        sl = slice(g * A_HEADS_PER_GROUP, (g + 1) * A_HEADS_PER_GROUP)
        outs.append(dilated_window_group(q[:, :, sl], k[:, :, sl], v[:, :, sl], w, d, bias_table[:, sl]))
    m_all = jnp.stack([m for _, m, _ in outs])
    scale = jnp.exp(m_all - jnp.max(m_all, axis=0))
    num = sum(scale[g][..., None] * outs[g][0] for g in range(len(DIL_GROUPS)))
    den = sum(scale[g] * outs[g][2] for g in range(len(DIL_GROUPS)))
    return num / den[..., None]

def diff_attention(qs, ks, v, lam, bias_table):
    t = qs.shape[1]
    dh = qs.shape[-1]
    outs = []
    for start in range(0, t, Q_BLOCK):
        end = start + Q_BLOCK
        logits = jnp.einsum('bqmhe,bkmhe->bmhqk', qs[:, start:end], ks[:, :end]).astype(jnp.float32) * (dh ** -0.5)
        dist = jnp.arange(start, end)[:, None] - jnp.arange(end)[None, :]
        bias = bias_table[rel_bucket(dist)].astype(jnp.float32).transpose(2, 0, 1)
        logits = jnp.where(dist >= 0, logits + bias, -jnp.inf)
        p = jax.nn.softmax(logits, axis=-1)
        w = p[:, 0] - lam * p[:, 1]
        outs.append(jnp.einsum('bhqk,bkhe->bqhe', w, v[:, :end].astype(jnp.float32)))
    return jnp.concatenate(outs, axis=1)

def dsa_attention(q, k, v, q_idx, k_idx, w_idx, bias_table):
    t = q.shape[1]
    dh = q.shape[-1]
    k_sel = min(TOPK_MAX, t // 4)
    gather = jax.vmap(lambda z, i: z[i])
    outs = []
    for start in range(0, t, Q_BLOCK):
        end = start + Q_BLOCK
        n_sel = min(k_sel, end)
        qpos = jnp.arange(start, end)
        raw = jnp.einsum('bqhe,bke->bqhk', q_idx[:, start:end], k_idx[:, :end]).astype(jnp.float32) * (IDX_DIM ** -0.5)
        score = jnp.einsum('bqh,bqhk->bqk', w_idx[:, start:end].astype(jnp.float32) * (IDX_HEADS ** -0.5),
                           jax.nn.relu(raw))
        score = jnp.where(jnp.arange(end)[None, :] <= qpos[:, None], score, -jnp.inf)
        top_val, top_idx = lax.top_k(score, n_sel)
        valid = jnp.isfinite(top_val)
        k_g = gather(k[:, :end], top_idx)
        v_g = gather(v[:, :end], top_idx)
        logits = jnp.einsum('bqhe,bqne->bhqn', q[:, start:end], k_g).astype(jnp.float32) * (dh ** -0.5)
        bias = bias_table[rel_bucket(qpos[None, :, None] - top_idx)].astype(jnp.float32)
        logits = jnp.where(valid[:, None], logits + jnp.moveaxis(bias, 3, 1), -jnp.inf)
        p = jax.nn.softmax(logits, axis=-1)
        outs.append(jnp.einsum('bhqn,bqne->bqhe', p, v_g.astype(jnp.float32)))
    return jnp.concatenate(outs, axis=1)

def token_mixer(h, w_in, qk_gain, diff_lambda, diff_out_norm, w_branch_a, w_branch_b, w_branch_c,
                w_out, rel_bias, layer_idx):
    b, t, _ = h.shape
    proj = h @ w_in
    a_qkv, b_qk, b_v, c_qkv, ix, gates = jnp.split(proj, SPLIT_POINTS, axis=-1)

    a_qkv = a_qkv.reshape(b, t, 3, A_HEADS, HEAD_DIM)
    qa = rms_norm(a_qkv[:, :, 0], qk_gain[0, 0])
    ka = rms_norm(a_qkv[:, :, 1], qk_gain[0, 1])
    o_a = dilated_attention(qa, ka, a_qkv[:, :, 2], rel_bias[:, :A_HEADS])
    o_a = o_a.reshape(b, t, A_OUT).astype(h.dtype)

    b_qk = b_qk.reshape(b, t, 4, B_HEADS, HEAD_DIM)
    qb = rms_norm(b_qk[:, :, 0:2], qk_gain[1, 0])
    kb = rms_norm(b_qk[:, :, 2:4], qk_gain[1, 1])
    lam_init = 0.8 - 0.6 * math.exp(-0.3 * layer_idx)
    lv = diff_lambda.astype(jnp.float32)
    lam = jnp.exp(jnp.sum(lv[0] * lv[1])) - jnp.exp(jnp.sum(lv[2] * lv[3])) + lam_init
    o_b = diff_attention(qb, kb, b_v.reshape(b, t, B_HEADS, B_V_DIM), lam, rel_bias[:, A_HEADS:A_HEADS + B_HEADS])
    o_b = rms_norm(o_b, diff_out_norm) * (1.0 - lam_init)
    o_b = o_b.reshape(b, t, B_OUT).astype(h.dtype)

    qc = rms_norm(c_qkv[..., :C_HEADS * HEAD_DIM].reshape(b, t, C_HEADS, HEAD_DIM), qk_gain[2, 0])
    kc = rms_norm(c_qkv[..., C_HEADS * HEAD_DIM:C_HEADS * HEAD_DIM + HEAD_DIM], qk_gain[2, 1])
    vc = c_qkv[..., C_HEADS * HEAD_DIM + HEAD_DIM:]
    q_idx = ix[..., :IDX_HEADS * IDX_DIM].reshape(b, t, IDX_HEADS, IDX_DIM)
    k_idx = ix[..., IDX_HEADS * IDX_DIM:IDX_HEADS * IDX_DIM + IDX_DIM]
    w_idx = ix[..., IDX_HEADS * IDX_DIM + IDX_DIM:]
    o_c = dsa_attention(qc, kc, vc, q_idx, k_idx, w_idx, rel_bias[:, A_HEADS + B_HEADS:])
    o_c = o_c.reshape(b, t, C_OUT).astype(h.dtype)

    g = jax.nn.sigmoid(gates.reshape(b, t, 3, D_MODEL))
    y = (g[:, :, 0] * (o_a @ w_branch_a) + g[:, :, 1] * (o_b @ w_branch_b)
         + g[:, :, 2] * (o_c @ w_branch_c))
    return y @ w_out

def first_inputs(seed: int = 0) -> dict:
    key = jax.random.key(seed)
    ks = jax.random.split(key, 20)
    f32 = jnp.float32

    def dense(k, shape, fan_in):
        return jax.random.normal(k, shape, f32) * fan_in ** -0.5

    def gain(k, shape):
        return 1.0 + 0.05 * jax.random.normal(k, shape, f32)

    return {
        "x": jax.random.normal(ks[0], (BATCH, SEQ, D_MODEL), f32),
        "rel_bias": 0.5 * jax.random.normal(ks[1], (NUM_BUCKETS, BIAS_HEADS), f32),
        "ffn1_norm": gain(ks[2], (DEPTH, D_MODEL)),
        "ffn1_w_gate": dense(ks[3], (DEPTH, D_MODEL, D_FF), D_MODEL),
        "ffn1_w_up": dense(ks[4], (DEPTH, D_MODEL, D_FF), D_MODEL),
        "ffn1_w_down": dense(ks[5], (DEPTH, D_FF, D_MODEL), D_FF),
        "mix_norm": gain(ks[6], (DEPTH, D_MODEL)),
        "w_in": dense(ks[7], (DEPTH, D_MODEL, N_IN), D_MODEL),
        "qk_gain": gain(ks[8], (DEPTH, 3, 2, HEAD_DIM)),
        "diff_lambda": 0.1 * jax.random.normal(ks[9], (DEPTH, 4, HEAD_DIM), f32),
        "diff_out_norm": gain(ks[10], (DEPTH, B_V_DIM)),
        "w_branch_a": dense(ks[11], (DEPTH, A_OUT, D_MODEL), A_OUT),
        "w_branch_b": dense(ks[12], (DEPTH, B_OUT, D_MODEL), B_OUT),
        "w_branch_c": dense(ks[13], (DEPTH, C_OUT, D_MODEL), C_OUT),
        "w_out": dense(ks[14], (DEPTH, D_MODEL, D_MODEL), D_MODEL),
        "ffn2_norm": gain(ks[15], (DEPTH, D_MODEL)),
        "ffn2_w_gate": dense(ks[16], (DEPTH, D_MODEL, D_FF), D_MODEL),
        "ffn2_w_up": dense(ks[17], (DEPTH, D_MODEL, D_FF), D_MODEL),
        "ffn2_w_down": dense(ks[18], (DEPTH, D_FF, D_MODEL), D_FF),
    }

def first_block(x, rel_bias, ffn1_norm, ffn1_w_gate, ffn1_w_up, ffn1_w_down, mix_norm, w_in, qk_gain,
              diff_lambda, diff_out_norm, w_branch_a, w_branch_b, w_branch_c, w_out,
              ffn2_norm, ffn2_w_gate, ffn2_w_up, ffn2_w_down):
    for i in range(DEPTH):
        x = x + 0.5 * swiglu(rms_norm(x, ffn1_norm[i]), ffn1_w_gate[i], ffn1_w_up[i], ffn1_w_down[i])
        x = x + token_mixer(rms_norm(x, mix_norm[i]), w_in[i], qk_gain[i], diff_lambda[i], diff_out_norm[i],
                            w_branch_a[i], w_branch_b[i], w_branch_c[i], w_out[i], rel_bias, i)
        x = x + 0.5 * swiglu(rms_norm(x, ffn2_norm[i]), ffn2_w_gate[i], ffn2_w_up[i], ffn2_w_down[i])
    return x


CTX_LEN = 256
GRID_W = 64

HY_WIDTH = 512
HY_BANDS = 16
HY_EMB = 2 * HY_BANDS + 1
HY_FILTER_ORDER = 64
HY_DECAY_TARGET = 1e-2
HY_DECAY_SHORT = 0.3
HY_DECAY_LONG = 1.5

RW_HEADS = 8
RW_HEAD = 64
RW_WIDTH = RW_HEADS * RW_HEAD
LORA_W = 64
LORA_A = 64
LORA_G = 128
RW_LN_EPS = 64e-5
SCAN_DIRECTIONS = (False, True)

HY_COLS = 3 * HY_WIDTH
RW_COLS = 3 * RW_WIDTH + LORA_W + LORA_A + LORA_G
GATE_COLS_2 = 2 * D_MODEL
IN_COLS = HY_COLS + RW_COLS + GATE_COLS_2
RW_SPLITS = (RW_WIDTH, 2 * RW_WIDTH, 3 * RW_WIDTH, 3 * RW_WIDTH + LORA_W, 3 * RW_WIDTH + LORA_W + LORA_A)
STATE_LO = RW_WIDTH
STATE_HI = 3 * RW_WIDTH + LORA_W + LORA_A

N_EXPERTS = 16
D_EXPERT = 2048
EC_CAPACITY = 2
NORM_EPS = 1e-6


def rmsnorm(x, g):
    x32 = x.astype(jnp.float32)
    y = x32 * lax.rsqrt(jnp.mean(x32 * x32, axis=-1, keepdims=True) + NORM_EPS)
    return y.astype(x.dtype) * g

def modulation(cvec, p):
    return jnp.split(jax.nn.silu(cvec) @ p['mod_w'] + p['mod_b'], 6, axis=-1)

def shift_prev(z):
    return jnp.pad(z, ((0, 0), (1, 0), (0, 0)))[:, :-1]

def shift_next(z):
    return jnp.pad(z, ((0, 0), (0, 1), (0, 0)))[:, 1:]

def centred_mix(z, mu):
    return z + mu[0] * (shift_prev(z) - z) + mu[1] * (shift_next(z) - z)

def heads(z):
    return z.reshape(z.shape[:-1] + (RW_HEADS, RW_HEAD))

def hyena_filter_spectrum(L, p):
    f32 = jnp.float32
    t = jnp.linspace(0.0, 1.0, L, dtype=f32)[:, None]
    ang = (2.0 * math.pi / L) * jnp.arange(L, dtype=f32)[:, None]
    bands = jnp.linspace(1e-4, HY_BANDS - 1, HY_BANDS, dtype=f32)
    feat = jnp.concatenate([t, jnp.cos(bands * ang), -jnp.sin(bands * ang)], axis=-1)
    freq = p['hy_freq'].astype(f32)
    hid = jnp.sin(freq * (feat @ p['hy_ffn_w1'].astype(f32) + p['hy_ffn_b1'].astype(f32)))
    hid = jnp.sin(freq * (hid @ p['hy_ffn_w2'].astype(f32) + p['hy_ffn_b2'].astype(f32)))
    filt = (hid @ p['hy_ffn_w3'].astype(f32)).reshape(L, 2, HY_WIDTH)
    deltas = jnp.abs(jnp.linspace(math.log(HY_DECAY_TARGET) / HY_DECAY_LONG,
                                  math.log(HY_DECAY_TARGET) / HY_DECAY_SHORT, HY_WIDTH, dtype=f32))
    filt = filt * jnp.exp(-t[:, :, None] * deltas)
    circ = jnp.concatenate([filt[:, 0], jnp.zeros((1, HY_WIDTH), f32), filt[:0:-1, 1]], axis=0)
    circ = circ / jnp.sum(jnp.abs(circ), axis=0, keepdims=True)
    return jnp.fft.rfft(circ, axis=0)

def long_conv(z, spec):
    L = z.shape[1]
    zf = jnp.fft.rfft(z.astype(jnp.float32), n=2 * L, axis=1)
    return jnp.fft.irfft(zf * spec, n=2 * L, axis=1)[:, :L].astype(z.dtype)

def hyena_branch(cols, p):
    w = p['hy_conv_w']
    u = w[0] * shift_prev(cols) + w[1] * cols + w[2] * shift_next(cols) + p['hy_conv_b']
    x0, x1, v = jnp.split(u, 3, axis=-1)
    z = v * x1
    z = long_conv(z, hyena_filter_spectrum(cols.shape[1], p)) + p['hy_bias'] * z
    return z * x0

def rwkv_direction(k, lw, la, p, d):
    w = -jax.nn.softplus(-(p['rw_w0'][d] + jnp.tanh(lw) @ p['rw_w_up'][d])) - 0.5
    decay = jnp.exp(-jnp.exp(w.astype(jnp.float32)))
    a = jax.nn.sigmoid(p['rw_a0'][d] + la @ p['rw_a_up'][d])
    kk = heads(k * p['rw_k_k']).astype(jnp.float32)
    kk = kk * lax.rsqrt(jnp.maximum(jnp.sum(kk * kk, axis=-1, keepdims=True), 1e-24))
    k_mod = heads(k * (1.0 + (a - 1.0) * p['rw_k_a']))
    return heads(decay), k_mod, -kk, kk * heads(a).astype(jnp.float32)

def rwkv_scan(decay, k, v, a_vec, b_vec, r, state0, reverse):
    emit = r is not None
    xs = (decay, k, v, a_vec, b_vec) + ((r,) if emit else ())
    xs = tuple(jnp.moveaxis(t.astype(jnp.float32), 1, 0) for t in xs)

    def step(S, inp):
        w_t, k_t, v_t, a_t, b_t = inp[:5]
        sa = jnp.einsum('bhij,bhj->bhi', S, a_t)
        S = S * w_t[:, :, None, :] + sa[..., None] * b_t[:, :, None, :] + v_t[..., None] * k_t[:, :, None, :]
        y = jnp.einsum('bhij,bhj->bhi', S, inp[5]) if emit else None
        return S, y

    S, ys = lax.scan(step, state0, xs, reverse=reverse)
    return S, (jnp.moveaxis(ys, 0, 1) if emit else None)

def head_groupnorm(y, g, b):
    y32 = y.astype(jnp.float32)
    mu = jnp.mean(y32, axis=-1, keepdims=True)
    var = jnp.mean(jnp.square(y32 - mu), axis=-1, keepdims=True)
    yn = (y32 - mu) * lax.rsqrt(var + RW_LN_EPS)
    return yn.reshape(y.shape[:-2] + (RW_WIDTH,)).astype(g.dtype) * g + b

def rwkv_branch(cols, p, states0):
    z = centred_mix(cols, p['rw_mu'])
    r, k, v, lw, la, lg = jnp.split(z, RW_SPLITS, axis=-1)
    r_h, v_h = heads(r), heads(v)
    outs, bonuses, finals = [], [], []
    for d, reverse in enumerate(SCAN_DIRECTIONS):
        decay, k_mod, a_vec, b_vec = rwkv_direction(k, lw, la, p, d)
        S, y_d = rwkv_scan(decay, k_mod, v_h, a_vec, b_vec, r_h, states0[d], reverse)
        outs.append(y_d)
        finals.append(S)
        bonuses.append(jnp.sum(r_h * k_mod * p['rw_r_k'], axis=-1, keepdims=True) * v_h)
    y = head_groupnorm(outs[0] + outs[1], p['rw_ln_g'], p['rw_ln_b'])
    y = y + (bonuses[0] + bonuses[1]).reshape(cols.shape[:-1] + (RW_WIDTH,))
    g = jax.nn.sigmoid(lg) @ p['rw_g_up']
    return y * g, finals

def rwkv_context_states(cols, p, state0):
    z = centred_mix(cols, p['rw_mu'][:, STATE_LO:STATE_HI])
    k, v, lw, la = jnp.split(z, (RW_WIDTH, 2 * RW_WIDTH, 2 * RW_WIDTH + LORA_W), axis=-1)
    v_h = heads(v)
    finals = []
    for d, reverse in enumerate(SCAN_DIRECTIONS):
        decay, k_mod, a_vec, b_vec = rwkv_direction(k, lw, la, p, d)
        S, _ = rwkv_scan(decay, k_mod, v_h, a_vec, b_vec, None, state0, reverse)
        finals.append(S)
    return finals

def token_mixer_2(h, p, states0):
    cols = h @ p['w_in']
    hy_cols, rw_cols, gate_cols = jnp.split(cols, (HY_COLS, HY_COLS + RW_COLS), axis=-1)
    y_hy = hyena_branch(hy_cols, p) @ p['hy_proj']
    y_rw, finals = rwkv_branch(rw_cols, p, states0)
    g_hy, g_rw = jnp.split(jax.nn.sigmoid(gate_cols), 2, axis=-1)
    mixed = (g_hy * y_hy + g_rw * (y_rw @ p['rw_proj'])) @ p['w_out']
    return mixed, finals

def expert_choice_moe(h, p):
    B, T, D = h.shape
    cap = EC_CAPACITY * T // N_EXPERTS
    affinity = jax.nn.softmax((h @ p['router_w']).astype(jnp.float32), axis=-1)
    gates, idx = lax.top_k(jnp.swapaxes(affinity, 1, 2), cap)
    xe = jax.vmap(lambda hb, ib: hb[ib])(h, idx)
    hid = jax.nn.silu(jnp.einsum('becd,edf->becf', xe, p['exp_w1'])) * jnp.einsum('becd,edf->becf', xe, p['exp_w3'])
    ye = jnp.einsum('becf,efd->becd', hid, p['exp_w2']) * gates[..., None].astype(h.dtype)
    return jax.vmap(lambda ib, yb: jnp.zeros((T, D), yb.dtype).at[ib.reshape(-1)].add(yb.reshape(-1, D)))(idx, ye)

def layer(x, ctx, c, c_ctx, p, ctx_out):
    m_lat = modulation(c[:, None, :], p)
    m_ctx = modulation(c_ctx, p)
    zero_state = jnp.zeros((ctx.shape[0], RW_HEADS, RW_HEAD, RW_HEAD), jnp.float32)
    h_ctx = rmsnorm(ctx, p['norm1_pre']) * (1.0 + m_ctx[1]) + m_ctx[0]
    if ctx_out:
        mixed_ctx, ctx_states = token_mixer_2(h_ctx, p, (zero_state, zero_state))
        ctx = ctx + m_ctx[2] * rmsnorm(mixed_ctx, p['norm1_post'])
        h2_ctx = rmsnorm(ctx, p['norm2_pre']) * (1.0 + m_ctx[4]) + m_ctx[3]
        ctx = ctx + m_ctx[5] * rmsnorm(expert_choice_moe(h2_ctx, p), p['norm2_post'])
    else:
        cols = h_ctx @ p['w_in'][:, HY_COLS + STATE_LO:HY_COLS + STATE_HI]
        ctx_states = rwkv_context_states(cols, p, zero_state)
    h = rmsnorm(x, p['norm1_pre']) * (1.0 + m_lat[1]) + m_lat[0]
    mixed, _ = token_mixer_2(h, p, ctx_states)
    x = x + m_lat[2] * rmsnorm(mixed, p['norm1_post'])
    h2 = rmsnorm(x, p['norm2_pre']) * (1.0 + m_lat[4]) + m_lat[3]
    x = x + m_lat[5] * rmsnorm(expert_choice_moe(h2, p), p['norm2_post'])
    return x, ctx

def second_inputs(seed: int = 0) -> dict:
    key = jax.random.key(seed)
    ks = iter(jax.random.split(key, 64))
    f32 = jnp.float32

    def nrm(shape, scale=1.0):
        return scale * jax.random.normal(next(ks), shape, f32)

    def unif(shape, lo, hi):
        return jax.random.uniform(next(ks), shape, f32, lo, hi)

    L, D, E = DEPTH, D_MODEL, N_EXPERTS
    return {
        'x': nrm((BATCH, SEQ, D)),
        'c': nrm((BATCH, D)),
        'ctx': nrm((BATCH, CTX_LEN, D)),
        'c_ctx': nrm((D,)),
        'mod_w': nrm((L, D, 6 * D), 0.5 * D ** -0.5),
        'mod_b': nrm((L, 6 * D), 0.02),
        'norm1_pre': 1.0 + nrm((L, D), 0.1),
        'norm1_post': 1.0 + nrm((L, D), 0.1),
        'norm2_pre': 1.0 + nrm((L, D), 0.1),
        'norm2_post': 1.0 + nrm((L, D), 0.1),
        'w_in': nrm((L, D, IN_COLS), D ** -0.5),
        'hy_conv_w': nrm((L, 3, HY_COLS), 0.5),
        'hy_conv_b': nrm((L, HY_COLS), 0.02),
        'hy_ffn_w1': nrm((L, HY_EMB, HY_FILTER_ORDER), HY_EMB ** -0.5),
        'hy_ffn_b1': nrm((L, HY_FILTER_ORDER), 0.1),
        'hy_ffn_w2': nrm((L, HY_FILTER_ORDER, HY_FILTER_ORDER), HY_FILTER_ORDER ** -0.5),
        'hy_ffn_b2': nrm((L, HY_FILTER_ORDER), 0.1),
        'hy_ffn_w3': nrm((L, HY_FILTER_ORDER, 2 * HY_WIDTH), HY_FILTER_ORDER ** -0.5),
        'hy_freq': 1.0 + nrm((L, HY_FILTER_ORDER), 0.1),
        'hy_bias': nrm((L, HY_WIDTH), 0.5),
        'hy_proj': nrm((L, HY_WIDTH, D), HY_WIDTH ** -0.5),
        'rw_mu': unif((L, 2, RW_COLS), 0.0, 0.5),
        'rw_w0': unif((L, 2, RW_WIDTH), -6.0, 0.0),
        'rw_w_up': nrm((L, 2, LORA_W, RW_WIDTH), 0.1),
        'rw_a0': nrm((L, 2, RW_WIDTH), 0.3),
        'rw_a_up': nrm((L, 2, LORA_A, RW_WIDTH), 0.1),
        'rw_g_up': nrm((L, LORA_G, RW_WIDTH), LORA_G ** -0.5),
        'rw_k_k': 0.85 + nrm((L, RW_WIDTH), 0.1),
        'rw_k_a': 1.0 + nrm((L, RW_WIDTH), 0.1),
        'rw_r_k': nrm((L, RW_HEADS, RW_HEAD), 0.1),
        'rw_ln_g': 1.0 + nrm((L, RW_WIDTH), 0.1),
        'rw_ln_b': nrm((L, RW_WIDTH), 0.02),
        'rw_proj': nrm((L, RW_WIDTH, D), RW_WIDTH ** -0.5),
        'w_out': nrm((L, D, D), D ** -0.5),
        'router_w': nrm((L, D, E), D ** -0.5),
        'exp_w1': nrm((L, E, D, D_EXPERT), D ** -0.5),
        'exp_w3': nrm((L, E, D, D_EXPERT), D ** -0.5),
        'exp_w2': nrm((L, E, D_EXPERT, D), D_EXPERT ** -0.5),
    }

def second_block(x, c, ctx, c_ctx, mod_w, mod_b, norm1_pre, norm1_post, norm2_pre, norm2_post, w_in,
              hy_conv_w, hy_conv_b, hy_ffn_w1, hy_ffn_b1, hy_ffn_w2, hy_ffn_b2, hy_ffn_w3, hy_freq,
              hy_bias, hy_proj, rw_mu, rw_w0, rw_w_up, rw_a0, rw_a_up, rw_g_up, rw_k_k, rw_k_a,
              rw_r_k, rw_ln_g, rw_ln_b, rw_proj, w_out, router_w, exp_w1, exp_w3, exp_w2):
    for l in range(DEPTH):
        p = {
            'mod_w': mod_w[l], 'mod_b': mod_b[l],
            'norm1_pre': norm1_pre[l], 'norm1_post': norm1_post[l],
            'norm2_pre': norm2_pre[l], 'norm2_post': norm2_post[l],
            'w_in': w_in[l],
            'hy_conv_w': hy_conv_w[l], 'hy_conv_b': hy_conv_b[l],
            'hy_ffn_w1': hy_ffn_w1[l], 'hy_ffn_b1': hy_ffn_b1[l],
            'hy_ffn_w2': hy_ffn_w2[l], 'hy_ffn_b2': hy_ffn_b2[l],
            'hy_ffn_w3': hy_ffn_w3[l], 'hy_freq': hy_freq[l],
            'hy_bias': hy_bias[l], 'hy_proj': hy_proj[l],
            'rw_mu': rw_mu[l], 'rw_w0': rw_w0[l], 'rw_w_up': rw_w_up[l],
            'rw_a0': rw_a0[l], 'rw_a_up': rw_a_up[l], 'rw_g_up': rw_g_up[l],
            'rw_k_k': rw_k_k[l], 'rw_k_a': rw_k_a[l], 'rw_r_k': rw_r_k[l],
            'rw_ln_g': rw_ln_g[l], 'rw_ln_b': rw_ln_b[l], 'rw_proj': rw_proj[l],
            'w_out': w_out[l], 'router_w': router_w[l],
            'exp_w1': exp_w1[l], 'exp_w3': exp_w3[l], 'exp_w2': exp_w2[l],
        }
        x, ctx = layer(x, ctx, c, c_ctx, p, l < DEPTH - 1)
    return x


def setup_inputs(seed=0):
    out = dict(first_inputs(seed))
    for name, value in second_inputs(seed + 1).items():
        if name != "x":
            out[name + "_2"] = value
    return out


def reference(
    x, rel_bias, ffn1_norm, ffn1_w_gate, ffn1_w_up, ffn1_w_down, mix_norm, w_in, qk_gain,
    diff_lambda, diff_out_norm, w_branch_a, w_branch_b, w_branch_c, w_out, ffn2_norm,
    ffn2_w_gate, ffn2_w_up, ffn2_w_down, c_2, ctx_2, c_ctx_2, mod_w_2, mod_b_2, norm1_pre_2,
    norm1_post_2, norm2_pre_2, norm2_post_2, w_in_2, hy_conv_w_2, hy_conv_b_2, hy_ffn_w1_2,
    hy_ffn_b1_2, hy_ffn_w2_2, hy_ffn_b2_2, hy_ffn_w3_2, hy_freq_2, hy_bias_2, hy_proj_2,
    rw_mu_2, rw_w0_2, rw_w_up_2, rw_a0_2, rw_a_up_2, rw_g_up_2, rw_k_k_2, rw_k_a_2, rw_r_k_2,
    rw_ln_g_2, rw_ln_b_2, rw_proj_2, w_out_2, router_w_2, exp_w1_2, exp_w3_2, exp_w2_2,
):
    x = first_block(
        x, rel_bias, ffn1_norm, ffn1_w_gate, ffn1_w_up, ffn1_w_down, mix_norm, w_in, qk_gain,
        diff_lambda, diff_out_norm, w_branch_a, w_branch_b, w_branch_c, w_out, ffn2_norm,
        ffn2_w_gate, ffn2_w_up, ffn2_w_down,
    )
    return second_block(
        x, c_2, ctx_2, c_ctx_2, mod_w_2, mod_b_2, norm1_pre_2, norm1_post_2, norm2_pre_2,
        norm2_post_2, w_in_2, hy_conv_w_2, hy_conv_b_2, hy_ffn_w1_2, hy_ffn_b1_2, hy_ffn_w2_2,
        hy_ffn_b2_2, hy_ffn_w3_2, hy_freq_2, hy_bias_2, hy_proj_2, rw_mu_2, rw_w0_2, rw_w_up_2,
        rw_a0_2, rw_a_up_2, rw_g_up_2, rw_k_k_2, rw_k_a_2, rw_r_k_2, rw_ln_g_2, rw_ln_b_2,
        rw_proj_2, w_out_2, router_w_2, exp_w1_2, exp_w3_2, exp_w2_2,
    )


_drawn_inputs = setup_inputs


def setup_inputs(seed=0):
    import zlib

    import numpy as np

    out = dict(_drawn_inputs(seed))
    spreads = {}
    factors = {'diff_lambda': 3.464,
     'hy_conv_b_2': 3.187,
     'hy_ffn_b1_2': 4.201,
     'hy_ffn_b2_2': 2.736,
     'hy_freq_2': 7.518,
     'rw_ln_b_2': 7.163}
    for name, (base, spread) in spreads.items():
        noise = np.random.default_rng([zlib.crc32(name.encode()), seed]).standard_normal(out[name].shape)
        drawn = base * np.exp(spread * noise) if base else spread * noise
        out[name] = jnp.asarray(drawn.astype(out[name].dtype))
    for name, factor in factors.items():
        out[name] = (out[name] * factor).astype(out[name].dtype)
    return out
```

```python
import math
from contextlib import ExitStack

import concourse.bass as bass
import numpy as np
from concourse import mybir

P = 128
T = 256
TT = T // P
D = 1024
KC = D // P
D_FF = 2816
FC = D_FF // P
HD = 64
N_IN = 7880
A_COL, BQK_COL, BV_COL, C_COL, IX_COL, GATE_COL = 0, 2304, 3328, 3840, 4224, 4808
A_HEADS, B_HEADS, C_HEADS, IDX_HEADS = 12, 4, 4, 8
BIAS_HEADS = 20
NUM_BUCKETS, MAX_DISTANCE = 32, 2048
TOP_KEYS = 64
LAM_INIT = 0.8 - 0.6 * math.exp(-0.3 * 0)
EPS = 1e-6
MASKED = -1e30
HY_COLS, RW_COLS, GATE2_COLS = 1536, 1792, 2048
IN2_COLS = HY_COLS + RW_COLS + GATE2_COLS
HYC, RWC = HY_COLS // P, RW_COLS // P
RW_WIDTH = 512
STATE_LO, STATE_HI = RW_WIDTH, 3 * RW_WIDTH + 128
HY_W = 512
NE, CAP, D_EXP = 16, 32, 2048
DIST = 383

ALU = mybir.AluOpType
ACT = mybir.ActivationFunctionType
F32 = mybir.dt.float32
AX_X = mybir.AxisListType.X
AX_XY = mybir.AxisListType.XY

WT = 2048
R = 6


class Stream:

    def __init__(self):
        self.src, self.first = [], {}

    def mark(self, name):
        self.first[name] = len(self.src)

    def columns(self, name, w, c0, c1):
        self.mark(name)
        for c in range(c0, c1, 256):
            n = min(256, c1 - c)
            self.src.append((KC * n, w[:, c:c + n].rearrange("(k p) n -> p k n", p=P)))

    def rows(self, name, w, pairs=None):
        self.mark(name)
        chunks = w.rearrange("(k p) n -> p k n", p=P)
        k = chunks.shape[1]
        step = 1 if pairs is None else k // 2
        for i in range(k // 2):
            lo = 2 * i if pairs is None else i
            self.src.append((WT, chunks[:, lo:lo + step + 1:step, :]))


VEC_A = ["ffn1_norm", "mix_norm", "ffn2_norm", "norm1_pre_2", "norm2_pre_2", "c_2", "c_ctx_2", "mod_b_2",
         "diff_out_norm", "qk_gain"]
VEC_A_ROWS = [8, 8, 8, 8, 8, 8, 8, 48, 1, 6]
VEC_B = ["hy_conv_w_2", "hy_conv_b_2", "hy_bias_2", "rw_mu_2", "rw_w0_2", "rw_a0_2", "rw_k_k_2", "rw_k_a_2", "rw_r_k_2"]
VEC_B_ROWS = [36, 12, 4, 28, 8, 8, 4, 4, 4]
ROW_A = {n: sum(VEC_A_ROWS[:i]) for i, n in enumerate(VEC_A)}
ROW_B = {n: sum(VEC_B_ROWS[:i]) for i, n in enumerate(VEC_B)}
HY64_ROW = sum(VEC_A_ROWS)
NA, NB = HY64_ROW + 3, sum(VEC_B_ROWS)


class Sems:

    def __init__(self, nc, ctx, phase):
        self.nc, self.ctx, self.phase, self.made = nc, ctx, phase, {}
        ctx.callback(self.clear)

    def clear(self):
        for sem in self.made.values():
            self.nc.gpsimd.sem_clear(sem)
            self.nc.release_semaphore(sem)

    def __getitem__(self, name):
        if name not in self.made:
            self.made[name] = self.nc.alloc_semaphore(f"{self.phase}_{name}")
        return self.made[name]


class Chain:

    def __init__(self, eng, sem):
        self.eng, self.sem, self.n = eng, sem, 0

    def __call__(self, ins):
        self.n += 1
        ins.then_inc(self.sem, 1)
        self.eng.wait_ge(self.sem, self.n)

    def add(self, ins):
        self.n += 1
        ins.then_inc(self.sem, 1)

    def sync(self):
        self.eng.wait_ge(self.sem, self.n)


class G:
    pass


def load_tiles(g, sp, upto):
    while g.issued < min(upto, len(g.stream.src)):
        i = g.issued
        if i >= R:
            sp.wait_ge(g.tiles_used, i - R + 1)
        n, src = g.stream.src[i]
        dst = g.ring[:, i % R, 0:n]
        if len(src.shape) == 3:
            dst = dst.rearrange("p (k n) -> p k n", k=src.shape[1])
        sp.dma_start(dst, src).then_inc(g.tile_loaded[i % R], 16)
        g.issued += 1


def wait_tile(g, pe, i):
    pe.wait_ge(g.tile_loaded[i % R], 16 * (i // R + 1))


def tile3(g, i, k):
    n = g.stream.src[i][0]
    return g.ring[:, i % R, 0:n].rearrange("p (k n) -> p k n", k=k)


def rms_transposed(g, nc, S, src, dst, gain, shift=None):
    xn, ss, ps = g.xn, g.ss, g.ps

    def act(eng):
        for t in range(TT):
            nc.scalar.activation(xn[:, t], src[:, t], ACT.Square, accum_out=ss[:, t:t + 1]).then_inc(S["squares"], 1)
        eng.wait_ge(S["mean"], 1)
        nc.scalar.activation(ss[:, 4:6], ss[:, 2:4], ACT.Sqrt).then_inc(S["root"], 1)

    def dve(eng, ch):
        eng.wait_ge(S["squares"], TT)
        nc.vector.tensor_scalar(ss[:, 2:4], ss[:, 0:2], 1.0 / D, EPS, ALU.mult, ALU.add).then_inc(S["mean"], 1)
        eng.wait_ge(S["root"], 1)
        ch(nc.vector.reciprocal(ss[:, 4:6], ss[:, 4:6]))
        for t in range(TT):
            nc.vector.tensor_scalar(xn[:, t], src[:, t], ss[:, 4 + t:5 + t], None, ALU.mult).then_inc(S["normed"], 1)
        for q in range(4):
            t, half = q // 2, q % 2
            eng.wait_ge(S["turned"], q + 1)
            pq = ps[:, q % 2, :].rearrange("p (k n) -> p k n", k=4)
            out = dst[:, 4 * half:4 * half + 4, P * t:P * t + P]
            gq = gain[:, 4 * half:4 * half + 4].unsqueeze(2).to_broadcast([P, 4, P])
            ins = nc.vector.tensor_tensor(out, pq, gq, ALU.mult)
            if shift is None:
                ins.then_inc(S["xt"], 1)
            else:
                ch(ins)
                sq = shift[:, 4 * half:4 * half + 4].unsqueeze(2).to_broadcast([P, 4, P])
                nc.vector.tensor_tensor(out, out, sq, ALU.add).then_inc(S["xt"], 1)

    def pe(eng):
        for q in range(4):
            t, half = q // 2, q % 2
            if half == 0:
                eng.wait_ge(S["normed"], t + 1)
            if q >= 2:
                eng.wait_ge(S["xt"], q - 1)
            for k in range(4):
                kk = 4 * half + k
                mm = nc.tensor.transpose(ps[:, q % 2, k * P:k * P + P], xn[:, t, kk * P:kk * P + P], g.ident[:])
            mm.then_inc(S["turned"], 1)
        eng.wait_ge(S["xt"], 4)

    return act, dve, pe


def setup_phase(nc, g, I):
    with ExitStack() as ctx:
        S = Sems(nc, ctx, "setup")
        rows = ctx.enter_context(nc.sbuf_tensor("vec_rows", [P, 2, P], F32))
        buckets = ctx.enter_context(nc.sbuf_tensor("buckets", [NUM_BUCKETS, BIAS_HEADS + DIST], F32))
        dmask = ctx.enter_context(nc.sbuf_tensor("dist_mask", [BIAS_HEADS, DIST], F32))
        dbias = ctx.enter_context(nc.sbuf_tensor("dist_bias", [BIAS_HEADS, DIST], F32))
        lamv = ctx.enter_context(nc.sbuf_tensor("lam_rows", [P, 4 * HD + 8], F32))
        skewed = ctx.enter_context(nc.sbuf_tensor("bias_skewed", [P, BIAS_HEADS, T], F32))
        flip = ctx.enter_context(nc.sbuf_tensor("flip", [P, P], F32))
        n_rows = [0]
        block = ctx.enter_context(nc.Block(no_gpsimd_drain=True))

        @block.scalar
        def _(act):
            def put(dst, src):
                act.dma_start(dst, src).then_inc(S["rows"], 16)
                n_rows[0] += 16
            put(g.ident[:], I["k_ident"])
            put(g.causal[:], I["k_causal"])
            put(g.x[:], I["x"].rearrange("b (t p) d -> p (b t) d", p=P))
            for names, counts, start, half in ((VEC_A, VEC_A_ROWS, ROW_A, 0), (VEC_B, VEC_B_ROWS, ROW_B, 1)):
                for n, k in zip(names, counts):
                    r0 = start[n]
                    if n == "qk_gain":
                        flat = I[n].rearrange("l a b e -> (l a b) e")
                        put(rows[r0:r0 + k, half, 0:HD], flat)
                        put(rows[r0:r0 + k, half, HD:P], flat)
                        continue
                    shape = I[n].shape
                    letters = "abcd"[:len(shape)]
                    flat = I[n].rearrange(f"{' '.join(letters)} -> ({' '.join(letters)})")
                    put(rows[r0:r0 + k, half, :], flat.rearrange("(r n) -> r n", n=P))
            for j, n in enumerate(("hy_freq_2", "hy_ffn_b1_2", "hy_ffn_b2_2")):
                put(rows[HY64_ROW + j:HY64_ROW + j + 1, 0, 0:HD], I[n])
                put(rows[HY64_ROW + j:HY64_ROW + j + 1, 0, HD:P], I[n])
            act.wait_ge(S["lamsum"], 1)
            nc.scalar.activation(lamv[:, 258:260], lamv[:, 256:258], ACT.Exp).then_inc(S["lamexp"], 1)

        @block.sync
        def _(sp):
            load_tiles(g, sp, R)
            sp.dma_start(buckets[:, 0:BIAS_HEADS], I["rel_bias"]).then_inc(S["buckets"], 16)
            sp.dma_start(buckets[:, BIAS_HEADS:], I["k_onehot"]).then_inc(S["buckets"], 16)
            sp.dma_start(dmask[:], I["k_dmask"]).then_inc(S["buckets"], 16)
            sp.dma_start(lamv[:, 0:256], I["diff_lambda"].rearrange("l a b -> l (a b)").to_broadcast([P, 256])
                         ).then_inc(S["lam"], 16)
            sp.wait_ge(S["dbias"], 1)
            sp.dma_start(g.bias_dram, dbias[:]).then_inc(S["stored"], 16)
            sp.wait_ge(S["stored"], 16)
            skew = bass.AP(tensor=g.bias_dram.tensor, offset=0, ap=[[1, P], [DIST, BIAS_HEADS], [1, T]])
            sp.dma_start(skewed[:], skew).then_inc(S["skewed"], 16)
            sp.dma_start(flip[:], I["k_flip"]).then_inc(S["skewed"], 16)

        @block.tensor
        def _(pe):
            pe.wait_ge(S["rows"], n_rows[0])
            nc.tensor.transpose(g.ps[:, 0, 0:NA], rows[0:NA, 0, :], g.ident[0:NA, 0:NA])
            nc.tensor.transpose(g.ps[:, 1, 0:NB], rows[0:NB, 1, :], g.ident[0:NB, 0:NB]).then_inc(S["cols"], 1)
            pe.wait_ge(S["buckets"], 48)
            nc.tensor.matmul(g.ps[0:BIAS_HEADS, 2, 0:DIST], buckets[:, 0:BIAS_HEADS], buckets[:, BIAS_HEADS:],
                             start=True, stop=True).then_inc(S["bias_ps"], 1)
            pe.wait_ge(S["skewed"], 32)
            for n in range(BIAS_HEADS // 2):
                if n >= 4:
                    pe.wait_ge(S["flipped"], n - 3)
                nc.tensor.matmul(g.ps[:, 4 + n % 4, :], flip[:], skewed[:, 2 * n:2 * n + 2].rearrange("p h n -> p (h n)"),
                                 start=True, stop=True).then_inc(S["flip_ps"], 1)

        @block.vector
        def _(dve):
            ch = Chain(dve, S["dve"])
            nc.vector.memset(g.ones[:], 1.0)
            dve.wait_ge(S["cols"], 1)
            nc.vector.tensor_copy(g.va[:, 0:NA], g.ps[:, 0, 0:NA])
            nc.vector.tensor_copy(g.vb[:, 0:NB], g.ps[:, 1, 0:NB])
            dve.wait_ge(S["bias_ps"], 1)
            dve.wait_ge(S["buckets"], 48)
            nc.vector.tensor_tensor(dbias[:], g.ps[0:BIAS_HEADS, 2, 0:DIST], dmask[:], ALU.add).then_inc(S["dbias"], 1)
            dve.wait_ge(S["lam"], 16)
            pair = lamv[:, 0:256].rearrange("p (a b e) -> p a b e", a=2, b=2)
            ch(nc.vector.tensor_tensor(pair[:, :, 0, :], pair[:, :, 0, :], pair[:, :, 1, :], ALU.mult))
            nc.vector.tensor_reduce(lamv[:, 256:258], pair[:, :, 0, :], AX_X, ALU.add).then_inc(S["lamsum"], 1)
            dve.wait_ge(S["lamexp"], 1)
            ch(nc.vector.tensor_tensor(lamv[:, 260:261], lamv[:, 258:259], lamv[:, 259:260], ALU.subtract))
            ch(nc.vector.tensor_scalar(g.lam[:], lamv[:, 260:261], LAM_INIT, None, ALU.add))
            for n in range(BIAS_HEADS // 2):
                dve.wait_ge(S["flip_ps"], n + 1)
                nc.vector.tensor_copy(g.bias[:, 2 * n:2 * n + 2].rearrange("p h n -> p (h n)"), g.ps[:, 4 + n % 4, :]
                                      ).then_inc(S["flipped"], 1)


def ffn_phase(nc, g, name, gain_row):
    with ExitStack() as ctx:
        S = Sems(nc, ctx, name)
        hid = ctx.enter_context(nc.sbuf_tensor(f"{name}_hid", [P, FC, T], F32))
        silu = ctx.enter_context(nc.sbuf_tensor(f"{name}_silu", [P, 2, T], F32))
        xt, ps = g.xt, g.ps
        act_n, dve_n, pe_n = rms_transposed(g, nc, S, g.x, xt, g.va[:, gain_row:gain_row + KC])
        first = g.stream.first[name]
        down0 = g.stream.first[name + "_down"]
        block = ctx.enter_context(nc.Block(no_gpsimd_drain=True))

        @block.sync
        def _(sp):
            load_tiles(g, sp, down0 + FC // 2 + R)

        @block.tensor
        def _(pe):
            pe_n(pe)
            for f in range(FC):
                gt = first + 2 * (f // 2)
                if f % 2 == 0:
                    wait_tile(g, pe, gt)
                    wait_tile(g, pe, gt + 1)
                if f >= 2:
                    pe.wait_ge(S["hid"], f - 1)
                for u in range(2):
                    w = tile3(g, gt + u, KC)
                    for k in range(KC):
                        mm = nc.tensor.matmul(ps[:, f % 2, u * T:u * T + T], w[:, k, P * (f % 2):P * (f % 2) + P],
                                              xt[:, k, :], start=k == 0, stop=k == KC - 1)
                    if f % 2:
                        mm.then_inc(g.tiles_used, 1)
                    elif u:
                        mm.then_inc(S["even_chunk"], 1)
            for m in range(FC // 2):
                i = down0 + m
                wait_tile(g, pe, i)
                w = tile3(g, i, 2)
                for c in range(2):
                    f = 2 * m + c
                    pe.wait_ge(S["hid"], f + 1)
                    for t in range(TT):
                        for n in range(2):
                            mm = nc.tensor.matmul(ps[:, 4 + 2 * t + n, :], hid[:, f, P * t:P * t + P],
                                                  w[:, c, 512 * n:512 * n + 512], start=f == 0, stop=f == FC - 1)
                mm.then_inc(g.tiles_used, 1)

        @block.scalar
        def _(act):
            act_n(act)
            for f in range(FC):
                if f % 2:
                    act.wait_ge(g.tiles_used, first + f + 1)
                else:
                    act.wait_ge(S["even_chunk"], f // 2 + 1)
                if f >= 2:
                    act.wait_ge(S["hid"], f - 1)
                nc.scalar.activation(silu[:, f % 2], ps[:, f % 2, 0:T], ACT.Silu).then_inc(S["silu"], 1)

        @block.vector
        def _(dve):
            ch = Chain(dve, S["dve"])
            dve_n(dve, ch)
            for f in range(FC):
                dve.wait_ge(S["silu"], f + 1)
                nc.vector.tensor_tensor(hid[:, f], ps[:, f % 2, T:2 * T], silu[:, f % 2], ALU.mult).then_inc(S["hid"], 1)
            dve.wait_ge(g.tiles_used, down0 + FC // 2)
            for t in range(TT):
                for n in range(2):
                    xs = g.x[:, t, 512 * n:512 * n + 512]
                    nc.vector.scalar_tensor_tensor(xs, ps[:, 4 + 2 * t + n, :], 0.5, xs, ALU.mult, ALU.add)


QK_HEADS_A, QK_HEADS_B, QK_HEADS_C = 24, 16, 5
QT_CHUNKS = ([(A_COL + P * i, "qk_gain", 0 if i < 6 else 1) for i in range(12)]
             + [(BQK_COL + P * i, "qk_gain", 2 if i < 4 else 3) for i in range(8)]
             + [(C_COL + P * i, "qk_gain", 4) for i in range(2)] + [(C_COL + 256, "qk_gain", 5)]
             + [(IX_COL + P * i, None, 0) for i in range(4)] + [(IX_COL + 512, None, 0)])
QC, QI = 20, 23
UNITS = [("a", i) for i in range(4)] + [("b", i) for i in range(4)] + [("c", 0)]


def mixer_phase(nc, g):
    with ExitStack() as ctx:
        S = Sems(nc, ctx, "mix")

        def sb(name, shape):
            return ctx.enter_context(nc.sbuf_tensor(name, shape, F32))
        pr = sb("proj", [P, TT, N_IN])
        ps = g.ps
        in0 = g.stream.first["w_in"]
        n_in = g.stream.first["w_branch_a"] - in0
        with ExitStack() as inner:
            S1 = Sems(nc, inner, "mixin")
            act_n, dve_n, pe_n = rms_transposed(g, nc, S1, g.x, g.xt, g.va[:, ROW_A["mix_norm"]:ROW_A["mix_norm"] + KC])
            block = inner.enter_context(nc.Block(no_gpsimd_drain=True))

            @block.sync
            def _(sp):
                load_tiles(g, sp, in0 + n_in + R)

            @block.tensor
            def _(pe):
                pe_n(pe)
                for i in range(n_in):
                    wait_tile(g, pe, in0 + i)
                    w = tile3(g, in0 + i, KC)
                    n = w.shape[2]
                    if i >= 4:
                        pe.wait_ge(S1["copied"], i - 3)
                    for t in range(TT):
                        for k in range(KC):
                            mm = nc.tensor.matmul(ps[:, i % 4, 256 * t:256 * t + n], g.xt[:, k, P * t:P * t + P], w[:, k, :],
                                                  start=k == 0, stop=k == KC - 1)
                    mm.then_inc(g.tiles_used, 1)

            def copy_out(eng, copy, i):
                c0 = 256 * i
                n = min(256, N_IN - c0)
                eng.wait_ge(g.tiles_used, in0 + i + 1)
                src = ps[:, i % 4, :].rearrange("p (t n) -> p t n", t=TT)[:, :, 0:n]
                if i:
                    eng.wait_ge(S1["copied"], i)
                copy(pr[:, :, c0:c0 + n], src).then_inc(S1["copied"], 1)

            @block.scalar
            def _(act):
                act_n(act)
                for i in range(1, n_in, 2):
                    copy_out(act, nc.scalar.copy, i)

            @block.vector
            def _(dve):
                ch = Chain(dve, S1["dve"])
                dve_n(dve, ch)
                for i in range(0, n_in, 2):
                    copy_out(dve, nc.vector.tensor_copy, i)

        mixer_attention(nc, g, pr)
        mixer_out(nc, g, pr)


def mixer_attention(nc, g, pr):
    with ExitStack() as ctx:
        S = Sems(nc, ctx, "att")

        def sb(name, shape):
            return ctx.enter_context(nc.sbuf_tensor(name, shape, F32))
        ps = g.ps
        qt = sb("qt", [P, len(QT_CHUNKS), T])
        hs = sb("head_sums", [P, TT, 48])
        with ExitStack() as inner:
            sq = inner.enter_context(nc.sbuf_tensor("head_squares", [P, QK_HEADS_A * HD], F32))
            twice = inner.enter_context(nc.sbuf_tensor("keys_twice", [P, TT, 2, P], F32))
            S1 = Sems(nc, inner, "qk")
            block = inner.enter_context(nc.Block(no_gpsimd_drain=True))
            groups = [(A_COL, QK_HEADS_A, 0), (BQK_COL, QK_HEADS_B, 24), (C_COL, QK_HEADS_C, 40)]

            @block.scalar
            def _(act):
                n = 0
                for t in range(TT):
                    for c0, heads, h0 in groups:
                        if n:
                            act.wait_ge(S1["summed"], n)
                        nc.scalar.activation(sq[:, 0:heads * HD], pr[:, t, c0:c0 + heads * HD], ACT.Square).then_inc(S1["squared"], 1)
                        n += 1
                act.wait_ge(S1["mean"], 1)
                nc.scalar.activation(hs[:, :, 0:45], hs[:, :, 0:45], ACT.Sqrt).then_inc(S1["root"], 1)
                for i, (c0, gname, gr) in enumerate(QT_CHUNKS):
                    act.wait_ge(S1["turned"], i + 1)
                    src = ps[:, i % 4, 0:T]
                    if gname:
                        r = ROW_A[gname] + gr
                        nc.scalar.activation(qt[:, i, :], src, ACT.Copy, scale=g.va[:, r:r + 1]).then_inc(S1["evac"], 1)
                    else:
                        nc.scalar.copy(qt[:, i, :], src).then_inc(S1["evac"], 1)
                act.wait_ge(S1["evac"], len(QT_CHUNKS))

            @block.vector
            def _(dve):
                ch = Chain(dve, S1["dve"])
                n = 0
                for t in range(TT):
                    for c0, heads, h0 in groups:
                        dve.wait_ge(S1["squared"], n + 1)
                        s3 = sq[:, 0:heads * HD].rearrange("p (h e) -> p h e", e=HD)
                        nc.vector.tensor_reduce(hs[:, t, h0:h0 + heads], s3, AX_X, ALU.add).then_inc(S1["summed"], 1)
                        n += 1
                dve.wait_ge(S1["summed"], n)
                nc.vector.tensor_scalar(hs[:, :, 0:45], hs[:, :, 0:45], 1.0 / HD, EPS, ALU.mult, ALU.add).then_inc(S1["mean"], 1)
                dve.wait_ge(S1["root"], 1)
                ch(nc.vector.reciprocal(hs[:, :, 0:45], hs[:, :, 0:45]))
                for c0, heads, h0 in groups:
                    for t in range(TT):
                        p3 = pr[:, t, c0:c0 + heads * HD].rearrange("p (h e) -> p h e", e=HD)
                        r3 = hs[:, t, h0:h0 + heads].unsqueeze(2).to_broadcast([P, heads, HD])
                        nc.vector.tensor_tensor(p3, p3, r3, ALU.mult).then_inc(S1["unit"], 1)
                dve.wait_ge(S1["unit"], 6)
                for t in range(TT):
                    for j, c0 in enumerate((C_COL + 256, IX_COL + 512)):
                        nc.vector.tensor_copy(twice[:, t, j, :].rearrange("p (a e) -> p a e", a=2),
                                              pr[:, t, c0:c0 + HD].unsqueeze(1).to_broadcast([P, 2, HD])).then_inc(S1["twice"], 1)

            @block.tensor
            def _(pe):
                for i, (c0, gname, gr) in enumerate(QT_CHUNKS):
                    pe.wait_ge(S1["unit"], 2 if i < 12 else 4 if i < 20 else 6)
                    if i >= 4:
                        pe.wait_ge(S1["evac"], i - 3)
                    single = c0 in (C_COL + 256, IX_COL + 512)
                    if single:
                        pe.wait_ge(S1["twice"], 4)
                    for t in range(TT):
                        if single:
                            src = twice[:, t, int(c0 > C_COL + 256), :]
                        else:
                            src = pr[:, t, c0:c0 + P]
                        mm = nc.tensor.transpose(ps[:, i % 4, P * t:P * t + P], src, g.ident[:])
                    mm.then_inc(S1["turned"], 1)

        keep = sb("keep", [P, TT, T])
        select_keys(nc, g, pr, qt, keep)
        softmax_units(nc, g, pr, qt, keep)


def causal_keys(t):
    return P * (t + 1), P * (1 - t)


def select_keys(nc, g, pr, qt, keep):
    with ExitStack() as ctx:
        S = Sems(nc, ctx, "idx")

        def sb(name, shape):
            return ctx.enter_context(nc.sbuf_tensor(name, shape, F32))
        relu = sb("relu", [P, 2, T])
        score = sb("score", [P, TT, T])
        work = sb("work", [P, T])
        sel = sb("sel", [P, 3, T])
        top = sb("top", [P, 8])
        cnt = sb("cnt", [P, 4])
        wix = sb("wix", [P, TT, IDX_HEADS])
        ps = g.ps
        block = ctx.enter_context(nc.Block(no_gpsimd_drain=True))
        steps = [(t, h) for t in range(TT) for h in range(IDX_HEADS)]

        @block.tensor
        def _(pe):
            for i, (t, h) in enumerate(steps):
                nk = causal_keys(t)[0]
                lo = HD * (h % 2)
                if i >= 4:
                    pe.wait_ge(S["relu"], i - 3)
                nc.tensor.matmul(ps[:, i % 4, 0:nk], qt[lo:lo + HD, QI + h // 2, P * t:P * t + P],
                                 qt[lo:lo + HD, QI + 4, 0:nk], start=True, stop=True).then_inc(S["raw"], 1)

        @block.scalar
        def _(act):
            for i, (t, h) in enumerate(steps):
                nk = causal_keys(t)[0]
                act.wait_ge(S["raw"], i + 1)
                if i >= 2:
                    act.wait_ge(S["added"], i - 1)
                nc.scalar.activation(relu[:, i % 2, 0:nk], ps[:, i % 4, 0:nk], ACT.Relu, scale=HD ** -0.5).then_inc(S["relu"], 1)

        @block.vector
        def _(dve):
            ch = Chain(dve, S["dve"])
            c0 = IX_COL + IDX_HEADS * HD + HD
            ch(nc.vector.tensor_scalar(wix[:], pr[:, :, c0:c0 + IDX_HEADS], IDX_HEADS ** -0.5, None, ALU.mult))
            for i, (t, h) in enumerate(steps):
                nk, b0 = causal_keys(t)
                dve.wait_ge(S["relu"], i + 1)
                if i:
                    dve.wait_ge(S["added"], i)
                sc = score[:, t, 0:nk]
                w = wix[:, t, h:h + 1]
                if h == 0:
                    ins = nc.vector.tensor_scalar(sc, relu[:, i % 2, 0:nk], w, None, ALU.mult)
                else:
                    ins = nc.vector.scalar_tensor_tensor(sc, relu[:, i % 2, 0:nk], w, sc, ALU.mult, ALU.add)
                ins.then_inc(S["added"], 1)
            dve.wait_ge(S["added"], len(steps))
            for t in range(TT):
                nk, b0 = causal_keys(t)
                sc, wk = score[:, t, 0:nk], work[:, 0:nk]
                ch(nc.vector.tensor_tensor(sc, sc, g.causal[:, b0:b0 + nk], ALU.add))
                first_by_rank(nc, ch, sc, wk, top, sel[:, :, 0:nk], cnt, TOP_KEYS, g.ones[:, 0:nk])
                ch(nc.vector.tensor_scalar(keep[:, t, 0:nk], sel[:, 0, 0:nk], -1.0, -MASKED, ALU.add, ALU.mult))


def first_by_rank(nc, ch, sc, wk, top, sel, cnt, count, ones):
    v = nc.vector
    for r in range(count // 8):
        src = sc if r == 0 else wk
        ch(v.max(top[:], src))
        if r < count // 8 - 1:
            ch(v.match_replace(out=wk, in_to_replace=top[:], in_values=src, imm_value=-3e38))
    thr = top[:, 7:8]
    gt, eq, run = sel[:, 0], sel[:, 1], sel[:, 2]
    ch(v.tensor_scalar(gt, sc, thr, None, ALU.is_gt))
    ch(v.tensor_reduce(cnt[:, 0:1], gt, AX_X, ALU.add))
    ch(v.tensor_scalar(cnt[:, 1:2], cnt[:, 0:1], -1.0, float(count), ALU.mult, ALU.add))
    ch(v.tensor_scalar(eq, sc, thr, None, ALU.is_equal))
    ch(v.tensor_tensor_scan(run, ones, eq, 0.0, ALU.mult, ALU.add))
    ch(v.scalar_tensor_tensor(eq, run, cnt[:, 1:2], eq, ALU.is_le, ALU.mult))
    ch(v.tensor_tensor(gt, gt, eq, ALU.add))


def softmax_units(nc, g, pr, qt, keep):
    with ExitStack() as ctx:
        S = Sems(nc, ctx, "sm")

        def sb(name, shape):
            return ctx.enter_context(nc.sbuf_tensor(name, shape, F32))
        lg = sb("logits", [P, 2, 4, T])
        pt = sb("probs_t", [P, 2, 8, P])
        st = sb("stats", [P, 2, 16])
        rden = sb("rden", [P, 2, 4])
        ps, o = g.ps, g.o
        steps = [(u, h, t) for u, h in UNITS for t in range(TT)]
        block = ctx.enter_context(nc.Block(no_gpsimd_drain=True))
        n_group = {"a": 3, "b": 2, "c": 4}
        n_turn = {"a": 3, "b": 1, "c": 4}
        bias_head = {"a": lambda h, j: 4 * j + h, "b": lambda h, j: A_HEADS + h, "c": lambda h, j: A_HEADS + B_HEADS + j}

        def heads_of(u, h, j):
            if u == "a":
                n = 4 * j + h
                return (n // 2, 6 + n // 2, HD * (n % 2))
            if u == "b":
                return (12 + 2 * j + h // 2, 16 + 2 * j + h // 2, HD * (h % 2))
            return (QC + j // 2, QC + 2, HD * (j % 2))

        def score_place(i, u, j, nk):
            b, c = (j % 2, j // 2) if u == "c" else (j // 2, j % 2)
            return ps[:, 2 * (i % 2) + b, T * c:T * c + nk]

        def values_of(u, h, j, kt):
            if u == "a":
                c = A_COL + 2 * A_HEADS * HD + HD * (4 * j + h)
                return pr[:, kt, c:c + HD]
            if u == "b":
                return pr[:, kt, BV_COL + P * h:BV_COL + P * h + P]
            return pr[:, kt, C_COL + 320:C_COL + 320 + HD]

        @block.tensor
        def _(pe):
            def scores(i):
                u, h, t = steps[i]
                nk = causal_keys(t)[0]
                if i >= 2:
                    pe.wait_ge(S["logits"], i - 1)
                for j in range(n_group[u]):
                    cq, ck, lo = heads_of(u, h, j)
                    mm = nc.tensor.matmul(score_place(i, u, j, nk),
                                          qt[lo:lo + HD, cq, P * t:P * t + P], qt[lo:lo + HD, ck, 0:nk],
                                          start=True, stop=True)
                mm.then_inc(S["scores"], 1)

            def outputs(i):
                u, h, t = steps[i]
                pe.wait_ge(S["probs"], i + 1)
                if i:
                    pe.wait_ge(S["pt"], i)
                for j in range(n_turn[u]):
                    for kt in range(t + 1):
                        n = (t + 1) * j + kt
                        mm = nc.tensor.transpose(ps[:, 4 + n // 4, P * (n % 4):P * (n % 4) + P],
                                                 lg[:, i % 2, j, P * kt:P * kt + P], g.ident[:])
                mm.then_inc(S["turned"], 1)
                pe.wait_ge(S["pt"], i + 1)
                if i >= 2:
                    pe.wait_ge(S["out"], i - 1)
                for j in range(n_turn[u]):
                    for kt in range(t + 1):
                        n = (t + 1) * j + kt
                        joint = u == "a"
                        v = values_of(u, h, j, kt)
                        w = v.shape[1]
                        c = 0 if joint else w * j
                        first = n == 0 if joint else kt == 0
                        last = n == 3 * (t + 1) - 1 if joint else kt == t
                        mm = nc.tensor.matmul(ps[:, 6 + i % 2, c:c + w], pt[:, i % 2, n, :], v, start=first, stop=last)
                mm.then_inc(S["o_ps"], 1)

            for i in range(len(steps) + 1):
                if i < len(steps):
                    scores(i)
                if i:
                    outputs(i - 1)

        @block.scalar
        def _(act):
            def copy_turned(i):
                u, h, t = steps[i]
                n = n_turn[u] * (t + 1)
                act.wait_ge(S["turned"], i + 1)
                if i >= 2:
                    act.wait_ge(S["o_ps"], i - 1)
                src = ps[:, 4:6, :].rearrange("p b (n q) -> p (b n) q", n=4)[:, 0:n, :]
                nc.scalar.copy(pt[:, i % 2, 0:n, :], src).then_inc(S["pt"], 1)

            for i, (u, h, t) in enumerate(steps):
                nk = causal_keys(t)[0]
                n = n_group[u]
                act.wait_ge(S["max"], i + 1)
                if u == "a":
                    nc.scalar.activation(lg[:, i % 2, 0:n, 0:nk], lg[:, i % 2, 0:n, 0:nk], ACT.Exp, bias=st[:, i % 2, 0:1],
                                         accum_out=st[:, i % 2, 8:9]).then_inc(S["exp"], 1)
                else:
                    for j in range(n):
                        ins = nc.scalar.activation(lg[:, i % 2, j, 0:nk], lg[:, i % 2, j, 0:nk], ACT.Exp,
                                                   bias=st[:, i % 2, j:j + 1], accum_out=st[:, i % 2, 8 + j:9 + j])
                    ins.then_inc(S["exp"], 1)
                if i:
                    copy_turned(i - 1)
            copy_turned(len(steps) - 1)

        @block.vector
        def _(dve):
            ch = Chain(dve, S["dve"])
            v = nc.vector

            def logits(i):
                u, h, t = steps[i]
                nk, b0 = causal_keys(t)
                n = n_group[u]
                dve.wait_ge(S["scores"], i + 1)
                if i >= 2:
                    dve.wait_ge(S["turned"], i - 1)
                for j in range(n):
                    src = score_place(i, u, j, nk)
                    b = bias_head[u](h, j)
                    ins = v.scalar_tensor_tensor(lg[:, i % 2, j, 0:nk], src, HD ** -0.5, g.bias[:, b, b0:b0 + nk],
                                                 ALU.mult, ALU.add)
                    if j < n - 1:
                        ch.add(ins)
                ins.then_inc(S["logits"], 1)
                dve.wait_ge(S["logits"], i + 1)
                ch.sync()
                l3 = lg[:, i % 2, 0:n, 0:nk]
                if u == "c":
                    k3 = keep[:, t, 0:nk].unsqueeze(1).to_broadcast([P, n, nk])
                    ch(v.tensor_tensor(l3, l3, k3, ALU.add))
                if u == "a":
                    ch(v.tensor_reduce(st[:, i % 2, 4:5], l3, AX_XY, ALU.max))
                    m = 1
                else:
                    ch(v.tensor_reduce(st[:, i % 2, 4:4 + n], l3, AX_X, ALU.max))
                    m = n
                v.tensor_scalar(st[:, i % 2, 0:m], st[:, i % 2, 4:4 + m], -1.0, None, ALU.mult).then_inc(S["max"], 1)

            def weights(i):
                u, h, t = steps[i]
                nk = causal_keys(t)[0]
                m = 1 if u == "a" else n_group[u]
                dve.wait_ge(S["exp"], i + 1)
                if i >= 2:
                    dve.wait_ge(S["out"], i - 1)
                ins = v.reciprocal(rden[:, i % 2, 0:m], st[:, i % 2, 8:8 + m])
                if u != "b":
                    ins.then_inc(S["probs"], 1)
                    return
                ch(ins)
                ch(v.tensor_tensor(rden[:, i % 2, 2:3], rden[:, i % 2, 1:2], g.lam[:], ALU.mult))
                l0, l1 = lg[:, i % 2, 0, 0:nk], lg[:, i % 2, 1, 0:nk]
                ch(v.tensor_scalar(l1, l1, rden[:, i % 2, 2:3], None, ALU.mult))
                v.scalar_tensor_tensor(l0, l0, rden[:, i % 2, 0:1], l1, ALU.mult, ALU.subtract).then_inc(S["probs"], 1)

            def scale_out(i):
                u, h, t = steps[i]
                dve.wait_ge(S["o_ps"], i + 1)
                dve.wait_ge(S["probs"], i + 1)
                src = ps[:, 6 + i % 2, :]
                if u == "a":
                    v.tensor_scalar(o[:, t, HD * h:HD * h + HD], src[:, 0:HD], rden[:, i % 2, 0:1], None,
                                    ALU.mult).then_inc(S["out"], 1)
                elif u == "b":
                    v.tensor_copy(o[:, t, 256 + P * h:256 + P * h + P], src[:, 0:P]).then_inc(S["out"], 1)
                else:
                    dst = o[:, t, 768:1024].rearrange("p (h e) -> p h e", e=HD)
                    r3 = rden[:, i % 2, 0:4].unsqueeze(2).to_broadcast([P, 4, HD])
                    v.tensor_tensor(dst, src[:, 0:256].rearrange("p (h e) -> p h e", e=HD), r3, ALU.mult).then_inc(S["out"], 1)

            for i in range(len(steps)):
                logits(i)
                if i >= 2:
                    scale_out(i - 2)
                weights(i)
            scale_out(len(steps) - 2)
            scale_out(len(steps) - 1)


def turn_rows(nc, g, pe, S, src, dst_name, n, bank0=0):
    q = 0
    for t in range(TT):
        for half in range(n // 4):
            if q >= 2:
                pe.wait_ge(S[dst_name], q - 1)
            for k in range(4):
                kk = 4 * half + k
                mm = nc.tensor.transpose(g.ps[:, bank0 + q % 2, P * k:P * k + P], src[:, t, P * kk:P * kk + P], g.ident[:])
            mm.then_inc(S[dst_name + "_turned"], 1)
            q += 1


def copy_turned_rows(nc, g, eng, copy, S, dst, dst_name, n, bank0=0):
    q = 0
    for t in range(TT):
        for half in range(n // 4):
            eng.wait_ge(S[dst_name + "_turned"], q + 1)
            copy(dst[:, 4 * half:4 * half + 4, P * t:P * t + P],
                 g.ps[:, bank0 + q % 2, :].rearrange("p (k n) -> p k n", k=4)).then_inc(S[dst_name], 1)
            q += 1


def mixer_out(nc, g, pr):
    with ExitStack() as ctx:
        S = Sems(nc, ctx, "mo")

        def sb(name, shape):
            return ctx.enter_context(nc.sbuf_tensor(name, shape, F32))
        ps, o, xt = g.ps, g.o, g.xt
        ot, y = sb("ot", [P, KC, T]), sb("y", [P, TT, D])
        st, sq, tmp = sb("st", [P, TT, 8]), sb("sq", [P, TT, 512]), sb("tmp", [P, TT, D])
        dnorm = sb("dnorm", [P, P])
        br0 = g.stream.first["w_branch_a"]
        out0 = g.stream.first["w_out"]
        branch_tiles = [[0], [1, 2], [3]]
        block = ctx.enter_context(nc.Block(no_gpsimd_drain=True))

        @block.sync
        def _(sp):
            sp.dma_start(dnorm[:], g.I["diff_out_norm"].to_broadcast([P, P])).then_inc(S["dnorm"], 16)
            load_tiles(g, sp, out0 + 4 + R)

        @block.scalar
        def _(act):
            for t in range(TT):
                nc.scalar.activation(sq[:, t], o[:, t, 256:768], ACT.Square).then_inc(S["sq"], 1)
            act.wait_ge(S["mean"], 1)
            nc.scalar.activation(st[:, :, 4:8], st[:, :, 0:4], ACT.Sqrt).then_inc(S["root"], 1)
            for t in range(TT):
                gt = pr[:, t, GATE_COL:GATE_COL + 3 * D]
                nc.scalar.activation(gt, gt, ACT.Sigmoid).then_inc(S["gates"], 1)
            copy_turned_rows(nc, g, act, nc.scalar.copy, S, ot, "ot", KC)
            copy_turned_rows(nc, g, act, nc.scalar.copy, S, xt, "yt", KC)

        @block.vector
        def _(dve):
            ch = Chain(dve, S["dve"])
            v = nc.vector
            dve.wait_ge(S["sq"], TT)
            ch(v.tensor_reduce(st[:, :, 0:4], sq[:].rearrange("p t (h e) -> p t h e", e=P), AX_X, ALU.add))
            v.tensor_scalar(st[:, :, 0:4], st[:, :, 0:4], 1.0 / P, EPS, ALU.mult, ALU.add).then_inc(S["mean"], 1)
            dve.wait_ge(S["root"], 1)
            ch(v.reciprocal(st[:, :, 4:8], st[:, :, 4:8]))
            ch(v.tensor_scalar(st[:, :, 0:4], st[:, :, 4:8], 1.0 - LAM_INIT, None, ALU.mult))
            dve.wait_ge(S["dnorm"], 16)
            for t in range(TT):
                o3 = o[:, t, 256:768].rearrange("p (h e) -> p h e", e=P)
                ch(v.tensor_tensor(o3, o3, dnorm[:].unsqueeze(1).to_broadcast([P, 4, P]), ALU.mult))
                v.tensor_tensor(o3, o3, st[:, t, 0:4].unsqueeze(2).to_broadcast([P, 4, P]), ALU.mult).then_inc(S["b_normed"], 1)
            dve.wait_ge(S["gates"], TT)
            for b in range(3):
                dve.wait_ge(g.tiles_used, br0 + branch_tiles[b][-1] + 1)
                for t in range(TT):
                    gt = pr[:, t, GATE_COL + D * b:GATE_COL + D * b + D]
                    src = ps[:, 4 + 2 * t:6 + 2 * t, :].rearrange("p b n -> p (b n)")
                    if b == 0:
                        ins = v.tensor_tensor(y[:, t], src, gt, ALU.mult)
                        ch(ins) if t == 0 else ins.then_inc(S["gated"], 1)
                    else:
                        ins = v.tensor_tensor(tmp[:, t], src, gt, ALU.mult)
                        ch(ins) if t == 0 else ins.then_inc(S["gated"], 1)
                if b:
                    dve.wait_ge(S["gated"], b + 1)
                    for t in range(TT):
                        ins = v.tensor_tensor(y[:, t], y[:, t], tmp[:, t], ALU.add)
                        if b == 2:
                            ins.then_inc(S["y"], 1)
                        else:
                            ch(ins)
            dve.wait_ge(S["y"], 2)
            dve.wait_ge(g.tiles_used, out0 + 4)
            for t in range(TT):
                xs = g.x[:, t]
                v.tensor_tensor(xs, ps[:, 4 + 2 * t:6 + 2 * t, :].rearrange("p b n -> p (b n)"), xs, ALU.add)

        @block.tensor
        def _(pe):
            pe.wait_ge(S["b_normed"], TT)
            turn_rows(nc, g, pe, S, o, "ot", KC)
            pe.wait_ge(S["ot"], 4)
            n_chunk = 0
            for b, tiles in enumerate(branch_tiles):
                if b:
                    pe.wait_ge(S["gated"], b)
                for i in tiles:
                    wait_tile(g, pe, br0 + i)
                    w = tile3(g, br0 + i, 2)
                    for c in range(2):
                        first, last = i == tiles[0] and c == 0, i == tiles[-1] and c == 1
                        for t in range(TT):
                            for n in range(2):
                                mm = nc.tensor.matmul(ps[:, 4 + 2 * t + n, :], ot[:, n_chunk, P * t:P * t + P],
                                                      w[:, c, 512 * n:512 * n + 512], start=first, stop=last)
                        n_chunk += 1
                    mm.then_inc(g.tiles_used, 1)
            pe.wait_ge(S["y"], TT)
            turn_rows(nc, g, pe, S, y, "yt", KC)
            pe.wait_ge(S["yt"], 4)
            token_product(nc, g, pe, xt, out0, 4)


def token_product(nc, g, pe, lhs, i0, n_tiles):
    for m in range(n_tiles):
        wait_tile(g, pe, i0 + m)
        w = tile3(g, i0 + m, 2)
        for c in range(2):
            k = 2 * m + c
            for t in range(TT):
                for n in range(2):
                    mm = nc.tensor.matmul(g.ps[:, 4 + 2 * t + n, :], lhs[:, k, P * t:P * t + P],
                                          w[:, c, 512 * n:512 * n + 512], start=k == 0, stop=k == 2 * n_tiles - 1)
        mm.then_inc(g.tiles_used, 1)


def allocate(nc, ctx, g):
    def sb(name, shape):
        return ctx.enter_context(nc.sbuf_tensor(name, shape, F32))
    g.ps = ctx.enter_context(nc.psum_tensor("ps", [P, 8, 512], F32))
    g.ring = sb("ring", [P, R, WT])
    g.ident, g.va, g.vb = sb("ident", [P, P]), sb("va", [P, NA]), sb("vb", [P, NB])
    g.ones = sb("ones", [P, T])
    g.lam, g.ss = sb("lam", [P, 1]), sb("ss", [P, 8])
    g.x, g.xt = sb("x", [P, TT, D]), sb("xt", [P, KC, T])
    g.tile_loaded = [ctx.enter_context(nc.semaphore(f"tile_loaded_{i}")) for i in range(R)]
    g.tiles_used = ctx.enter_context(nc.semaphore("tiles_used"))
    g.issued = 0


def first_stream(st, I):
    def ffn(name):
        gate, up = I[f"{name}_w_gate"][0], I[f"{name}_w_up"][0]
        st.mark(name)
        for c in range(0, D_FF, 256):
            for w in (gate, up):
                st.src.append((WT, w[:, c:c + 256].rearrange("(k p) n -> p k n", p=P)))
        st.rows(f"{name}_down", I[f"{name}_w_down"][0])
    ffn("ffn1")
    st.columns("w_in", I["w_in"][0], 0, N_IN)
    for b in "abc":
        st.rows(f"w_branch_{b}", I[f"w_branch_{b}"][0])
    st.rows("w_out", I["w_out"][0])
    ffn("ffn2")


def first_block(nc, g, I, ctx, dump=None):
    with ExitStack() as mine:
        def sb(name, shape):
            return mine.enter_context(nc.sbuf_tensor(name, shape, F32))
        g.o, g.bias = sb("o", [P, TT, D]), sb("bias", [P, BIAS_HEADS, T])
        g.xn = g.o
        g.causal = sb("causal", [P, T])
        setup_phase(nc, g, I)
        ffn_phase(nc, g, "ffn1", ROW_A["ffn1_norm"])
        if dump:
            dump("a")
        mixer_phase(nc, g)
        if dump:
            dump("b")
    g.xn = ctx.enter_context(nc.sbuf_tensor("xn", [P, TT, D], F32))
    ffn_phase(nc, g, "ffn2", ROW_A["ffn2_norm"])
    if dump:
        dump("c")


def constants():
    ident = np.eye(P, dtype=np.float32)
    dist = np.arange(-127, T)
    n = np.maximum(dist, 0)
    exact = NUM_BUCKETS // 2
    nf = np.maximum(n, 1).astype(np.float32)
    large = exact + (np.log(nf / np.float32(exact)) / np.float32(math.log(MAX_DISTANCE / exact))
                     * np.float32(NUM_BUCKETS - exact)).astype(np.int32)
    bucket = np.where(n < exact, n, np.minimum(large, NUM_BUCKETS - 1))
    bucket, d = bucket[::-1], dist[::-1]
    onehot = (bucket[None, :] == np.arange(NUM_BUCKETS)[:, None]).astype(np.float32)
    ok = np.zeros((BIAS_HEADS, DIST), bool)
    ok[:] = d >= 0
    ok[0:4] &= d <= 128
    ok[4:8] &= d % 4 == 0
    ok[8:12] &= d % 16 == 0
    dmask = np.where(ok, np.float32(0), np.float32(MASKED))
    q, c = np.arange(P)[:, None], np.arange(T)[None, :]
    causal = np.where(P + q - c >= 0, np.float32(0), np.float32(MASKED))
    return {"k_ident": ident, "k_flip": np.ascontiguousarray(ident[::-1]), "k_onehot": onehot, "k_dmask": dmask.astype(np.float32), "k_causal": causal.astype(np.float32)}


CH = 32
NCH = T // CH
PAIRS = 4
RW_HEADS = 8
DECAY = -math.exp(-0.5)
LN_EPS = 64e-5
FREQ = 2 * T
CTX0 = 4


def second_stream(st, I):
    st.columns("mod_w", I["mod_w_2"][0], 0, 6 * D)
    st.columns("w_state", I["w_in_2"][0], HY_COLS + STATE_LO, HY_COLS + STATE_HI)
    st.columns("w_in_2", I["w_in_2"][0], 0, HY_COLS + RW_COLS)
    st.columns("w_gates", I["w_in_2"][0], HY_COLS + RW_COLS, IN2_COLS)
    st.rows("hy_proj", I["hy_proj_2"][0])
    st.rows("rw_proj", I["rw_proj_2"][0])
    st.rows("w_out_2", I["w_out_2"][0])
    st.mark("experts")
    for e in range(NE):
        for w in ("exp_w1_2", "exp_w3_2"):
            for k in range(KC):
                st.src.append((WT, I[w][0, e, P * k:P * k + P, :]))
        down = I["exp_w2_2"][0, e].rearrange("(h k p) n -> k p h n", h=2, p=P)
        for k in range(KC):
            st.src.append((WT, down[k]))


def col(g, name, i=0, n=1):
    if name in ROW_A:
        return g.va[:, ROW_A[name] + i:ROW_A[name] + i + n]
    return g.vb[:, ROW_B[name] + i:ROW_B[name] + i + n]


def modulation_phase(nc, g, I):
    with ExitStack() as ctx:
        S = Sems(nc, ctx, "mod")

        def sb(name, shape):
            return ctx.enter_context(nc.sbuf_tensor(name, shape, F32))
        csil, rows, sel = sb("csil", [P, KC, 32]), sb("mod_rows", [P, 2, 256]), sb("mod_sel", [P, 2 + P])
        gate_b, post = sb("gate_bias", [P, 2, D]), sb("post", [P, 2, D])
        ps = g.ps
        i0 = g.stream.first["mod_w"]
        n_tiles = 6 * D // 256
        gate_tiles = {i: (i - 8, 0) if i < 12 else (i - 20, 1) for i in list(range(8, 12)) + list(range(20, 24))}
        block = ctx.enter_context(nc.Block(no_gpsimd_drain=True))

        @block.sync
        def _(sp):
            sp.dma_start(sel[:], I["k_modsel"]).then_inc(S["sel"], 16)
            for dst, name in ((g.masks[:].rearrange("p d n -> p (d n)"), "k_masks"), (g.blockones[:], "k_blockones"),
                              (g.blk16[:], "k_blk16"), (g.restart[:], "k_restart"), (g.ident2[:], "k_ident2")):
                sp.dma_start(dst, I[name]).then_inc(S["consts"], 16)
            sp.wait_ge(S["consts"], 80)
            for j, (m, norm) in enumerate(((2, "norm1_post_2"), (5, "norm2_post_2"))):
                sp.dma_start(gate_b[:, j], I["mod_b_2"][:, D * m:D * m + D].to_broadcast([P, D])).then_inc(S["gate_b"], 16)
                sp.dma_start(post[:, j], I[norm].to_broadcast([P, D])).then_inc(S["gate_b"], 16)
            load_tiles(g, sp, i0 + n_tiles + R)
            sp.wait_ge(S["post"], 8)
            sp.dma_start(g.post_dram, post[:]).then_inc(S["stored"], 16)
            sp.wait_ge(S["stored"], 16)

        @block.scalar
        def _(act):
            act.wait_ge(S["zeroed"], 1)
            nc.scalar.activation(csil[:, :, 0], col(g, "c_2", 0, KC), ACT.Silu).then_inc(S["csil"], 1)
            nc.scalar.activation(csil[:, :, 1], col(g, "c_ctx_2", 0, KC), ACT.Silu).then_inc(S["csil"], 1)

        @block.tensor
        def _(pe):
            pe.wait_ge(S["csil"], 2)
            pe.wait_ge(S["sel"], 16)

            def turn(i):
                pe.wait_ge(S["rows"], i + 1)
                for s in range(2):
                    m = 2 * i + s
                    mm = nc.tensor.matmul(ps[:, 2, 2 * m:2 * m + 2], rows[:, i % 2, P * s:P * s + P], sel[:, 0:2],
                                          start=True, stop=True)
                if i in gate_tiles:
                    n = list(gate_tiles).index(i)
                    if n:
                        pe.wait_ge(S["gate"], n)
                    mm = nc.tensor.matmul(ps[:, 3, 0:256], sel[:, 2:2 + P], rows[:, i % 2, :], start=True, stop=True)
                mm.then_inc(S["turned"], 1)

            for i in range(n_tiles):
                wait_tile(g, pe, i0 + i)
                w = tile3(g, i0 + i, KC)
                if i >= 2:
                    pe.wait_ge(S["rows"], i - 1)
                for kk in range(2):
                    for j in range(4):
                        mm = nc.tensor.matmul(ps[32 * j:32 * j + 32, i % 2, 0:256], csil[:, 4 * kk + j, :],
                                              w[:, 4 * kk + j, :], start=kk == 0, stop=kk == 1)
                mm.then_inc(g.tiles_used, 1)
                if i:
                    turn(i - 1)
            turn(n_tiles - 1)

        @block.vector
        def _(dve):
            v = nc.vector
            ch = Chain(dve, S["dve"])
            ch(v.scalar_tensor_tensor(g.own[:], col(g, "rw_mu_2", 0, RWC), -1.0, col(g, "rw_mu_2", RWC, RWC), ALU.mult, ALU.subtract))
            ch(v.tensor_scalar(g.own[:], g.own[:], 1.0, None, ALU.add))
            v.memset(csil[:], 0.0).then_inc(S["zeroed"], 1)
            dve.wait_ge(S["gate_b"], 64)

            def gate(i):
                c, j = gate_tiles[i]
                n = list(gate_tiles).index(i)
                dve.wait_ge(S["turned"], i + 1)
                gb = gate_b[:, j, 256 * c:256 * c + 256]
                po = post[:, j, 256 * c:256 * c + 256]
                v.tensor_tensor(gb, ps[:, 3, 0:256], gb, ALU.add).then_inc(S["gate"], 1)
                dve.wait_ge(S["gate"], n + 1)
                v.tensor_tensor(po, po, gb, ALU.mult).then_inc(S["post"], 1)

            for i in range(n_tiles):
                dve.wait_ge(g.tiles_used, i0 + i + 1)
                if i >= 2:
                    dve.wait_ge(S["turned"], i - 1)
                v.tensor_copy(rows[:, i % 2, :], ps[:, i % 2, 0:256]).then_inc(S["rows"], 1)
                if i - 1 in gate_tiles:
                    gate(i - 1)
            gate(n_tiles - 1)
            dve.wait_ge(S["turned"], n_tiles)
            m3 = g.mod[:].rearrange("p (m r) -> p m r", r=2)
            ch(v.tensor_tensor(m3, ps[:, 2, 0:96].rearrange("p (m r) -> p m r", r=2),
                               col(g, "mod_b_2", 0, 48).unsqueeze(2).to_broadcast([P, 48, 2]), ALU.add))
            for j, (m, r, norm) in enumerate(((1, 0, "norm1_pre_2"), (1, 1, "norm1_pre_2"), (4, 0, "norm2_pre_2"))):
                v.scalar_tensor_tensor(g.scale[:, j, :], m3[:, KC * m:KC * m + KC, r], 1.0, col(g, norm, 0, KC), ALU.add, ALU.mult)
            for j, (m, r) in enumerate(((0, 0), (0, 1), (3, 0))):
                v.tensor_copy(g.shift[:, j, :], m3[:, KC * m:KC * m + KC, r])


def feature_product(g, nc, pe, S, i0, c0, c1, x, banks=4):
    for n in range(c0, c1):
        i = i0 + (n - c0) // 2
        if (n - c0) % 2 == 0:
            wait_tile(g, pe, i)
        w = tile3(g, i, KC)
        if n - c0 >= banks:
            pe.wait_ge(S["fcopied"], n - c0 - banks + 1)
        s = P * ((n - c0) % 2)
        for k in range(KC):
            mm = nc.tensor.matmul(g.ps[:, (n - c0) % banks, 0:T], w[:, k, s:s + P], x[:, k, :], start=k == 0, stop=k == KC - 1)
        if (n - c0) % 2 or n == c1 - 1:
            mm.then_inc(g.tiles_used, 1)
        else:
            mm.then_inc(S["even_chunk"], 1)


def wait_feature(g, eng, S, i0, n, last):
    if n % 2 or n == last:
        eng.wait_ge(g.tiles_used, i0 + n // 2 + 1)
    else:
        eng.wait_ge(S["even_chunk"], n // 2 + 1)


def mix_neighbours(v, ch, dst, src, own, prev, nxt, add=None):
    if add is None:
        ch(v.tensor_scalar(dst, src, own, None, ALU.mult))
    else:
        ch(v.tensor_scalar(dst, src, own, add, ALU.mult, ALU.add))
    ch(v.scalar_tensor_tensor(dst[:, 1:T], src[:, 0:T - 1], prev, dst[:, 1:T], ALU.mult, ALU.add))
    return v.scalar_tensor_tensor(dst[:, 0:T - 1], src[:, 1:T], nxt, dst[:, 0:T - 1], ALU.mult, ALU.add)


def context_phase(nc, g, I, z):
    with ExitStack() as ctx:
        S = Sems(nc, ctx, "ctx")

        def sb(name, shape):
            return ctx.enter_context(nc.sbuf_tensor(name, shape, F32))
        cx, raw = sb("cx", [P, TT, D]), sb("ctx_raw", [P, 9, T])
        act_n, dve_n, pe_n = rms_transposed(g, nc, S, cx, g.xt, g.scale[:, 1, :], g.shift[:, 1, :])
        i0 = g.stream.first["w_state"]
        block = ctx.enter_context(nc.Block(no_gpsimd_drain=True))

        @block.sync
        def _(sp):
            sp.dma_start(cx[:], I["ctx_2"].rearrange("b (t p) d -> p (b t) d", p=P)).then_inc(S["cx"], 16)
            load_tiles(g, sp, i0 + 5 + R)

        @block.tensor
        def _(pe):
            pe_n(pe)
            feature_product(g, nc, pe, S, i0, CTX0, 13, g.xt)

        @block.scalar
        def _(act):
            act.wait_ge(S["cx"], 16)
            act_n(act)
            for n in range(9):
                wait_feature(g, act, S, i0, n, 8)
                nc.scalar.copy(raw[:, n, :], g.ps[:, n % 4, 0:T]).then_inc(S["fcopied"], 1)

        @block.vector
        def _(dve):
            ch = Chain(dve, S["dve"])
            dve.wait_ge(S["cx"], 16)
            dve_n(dve, ch)
            for n in range(9):
                dve.wait_ge(S["fcopied"], n + 1)
                c = CTX0 + n
                mix_neighbours(nc.vector, ch, z[:, c, :], raw[:, n, :], g.own[:, c:c + 1],
                               col(g, "rw_mu_2", c), col(g, "rw_mu_2", RWC + c))


def project_phase(nc, g, I, z, zh):
    with ExitStack() as ctx:
        S = Sems(nc, ctx, "proj2")

        def sb(name, shape):
            return ctx.enter_context(nc.sbuf_tensor(name, shape, F32))
        raw = sb("raw", [P, 4, T])
        act_n, dve_n, pe_n = rms_transposed(g, nc, S, g.x, g.xt, g.scale[:, 0, :], g.shift[:, 0, :])
        i0 = g.stream.first["w_in_2"]
        nf = HYC + RWC
        block = ctx.enter_context(nc.Block(no_gpsimd_drain=True))

        @block.sync
        def _(sp):
            load_tiles(g, sp, i0 + nf // 2 + R)

        @block.tensor
        def _(pe):
            pe_n(pe)
            feature_product(g, nc, pe, S, i0, 0, nf, g.xt)

        @block.scalar
        def _(act):
            act_n(act)
            for n in range(nf):
                wait_feature(g, act, S, i0, n, nf - 1)
                if n >= 4:
                    act.wait_ge(S["mixed"], n - 3)
                nc.scalar.copy(raw[:, n % 4, :], g.ps[:, n % 4, 0:T]).then_inc(S["fcopied"], 1)

        @block.vector
        def _(dve):
            ch = Chain(dve, S["dve"])
            dve_n(dve, ch)
            for n in range(nf):
                dve.wait_ge(S["fcopied"], n + 1)
                if n < HYC:
                    ins = mix_neighbours(nc.vector, ch, zh[:, n, :], raw[:, n % 4, :], col(g, "hy_conv_w_2", HYC + n),
                                         col(g, "hy_conv_w_2", n), col(g, "hy_conv_w_2", 2 * HYC + n), col(g, "hy_conv_b_2", n))
                else:
                    c = n - HYC
                    ins = mix_neighbours(nc.vector, ch, z[:, c, :], raw[:, n % 4, :], g.own[:, c:c + 1],
                                         col(g, "rw_mu_2", c), col(g, "rw_mu_2", RWC + c))
                ins.then_inc(S["mixed"], 1)


def recurrence_phase(nc, g, I, z, store, ctx_only, name):
    for d in range(2):
        nm = f"{name}{d}"
        with ExitStack() as ctx:
            def sb(n, shape):
                return ctx.enter_context(nc.sbuf_tensor(f"{nm}_{n}", shape, F32))
            ar, bk = sb("ar", [P, PAIRS, 2, T]), sb("bk", [P, PAIRS, 2, T])
            tok = sb("tok", [P, 3, TT, RW_WIDTH])
            pc = sb("pc", [P, PAIRS, NCH])
            recurrence_inputs(nc, g, I, z, ar, bk, tok, pc, store, ctx_only, nm, d)
            part = {"tm": sb("tm", [P, NCH, PAIRS, HD]), "rm": sb("rm", [P, NCH, PAIRS, HD])}
            if not ctx_only:
                part |= {"g1": sb("g1", [P, PAIRS, T]), "g2": sb("g2", [P, TT, RW_HEADS, P])}
            recurrence_chunks(nc, g, ar, bk, tok, pc, store, part, ctx_only, nm, d)
            st = sb("state", [P, NCH + 1, PAIRS, HD])
            recurrence_states(nc, g, store, part, st, ctx_only, nm, d)
            if not ctx_only:
                recurrence_outputs(nc, g, store, part, st, nm, d)


def recurrence_inputs(nc, g, I, z, ar, bk, tok, pc, store, ctx_only, name, d):
    with ExitStack() as ctx:
        S = Sems(nc, ctx, name + "i")

        def sb(nm, shape):
            return ctx.enter_context(nc.sbuf_tensor(f"{name}i_{nm}", shape, F32))
        tl = sb("tanh", [P, T])
        kk, w1, w2 = sb("kk", [P, PAIRS, T]), sb("w1", [P, PAIRS, T]), sb("w2", [P, PAIRS, T])
        ld, av, cum = sb("ld", [P, PAIRS, T]), sb("av", [P, PAIRS, T]), sb("cum", [P, PAIRS, T])
        ebk = sb("ebk", [P, 2, PAIRS, T])
        tot = sb("tot", [P, PAIRS, NCH])
        ps = g.ps
        k, v_, r = z[:, 4:8, :], z[:, 8:12, :], z[:, 0:4, :]
        v = nc.vector
        block = ctx.enter_context(nc.Block(no_gpsimd_drain=True))

        def per(nm, i=0):
            return col(g, nm, i, PAIRS).unsqueeze(2).to_broadcast([P, PAIRS, T])

        def chunked(x):
            return x.rearrange("p c (n s) -> p (c n) s", s=CH)

        def totb():
            return tot[:].rearrange("p c n -> p (c n)").unsqueeze(2).to_broadcast([P, PAIRS * NCH, CH])

        lora = sb("lora", [P, RW_WIDTH])

        @block.sync
        def _(sp):
            sp.dma_start(lora[0:64, :], I["rw_w_up_2"][0, d]).then_inc(S["lora_in"], 16)
            sp.dma_start(lora[64:P, :], I["rw_a_up_2"][0, d]).then_inc(S["lora_in"], 16)

        @block.tensor
        def _(pe):
            pe.wait_ge(S["ksq"], 1)
            for c in range(PAIRS):
                mm = nc.tensor.matmul(ps[:, c // 2, T * (c % 2):T * (c % 2) + T], g.blockones[:], w1[:, c, :], start=True, stop=True)
            mm.then_inc(S["ksum"], 1)
            pe.wait_ge(S["tanh"], 1)
            pe.wait_ge(S["lora_in"], 32)
            for c in range(PAIRS):
                nc.tensor.matmul(ps[:, 2 + c // 2, T * (c % 2):T * (c % 2) + T], lora[0:64, P * c:P * c + P],
                                 tl[0:64, :], start=True, stop=True)
            for c in range(PAIRS):
                mm = nc.tensor.matmul(ps[:, 4 + c // 2, T * (c % 2):T * (c % 2) + T], lora[64:P, P * c:P * c + P],
                                      z[64:P, 12, :], start=True, stop=True)
            mm.then_inc(S["lora"], 1)
            q = 0
            for j in range(d, 4):
                if j:
                    pe.wait_ge(S["ready"], 1)
                for t in range(TT):
                    if q >= 2:
                        pe.wait_ge(S["tokcopy"], q - 1)
                    for c in range(PAIRS):
                        src = (v_[:, c], ar[:, c, 0], ebk[:, 0, c], ebk[:, 1, c])[j][:, P * t:P * t + P]
                        mm = nc.tensor.transpose(ps[:, 6 + q % 2, P * c:P * c + P], src, g.ident[:])
                    mm.then_inc(S["tokturn"], 1)
                    q += 1

        @block.scalar
        def _(act):
            nc.scalar.activation(tl[0:64, :], z[0:64, 12, :], ACT.Tanh).then_inc(S["tanh"], 1)
            act.wait_ge(S["kmax"], 1)
            nc.scalar.activation(w2[:], w2[:], ACT.Sqrt).then_inc(S["kroot"], 1)
            act.wait_ge(S["lora"], 1)
            for c in range(PAIRS):
                nc.scalar.activation(ld[:, c, :], ps[:, 2 + c // 2, T * (c % 2):T * (c % 2) + T], ACT.Sigmoid,
                                     bias=col(g, "rw_w0_2", 4 * d + c))
            for c in range(PAIRS):
                ins = nc.scalar.activation(av[:, c, :], ps[:, 4 + c // 2, T * (c % 2):T * (c % 2) + T], ACT.Sigmoid,
                                           bias=col(g, "rw_a0_2", 4 * d + c))
            ins.then_inc(S["sig"], 1)
            act.wait_ge(S["logs"], 1)
            nc.scalar.activation(w1[:], w1[:], ACT.Exp).then_inc(S["exp"], 1)
            nc.scalar.activation(w2[:], cum[:], ACT.Exp).then_inc(S["exp"], 1)
            nc.scalar.activation(pc[:], tot[:], ACT.Exp).then_inc(S["exp"], 1)
            act.wait_ge(S["exp"], 3)
            nc.scalar.activation(cum[:], cum[:], ACT.Exp, scale=-1.0).then_inc(S["exp"], 1)
            q = 0
            for j in range(d, 4):
                for t in range(TT):
                    act.wait_ge(S["tokturn"], q + 1)
                    dst = store["v"][:, t, :] if j == 0 else tok[:, j - 1, t, :]
                    nc.scalar.copy(dst, ps[:, 6 + q % 2, :]).then_inc(S["tokcopy"], 1)
                    q += 1

        @block.vector
        def _(dve):
            ch = Chain(dve, S["dve"])
            ch(v.tensor_tensor(kk[:], k, per("rw_k_k_2"), ALU.mult))
            v.tensor_tensor(w1[:], kk[:], kk[:], ALU.mult).then_inc(S["ksq"], 1)
            dve.wait_ge(S["ksum"], 1)
            v.tensor_scalar(w2[:].rearrange("p c t -> p (c t)"), ps[:, 0:2, :].rearrange("p b n -> p (b n)"), 1e-24, None,
                            ALU.max).then_inc(S["kmax"], 1)
            dve.wait_ge(S["kroot"], 1)
            ch(v.reciprocal(w2[:], w2[:]))
            ch(v.tensor_tensor(kk[:], kk[:], w2[:], ALU.mult))
            dve.wait_ge(S["sig"], 1)
            ch(v.tensor_scalar(ld[:], ld[:], DECAY, None, ALU.mult))
            for c in range(PAIRS):
                ch.add(v.tensor_tensor_scan(cum[:, c, :], g.restart[:], ld[:, c, :], 0.0, ALU.mult, ALU.add))
            ch.sync()
            ch(v.tensor_copy(tot[:].rearrange("p c n -> p (c n)"), chunked(cum[:])[:, :, CH - 1]))
            if d:
                ch(v.tensor_tensor(cum[:], ld[:], cum[:], ALU.subtract))
                ch(v.tensor_tensor(chunked(cum[:]), chunked(cum[:]), totb(), ALU.add))
            v.tensor_tensor(w1[:], cum[:], ld[:], ALU.subtract).then_inc(S["logs"], 1)
            dve.wait_ge(S["exp"], 4)
            ch(v.scalar_tensor_tensor(ar[:, :, 0, :], kk[:], -1.0, w1[:], ALU.mult, ALU.mult))
            if not ctx_only:
                ch(v.tensor_tensor(ar[:, :, 1, :], r, w2[:], ALU.mult))
            ch(v.tensor_scalar(w1[:], av[:], -1.0, None, ALU.add))
            ch(v.tensor_tensor(w1[:], w1[:], per("rw_k_a_2"), ALU.mult))
            ch(v.scalar_tensor_tensor(w1[:], w1[:], 1.0, k, ALU.add, ALU.mult))
            ch(v.tensor_tensor(w2[:], kk[:], av[:], ALU.mult))
            if not ctx_only:
                if d == 0:
                    ch(v.tensor_copy(store["kmod"][:], w1[:]))
                else:
                    ch(v.tensor_tensor(store["kmod"][:], store["kmod"][:], w1[:], ALU.add))
            ch(v.tensor_tensor(bk[:, :, 0, :], w2[:], cum[:], ALU.mult))
            ch(v.tensor_tensor(bk[:, :, 1, :], w1[:], cum[:], ALU.mult))
            for j in range(2):
                for c in range(PAIRS):
                    src = bk[:, c, j, :].rearrange("p (n s) -> p n s", s=CH)
                    dst = ebk[:, j, c, :].rearrange("p (n s) -> p n s", s=CH)
                    ins = v.tensor_tensor(dst, src, pc[:, c, :].unsqueeze(2).to_broadcast([P, NCH, CH]), ALU.mult)
            ins.then_inc(S["ready"], 1)


def recurrence_chunks(nc, g, ar, bk, tok, pc, store, part, ctx_only, name, d):
    with ExitStack() as ctx:
        def sb(nm, shape):
            return ctx.enter_context(nc.sbuf_tensor(f"{name}c_{nm}", shape, F32))
        S = Sems(nc, ctx, name + "c")
        ps, v = g.ps, nc.vector
        tm, rm, vtok = part["tm"], part["rm"], store["v"]
        H4 = 4
        prod = sb("prod", [P, 2, H4, 4, P])
        a16, b16, x16, yv = (sb(n, [P, 2, H4, P]) for n in ("a16", "b16", "x16", "y"))
        ftil, km = sb("f", [P, 2, H4, HD]), sb("km", [P, 2, H4, HD])

        def a2(s):
            return prod[:, s, :, 0]

        def b2(s):
            return prod[:, s, :, 2]
        a4, b4 = a16, b16
        its = [(t, h4) for t in range(TT) for h4 in range(2)]
        block = ctx.enter_context(nc.Block(no_gpsimd_drain=True))
        NR = 10

        def order():
            for it in range(0, len(its), 2):
                for r in range(NR):
                    for j in range(2):
                        yield its[it + j], r, it + j

        def half(x, h):
            return x[HD * (h % 2):HD * (h % 2) + HD]

        @block.tensor
        def _(pe):
            mmf = nc.tensor.matmul
            for (t, h4), r, n in order():
                b = 4 * h4
                s = h4
                if r:
                    pe.wait_ge(S[f"rd{h4}"], NR * (n // 2) + r)
                elif n >= 2:
                    pe.wait_ge(S[f"rd{h4}"], NR * (n // 2))
                heads = [4 * h4 + i for i in range(H4)]
                tsl = slice(P * t, P * t + P)
                if r == 0:
                    for i, h in enumerate(heads):
                        ah, bh = half(ar[:, h // 2], h), half(bk[:, h // 2], h)
                        if ctx_only:
                            mmf(ps[:, b + i, 0:P], bh[:, 0, tsl], ah[:, 0, tsl], start=True, stop=True)
                        else:
                            mmf(ps[:, b + i, 0:2 * P], bh[:, 0, tsl], ah[:, :, tsl], start=True, stop=True)
                        mm = mmf(ps[:, b + i, 2 * P:4 * P], ah[:, 0, tsl], bh[:, :, tsl], start=True, stop=True)
                elif r == 1:
                    for i, h in enumerate(heads):
                        mmf(ps[:, b, P * i:P * i + P], b16[:, s, i], a16[:, s, i], start=True, stop=True)
                        mm = mmf(ps[:, b + 1, P * i:P * i + P], a16[:, s, i], b16[:, s, i], start=True, stop=True)
                    if not ctx_only:
                        for i, h in enumerate(heads):
                            ah, bh = half(ar[:, h // 2], h), half(bk[:, h // 2], h)
                            mm = mmf(ps[:, b + 2 + h % 2, P * (i // 2):P * (i // 2) + P], bh[:, 1, tsl], ah[:, 1, tsl],
                                     start=True, stop=True)
                elif r == 2:
                    for i in range(H4):
                        mmf(ps[:, b, P * i:P * i + P], b2(s)[:, i], a2(s)[:, i], start=True, stop=True)
                        mmf(ps[:, b + 1, P * i:P * i + P], a2(s)[:, i], b2(s)[:, i], start=True, stop=True)
                        mm = mmf(ps[:, b + 2, P * i:P * i + P], b2(s)[:, i], yv[:, s, i], start=True, stop=True)
                elif r == 3:
                    for i in range(H4):
                        mmf(ps[:, b, P * i:P * i + P], a4[:, s, i], b4[:, s, i], start=True, stop=True)
                        mm = mmf(ps[:, b + 1, P * i:P * i + P], b4[:, s, i], yv[:, s, i], start=True, stop=True)
                elif r == 4:
                    for i in range(H4):
                        mm = mmf(ps[:, b, P * i:P * i + P], b2(s)[:, i], yv[:, s, i], start=True, stop=True)
                elif r == 5:
                    for i in range(H4):
                        mmf(ps[:, b, P * i:P * i + P], x16[:, s, i], yv[:, s, i], start=True, stop=True)
                        mm = nc.tensor.transpose(ps[:, b + 1, P * i:P * i + P], yv[:, s, i], g.ident[:])
                elif r == 6:
                    for i in range(H4):
                        mm = mmf(ps[:, b, P * i:P * i + P], b2(s)[:, i], a2(s)[:, i], start=True, stop=True)
                elif r == 7:
                    for i, h in enumerate(heads):
                        if not ctx_only:
                            mmf(ps[:, b, P * i:P * i + P], yv[:, s, i], prod[:, s, i, 1], start=True, stop=True)
                        mm = mmf(ps[:, b + 1, HD * i:HD * i + HD], yv[:, s, i], tok[:, 1, t, HD * h:HD * h + HD],
                                 start=True, stop=True)
                elif r == 8:
                    for i, h in enumerate(heads):
                        mm = mmf(ps[:, b + 1, HD * i:HD * i + HD], prod[:, s, i, 3], ftil[:, s, i], start=True, stop=True)
                        if not ctx_only:
                            mmf(ps[:, b, P * i:P * i + P], prod[:, s, i, 3], a4[:, s, i], start=True, stop=True)
                            mm = mmf(half(ps[:, b + 2, P * (i // 2):P * (i // 2) + P], h), tok[:, 0, t, HD * h:HD * h + HD],
                                     a4[:, s, i], start=True, stop=True)
                else:
                    for i, h in enumerate(heads):
                        for c in range(4):
                            rows = slice(CH * c, CH * c + CH)
                            o0 = HD * (i // 2)
                            mmf(half(ps[:, b + c, o0:o0 + HD], h), tok[rows, 0, t, HD * h:HD * h + HD], ftil[rows, s, i],
                                start=True, stop=True)
                            mm = mmf(half(ps[:, b + c, P + o0:P + o0 + HD], h), km[rows, s, i], vtok[rows, t, HD * h:HD * h + HD],
                                     start=True, stop=True)
                mm.then_inc(S[f"pe{h4}"], 1)

        copy_rounds = (1, 2, 3, 5) if ctx_only else (1, 2, 3, 5, 7)

        def rows4(x):
            return x.rearrange("p (h q) -> p h q", h=H4)

        @block.scalar
        def _(act):
            for (t, h4), r, n in order():
                if r not in copy_rounds:
                    continue
                b, s = 4 * h4, h4
                act.wait_ge(S[f"pe{h4}"], NR * (n // 2) + r + 1)
                dst = b4[:, s] if r == 2 else a4[:, s] if r == 7 else b2(s)
                src = ps[:, b + (r in (1, 2, 5)), :]
                nc.scalar.copy(dst, rows4(src)).then_inc(S[f"cp{h4}"], 1)

        @block.vector
        def _(dve):
            ch = Chain(dve, S["dve"])
            flat = lambda x: x.rearrange("p h q -> p (h q)")
            copies = [0, 0]
            for (t, h4), r, n in order():
                b, s = 4 * h4, h4
                dve.wait_ge(S[f"pe{h4}"], NR * (n // 2) + r + 1)
                if r in copy_rounds:
                    copies[h4] += 1
                    dve.wait_ge(S[f"cp{h4}"], copies[h4])
                if r == 0:
                    m4 = g.masks[:, d].rearrange("p (k q) -> p k q", k=4)
                    for i in range(H4):
                        if ctx_only:
                            for k in (0, 2, 3):
                                ch.add(v.tensor_tensor(prod[:, s, i, k], ps[:, b + i, P * k:P * k + P], m4[:, k], ALU.mult))
                        else:
                            ch.add(v.tensor_tensor(prod[:, s, i], ps[:, b + i, :].rearrange("p (k q) -> p k q", k=4), m4, ALU.mult))
                    ch.sync()
                    blk = g.blk16[:].unsqueeze(1).to_broadcast([P, H4, P])
                    idb = g.ident[:].unsqueeze(1).to_broadcast([P, H4, P])
                    ch(v.tensor_tensor(a16[:, s], prod[:, s, :, 2], blk, ALU.mult))
                    ch.add(v.tensor_tensor(yv[:, s], a16[:, s], idb, ALU.add))
                    ch(v.tensor_tensor(b16[:, s], prod[:, s, :, 0], blk, ALU.mult))
                    ins = v.tensor_tensor(x16[:, s], prod[:, s, :, 0], b16[:, s], ALU.subtract)
                elif r == 1:
                    if not ctx_only:
                        incl = g.masks[:, d, P:2 * P].unsqueeze(1).to_broadcast([P, 2, P])
                        for e in range(2):
                            ch.add(v.tensor_tensor(part["g2"][:, t, 4 * h4 + e:4 * h4 + 4:2],
                                                   ps[:, b + 2 + e, 0:256].rearrange("p (k q) -> p k q", k=2), incl, ALU.mult))
                    ins = v.tensor_copy(a2(s), rows4(ps[:, b, :]))
                elif r == 2:
                    ch.add(v.tensor_copy(flat(a4[:, s]), ps[:, b, :]))
                    ins = v.tensor_tensor(flat(yv[:, s]), flat(yv[:, s]), ps[:, b + 2, :], ALU.add)
                elif r == 3:
                    ins = v.tensor_tensor(flat(yv[:, s]), flat(yv[:, s]), ps[:, b + 1, :], ALU.add)
                elif r == 4:
                    ins = v.tensor_tensor(flat(yv[:, s]), flat(yv[:, s]), ps[:, b, :], ALU.add)
                elif r == 5:
                    ins = v.tensor_copy(a2(s), rows4(ps[:, b, :]))
                elif r == 6:
                    ins = v.tensor_tensor(flat(yv[:, s]), flat(yv[:, s]), ps[:, b, :], ALU.add)
                elif r == 7:
                    ins = v.tensor_copy(flat(ftil[:, s]), ps[:, b + 1, 0:256])
                elif r == 8:
                    kt = tok[:, 2, t, 256 * h4:256 * h4 + 256]
                    ins = v.tensor_tensor(flat(km[:, s]), ps[:, b + 1, 0:256], kt, ALU.add)
                    if not ctx_only:
                        ch.add(ins)
                        g2 = part["g2"][:, t, 4 * h4:4 * h4 + 4]
                        ch.add(v.tensor_tensor(g2, rows4(ps[:, b, :]), g2, ALU.add))
                        ins = v.tensor_tensor(part["g1"][:, 2 * h4:2 * h4 + 2, P * t:P * t + P],
                                              ps[:, b + 2, 0:256].rearrange("p (k q) -> p k q", k=2),
                                              ar[:, 2 * h4:2 * h4 + 2, 1, P * t:P * t + P], ALU.add)
                else:
                    for c in range(4):
                        for k in range(2):
                            pr = 2 * h4 + k
                            ch.add(v.scalar_tensor_tensor(tm[:, 4 * t + c, pr], g.ident2[:], pc[:, pr, 4 * t + c:4 * t + c + 1],
                                                          ps[:, b + c, HD * k:HD * k + HD], ALU.mult, ALU.add))
                        ins = v.tensor_copy(rm[:, 4 * t + c, 2 * h4:2 * h4 + 2],
                                            ps[:, b + c, P:2 * P].rearrange("p (k e) -> p k e", k=2))
                        if c < 3:
                            ch.add(ins)
                ch.sync()
                ins.then_inc(S[f"rd{h4}"], 1)


def recurrence_states(nc, g, store, part, st, ctx_only, name, d):
    with ExitStack() as ctx:
        S = Sems(nc, ctx, name + "s")
        tm, rm, ps = part["tm"], part["rm"], g.ps
        block = ctx.enter_context(nc.Block(no_gpsimd_drain=True))

        def chunk(n):
            return NCH - 1 - n if d else n

        @block.tensor
        def _(pe):
            for n in range(NCH):
                pe.wait_ge(S["state"], n + 1)
                for par in range(2):
                    for pr in range(PAIRS):
                        lo = HD * par
                        mm = nc.tensor.matmul(ps[lo:lo + HD, n % 2, pr * HD:pr * HD + HD], tm[lo:lo + HD, chunk(n), pr],
                                              st[lo:lo + HD, n, pr], start=True, stop=True)
                mm.then_inc(S["moved"], 1)

        @block.vector
        def _(dve):
            if ctx_only:
                nc.vector.memset(st[:, 0], 0.0).then_inc(S["state"], 1)
            else:
                nc.vector.tensor_copy(st[:, 0], store["carry"][:, d]).then_inc(S["state"], 1)
            for n in range(NCH):
                dve.wait_ge(S["moved"], n + 1)
                dst = store["carry"][:, d] if ctx_only and n == NCH - 1 else st[:, n + 1]
                nc.vector.tensor_tensor(dst, ps[:, n % 2, 0:256].rearrange("p (c e) -> p c e", e=HD), rm[:, chunk(n)],
                                        ALU.add).then_inc(S["state"], 1)


def recurrence_outputs(nc, g, store, part, st, name, d):
    with ExitStack() as ctx:
        S = Sems(nc, ctx, name + "o")
        g1, g2, ps, y = part["g1"], part["g2"], g.ps, store["y"]
        block = ctx.enter_context(nc.Block(no_gpsimd_drain=True))

        @block.tensor
        def _(pe):
            for t in range(TT):
                for par in range(2):
                    lo = HD * par
                    bank = ps[:, 2 * t + par, :]
                    for pr in range(PAIRS):
                        h = 2 * pr + par
                        nc.tensor.matmul(bank[:, HD * pr:HD * pr + HD], g2[:, t, h], store["v"][:, t, HD * h:HD * h + HD],
                                         start=True, stop=False, skip_group_check=True)
                        for c in range(4):
                            n = 4 * t + c
                            before = NCH - 1 - n if d else n
                            mm = nc.tensor.matmul(bank[CH * c:CH * c + CH, HD * pr:HD * pr + HD],
                                                  g1[lo:lo + HD, pr, CH * n:CH * n + CH], st[lo:lo + HD, before, pr],
                                                  start=False, stop=True, skip_group_check=True)
                    mm.then_inc(S["y"], 1)

        @block.vector
        def _(dve):
            for t in range(TT):
                for par in range(2):
                    dve.wait_ge(S["y"], 2 * t + par + 1)
                    dst = y[:, t, :].rearrange("p (c two e) -> p two c e", two=2, e=HD)[:, par]
                    src = ps[:, 2 * t + par, 0:256].rearrange("p (c e) -> p c e", e=HD)
                    if d:
                        nc.vector.tensor_tensor(dst, src, dst, ALU.add)
                    else:
                        nc.vector.tensor_copy(dst, src)


def hyena_phase(nc, g, I, zh, yh):
    with ExitStack() as ctx:
        S = Sems(nc, ctx, "hy")

        def sb(name, shape):
            return ctx.enter_context(nc.sbuf_tensor("hy_" + name, shape, F32))
        fz = sb("fz", [P, TT, 3 * T + 1])
        gi = sb("gi", [P, 4, T])
        alt = sb("alt", [1, T])
        feat, w1, w2, w3 = sb("feat", [33, T]), sb("w1", [33, HD]), sb("w2", [HD, HD]), sb("w3", [HD, 2 * HY_W])
        decay, filt = sb("decay", [P, TT, 2 * HY_W]), sb("filt", [P, TT, 2 * HY_W])
        arg, k2 = sb("arg", [HD, T]), sb("turns", [HD, T])
        hid = sb("hid", [HD, 2, T])
        zt, absf = sb("zt", [P, TT, HY_W]), sb("abs", [P, TT, 2 * HY_W])
        zs, hs, ys = sb("zs", [P, 4, HY_W]), sb("hs", [P, 4, HY_W]), sb("ys", [P, 4, HY_W])
        ny, inorm = sb("ny", [1, 2, HY_W]), sb("inorm", [P, HY_W])
        ps, v = g.ps, nc.vector
        block = ctx.enter_context(nc.Block(no_gpsimd_drain=True))

        @block.sync
        def _(sp):
            for dst, src in ((feat[:], I["k_feat"]), (w1[:], I["hy_ffn_w1_2"][0]), (w2[:], I["hy_ffn_w2_2"][0]),
                             (w3[:], I["hy_ffn_w3_2"][0])):
                sp.dma_start(dst, src).then_inc(S["ffn_in"], 16)
            for dst, src in ((fz[:], I["k_fz"].rearrange("(t p) n -> p t n", p=P)), (gi[:], I["k_gi"].rearrange("(k p) n -> p k n", p=P)),
                             (alt[:], I["k_alt"]), (decay[:], I["k_decay"].rearrange("(t p) n -> p t n", p=P))):
                sp.dma_start(dst, src).then_inc(S["consts"], 16)

        @block.tensor
        def _(pe):
            mm_ = nc.tensor.matmul
            pe.wait_ge(S["ffn_in"], 64)
            mm_(ps[0:HD, 0, 0:T], w1[:], feat[:], start=True, stop=True).then_inc(S["ffn"], 1)
            pe.wait_ge(S["z"], 1)
            for t in range(TT):
                for c in range(4):
                    mm = nc.tensor.transpose(ps[:, 2 + t, P * c:P * c + P], zh[:, 4 + c, P * t:P * t + P], g.ident[:])
            mm.then_inc(S["zturn"], 1)
            pe.wait_ge(S["sin"], 1)
            mm_(ps[0:HD, 1, 0:T], w2[:], hid[:, 0], start=True, stop=True).then_inc(S["ffn"], 1)
            pe.wait_ge(S["zt"], 2)
            pe.wait_ge(S["consts"], 64)
            for k in range(4):
                for t in range(TT):
                    mm = mm_(ps[:, 4 + k, :], fz[:, t, P * k:P * k + P], zt[:, t], start=t == 0, stop=t == TT - 1)
            mm.then_inc(S["zspec"], 1)
            pe.wait_ge(S["sin"], 2)
            pe.wait_ge(S["turned_read"], 1)
            for t in range(TT):
                for n in range(2):
                    mm = mm_(ps[:, 2 * t + n, :], hid[:, 1, P * t:P * t + P], w3[:, 512 * n:512 * n + 512], start=True, stop=True)
            mm.then_inc(S["taps"], 1)
            pe.wait_ge(S["filt"], 1)
            for k in range(4):
                for t in range(TT):
                    for n in range(2):
                        lo = P * k if n == 0 or k < 2 else P * (k + 2)
                        mm = mm_(ps[:, k, :], fz[:, t, lo:lo + P], filt[:, t, HY_W * n:HY_W * n + HY_W],
                                 start=t == 0 and n == 0, stop=t == TT - 1 and n == 1)
            mm.then_inc(S["hspec"], 1)
            pe.wait_ge(S["zs"], 1)
            pe.wait_ge(S["abs"], 1)
            last = fz[:, :, 3 * T:3 * T + 1]
            for t in range(TT):
                mm_(ps[0:1, 4, :], last[:, t], zt[:, t], start=t == 0, stop=t == TT - 1)
            for t in range(TT):
                for n in range(2):
                    mm_(ps[0:1, 5, :], last[:, t], filt[:, t, HY_W * n:HY_W * n + HY_W], start=t == 0 and n == 0,
                        stop=t == TT - 1 and n == 1)
            for t in range(TT):
                for n in range(2):
                    mm = mm_(ps[:, 6, :], g.onesq[:], absf[:, t, HY_W * n:HY_W * n + HY_W], start=t == 0 and n == 0,
                             stop=t == TT - 1 and n == 1)
            mm.then_inc(S["norms"], 1)
            pe.wait_ge(S["ys"], 1)
            for c in range(4):
                for k in range(4):
                    mm_(ps[:, c, 0:T], ys[:, k, P * c:P * c + P], gi[:, k, :], start=k == 0, stop=False)
                mm = mm_(ps[:, c, 0:T], ny[0:1, 0, P * c:P * c + P], alt[0:1, :], start=False, stop=True)
            mm.then_inc(S["conv"], 1)

        @block.scalar
        def _(act):
            for j in range(2):
                act.wait_ge(S["arg"], j + 1)
                nc.scalar.activation(hid[:, j], arg[:], ACT.Sin).then_inc(S["sin"], 1)
                if j == 0:
                    act.wait_ge(S["zturn"], 1)
                    for t in range(TT):
                        nc.scalar.copy(zt[:, t], ps[:, 2 + t, :]).then_inc(S["zt"], 1)
            act.wait_ge(S["zspec"], 1)
            nc.scalar.copy(zs[:], ps[:, 4:8, :]).then_inc(S["zs"], 1)
            act.wait_ge(S["filt"], 1)
            nc.scalar.activation(absf[:], filt[:], ACT.Abs).then_inc(S["abs"], 1)

        @block.vector
        def _(dve):
            ch = Chain(dve, S["dve"])
            v.tensor_tensor(zh[:, 4:8], zh[:, 4:8], zh[:, 8:12], ALU.mult).then_inc(S["z"], 1)
            TWO_PI_HI, TWO_PI_LO = 6.28125, 2 * math.pi - 6.28125
            ROUND = 1.5 * 2 ** 23
            f0 = HY64_ROW
            for j in range(2):
                dve.wait_ge(S["ffn"], j + 1)
                if j:
                    dve.wait_ge(S["sin"], 1)
                ch(v.tensor_scalar(arg[:], ps[0:HD, j, 0:T], g.va[0:HD, f0 + 1 + j:f0 + 2 + j], g.va[0:HD, f0:f0 + 1], ALU.add, ALU.mult))
                ch(v.tensor_scalar(k2[:], arg[:], 1 / (2 * math.pi), ROUND, ALU.mult, ALU.add))
                ch(v.tensor_scalar(k2[:], k2[:], -ROUND, None, ALU.add))
                ch(v.scalar_tensor_tensor(arg[:], k2[:], -TWO_PI_HI, arg[:], ALU.mult, ALU.add))
                ch(v.scalar_tensor_tensor(arg[:], k2[:], -TWO_PI_LO, arg[:], ALU.mult, ALU.add))
                if j:
                    v.tensor_scalar(k2[:, 0:1], ps[0:HD, j, 0:1], 0.0, None, ALU.mult).then_inc(S["turned_read"], 1)
                v.tensor_scalar(arg[:], arg[:], 3.1415925, -3.1415925, ALU.min, ALU.max).then_inc(S["arg"], 1)
            dve.wait_ge(S["taps"], 1)
            dve.wait_ge(S["consts"], 64)
            v.tensor_tensor(filt[:].rearrange("p t n -> p (t n)"), ps[:, 0:4, :].rearrange("p b n -> p (b n)"),
                            decay[:].rearrange("p t n -> p (t n)"), ALU.mult).then_inc(S["filt"], 1)
            dve.wait_ge(S["norms"], 1)
            ch(v.reciprocal(inorm[:], ps[:, 6, :]))
            ch(v.tensor_tensor(hs[:], ps[:, 0:4, :], inorm[:].unsqueeze(1).to_broadcast([P, 4, HY_W]), ALU.mult))
            ch(v.tensor_copy(ny[0:1, 0], ps[0:1, 4, :]))
            ch(v.tensor_tensor(ny[0:1, 1], ps[0:1, 5, :], inorm[0:1, :], ALU.mult))
            ch(v.tensor_tensor(ny[0:1, 0], ny[0:1, 0], ny[0:1, 1], ALU.mult))
            ch.add(v.tensor_tensor(ys[:, 0:2], zs[:, 0:2], hs[:, 0:2], ALU.mult))
            ch.add(v.tensor_tensor(ys[:, 2:4], zs[:, 0:2], hs[:, 2:4], ALU.mult))
            ch.sync()
            a3 = absf[:].rearrange("p t (a n) -> p (t a) n", n=HY_W)
            ch.add(v.tensor_tensor(a3[:, 0:2], zs[:, 2:4], hs[:, 2:4], ALU.mult))
            ch.add(v.tensor_tensor(a3[:, 2:4], zs[:, 2:4], hs[:, 0:2], ALU.mult))
            ch.sync()
            ch(v.tensor_tensor(ys[:, 0:2], ys[:, 0:2], a3[:, 0:2], ALU.subtract))
            v.tensor_tensor(ys[:, 2:4], ys[:, 2:4], a3[:, 2:4], ALU.add).then_inc(S["ys"], 1)
            dve.wait_ge(S["conv"], 1)
            for c in range(4):
                ch(v.scalar_tensor_tensor(yh[:, c], zh[:, 4 + c], col(g, "hy_bias_2", c), ps[:, c, 0:T], ALU.mult, ALU.add))
            ch(v.tensor_tensor(yh[:], yh[:], zh[:, 0:4], ALU.mult))


def merge_phase(nc, g, I, z, yh, store):
    with ExitStack() as ctx:
        S = Sems(nc, ctx, "mg")

        def sb(name, shape):
            return ctx.enter_context(nc.sbuf_tensor("mg_" + name, shape, F32))
        gates, post = sb("gates", [P, TT, 2 * D]), sb("post", [P, D])
        lng, lnb, gup = sb("lng", [P, RW_WIDTH]), sb("lnb", [P, RW_WIDTH]), sb("gup", [P, RW_WIDTH])
        hsel = sb("hsel", [P, 2])
        slg, q, yt = sb("slg", [P, T]), sb("q", [P, PAIRS, T]), sb("yt", [P, PAIRS, T])
        cen, sq, st = sb("cen", [P, TT, RW_WIDTH]), sb("sq", [P, TT, RW_WIDTH]), sb("st", [P, TT, 4, RW_HEADS])
        mixed, tmp = sb("mixed", [P, TT, D]), sb("tmp", [P, TT, D])
        ss = sb("ss", [P, 8])
        y, vt = store["y"], store["v"]
        ps, v = g.ps, nc.vector
        i0, hy0, rw0, out0 = (g.stream.first[n] for n in ("w_gates", "hy_proj", "rw_proj", "w_out_2"))
        block = ctx.enter_context(nc.Block(no_gpsimd_drain=True))

        def heads(x):
            return x.rearrange("p t (h e) -> p t h e", e=HD)

        def per_head(x):
            return x.unsqueeze(3).to_broadcast([P, TT, RW_HEADS, HD])

        @block.sync
        def _(sp):
            for dst, src in ((lng[:], I["rw_ln_g_2"].to_broadcast([P, RW_WIDTH])), (lnb[:], I["rw_ln_b_2"].to_broadcast([P, RW_WIDTH])),
                             (gup[:], I["rw_g_up_2"][0]), (hsel[:], I["k_headsel"]), (post[:], g.post_dram[:, 0])):
                sp.dma_start(dst, src).then_inc(S["consts"], 16)
            load_tiles(g, sp, out0 + 4 + R)

        @block.tensor
        def _(pe):
            mm_ = nc.tensor.matmul
            for i in range(8):
                wait_tile(g, pe, i0 + i)
                w = tile3(g, i0 + i, KC)
                if i >= 2:
                    pe.wait_ge(S["gates"], i - 1)
                for t in range(TT):
                    for k in range(KC):
                        mm = mm_(ps[:, i % 2, 256 * t:256 * t + 256], g.xt[:, k, P * t:P * t + P], w[:, k, :], start=k == 0, stop=k == KC - 1)
                mm.then_inc(g.tiles_used, 1)
            pe.wait_ge(S["consts"], 80)
            pe.wait_ge(S["slg"], 1)
            pe.wait_ge(S["q"], 1)
            pe.wait_ge(S["gates"], 8)
            for t in range(TT):
                mm_(ps[:, 2 + t, :], slg[:, P * t:P * t + P], gup[:], start=True, stop=True)
                for c in range(PAIRS):
                    mm = mm_(ps[:, 0, 8 * t + 2 * c:8 * t + 2 * c + 2], q[:, c, P * t:P * t + P], hsel[:], start=True, stop=True)
            mm.then_inc(S["rwgate"], 1)
            token_product(nc, g, pe, yh, hy0, 2)
            pe.wait_ge(S["yrw"], 1)
            for t in range(TT):
                for c in range(PAIRS):
                    mm = nc.tensor.transpose(ps[:, 1 + t, P * c:P * c + P], y[:, t, P * c:P * c + P], g.ident[:])
            mm.then_inc(S["yturn"], 1)
            pe.wait_ge(S["yt"], 2)
            pe.wait_ge(S["hy_read"], 2)
            token_product(nc, g, pe, yt, rw0, 2)
            pe.wait_ge(S["mixed"], TT)
            turn_rows(nc, g, pe, S, mixed, "mt", KC)
            pe.wait_ge(S["mt"], 4)
            token_product(nc, g, pe, g.xt, out0, 4)

        @block.scalar
        def _(act):
            nc.scalar.activation(slg[:], z[:, 13, :], ACT.Sigmoid).then_inc(S["slg"], 1)
            for i in range(8):
                act.wait_ge(g.tiles_used, i0 + i + 1)
                nc.scalar.activation(gates[:, :, 256 * i:256 * i + 256],
                                     ps[:, i % 2, :].rearrange("p (t n) -> p t n", t=TT), ACT.Sigmoid).then_inc(S["gates"], 1)
            act.wait_ge(S["var"], 1)
            nc.scalar.activation(st[:, :, 2], st[:, :, 1], ACT.Sqrt).then_inc(S["root"], 1)
            act.wait_ge(S["yturn"], 1)
            for t in range(TT):
                nc.scalar.copy(yt[:, :, P * t:P * t + P], ps[:, 1 + t, :].rearrange("p (c n) -> p c n", c=PAIRS)).then_inc(S["yt"], 1)
            copy_turned_rows(nc, g, act, nc.scalar.copy, S, g.xt, "mt", KC)
            act.wait_ge(g.tiles_used, out0 + 4)
            for t in range(TT):
                nc.scalar.activation(tmp[:, t].rearrange("p (b n) -> p b n", b=2), ps[:, 4 + 2 * t:6 + 2 * t, :], ACT.Square,
                                     accum_out=ss[:, t:t + 1]).then_inc(S["ss"], 1)
            act.wait_ge(S["mean"], 1)
            nc.scalar.activation(ss[:, 4:6], ss[:, 2:4], ACT.Sqrt).then_inc(S["root2"], 1)

        @block.vector
        def _(dve):
            ch = Chain(dve, S["dve"])
            for c in range(PAIRS):
                ch(v.scalar_tensor_tensor(q[:, c], z[:, c], col(g, "rw_r_k_2", c), store["kmod"][:, c], ALU.mult, ALU.mult))
            v.memset(ss[:, 6:8], 0.0).then_inc(S["q"], 1)
            ch(v.tensor_reduce(st[:, :, 0], heads(y[:]), AX_X, ALU.add))
            ch(v.tensor_scalar(st[:, :, 0], st[:, :, 0], 1.0 / HD, None, ALU.mult))
            for t in range(TT):
                m3 = st[:, t, 0].unsqueeze(2).to_broadcast([P, RW_HEADS, HD])
                ch(v.tensor_tensor(cen[:, t].rearrange("p (h e) -> p h e", e=HD), y[:, t].rearrange("p (h e) -> p h e", e=HD), m3, ALU.subtract))
            ch(v.tensor_tensor(sq[:], cen[:], cen[:], ALU.mult))
            ch(v.tensor_reduce(st[:, :, 1], heads(sq[:]), AX_X, ALU.add))
            v.tensor_scalar(st[:, :, 1], st[:, :, 1], 1.0 / HD, LN_EPS, ALU.mult, ALU.add).then_inc(S["var"], 1)
            dve.wait_ge(S["root"], 1)
            ch(v.reciprocal(st[:, :, 2], st[:, :, 2]))
            dve.wait_ge(S["consts"], 80)
            dve.wait_ge(S["rwgate"], 1)
            ch(v.tensor_copy(st[:, :, 3], ps[:, 0, 0:16].rearrange("p (t h) -> p t h", t=TT)))
            for t in range(TT):
                c3, y3 = (x[:, t].rearrange("p (h e) -> p h e", e=HD) for x in (cen, y))
                ch(v.tensor_tensor(c3, c3, st[:, t, 2].unsqueeze(2).to_broadcast([P, RW_HEADS, HD]), ALU.mult))
                ch(v.tensor_tensor(cen[:, t], cen[:, t], lng[:], ALU.mult))
                ch(v.tensor_tensor(cen[:, t], cen[:, t], lnb[:], ALU.add))
                ch(v.tensor_tensor(y3, vt[:, t].rearrange("p (h e) -> p h e", e=HD), st[:, t, 3].unsqueeze(2).to_broadcast([P, RW_HEADS, HD]), ALU.mult))
                ch(v.tensor_tensor(y[:, t], y[:, t], cen[:, t], ALU.add))
                ins = v.tensor_tensor(y[:, t], y[:, t], ps[:, 2 + t, :], ALU.mult)
                ins.then_inc(S["yrw"], 1) if t else ch(ins)
            dve.wait_ge(g.tiles_used, hy0 + 2)
            for t in range(TT):
                bank = ps[:, 4 + 2 * t:6 + 2 * t, :].rearrange("p b n -> p (b n)")
                v.tensor_tensor(mixed[:, t], bank, gates[:, t, 0:D], ALU.mult).then_inc(S["hy_read"], 1)
            dve.wait_ge(g.tiles_used, rw0 + 2)
            for t in range(TT):
                bank = ps[:, 4 + 2 * t:6 + 2 * t, :].rearrange("p b n -> p (b n)")
                ch(v.tensor_tensor(tmp[:, t], bank, gates[:, t, D:2 * D], ALU.mult))
                v.tensor_tensor(mixed[:, t], mixed[:, t], tmp[:, t], ALU.add).then_inc(S["mixed"], 1)
            dve.wait_ge(S["ss"], TT)
            v.tensor_scalar(ss[:, 2:4], ss[:, 0:2], 1.0 / D, EPS, ALU.mult, ALU.add).then_inc(S["mean"], 1)
            dve.wait_ge(S["root2"], 1)
            ch(v.reciprocal(ss[:, 4:6], ss[:, 4:6]))
            for t in range(TT):
                bank = ps[:, 4 + 2 * t:6 + 2 * t, :].rearrange("p b n -> p (b n)")
                ch(v.scalar_tensor_tensor(tmp[:, t], bank, ss[:, 4 + t:5 + t], post[:], ALU.mult, ALU.mult))
                ch(v.tensor_tensor(g.x[:, t], g.x[:, t], tmp[:, t], ALU.add))


def router_phase(nc, g, I, xet, mt, aff):
    with ExitStack() as ctx:
        S = Sems(nc, ctx, "rt")

        def sb(name, shape):
            return ctx.enter_context(nc.sbuf_tensor("rt_" + name, shape, F32))
        rw, iota = sb("w", [P, KC, NE]), sb("iota", [P, CAP])
        st, at = sb("st", [P, TT, 4]), sb("at", [NE, T])
        work, top, cnt, sel = sb("work", [NE, T]), sb("top", [NE, 8]), sb("cnt", [NE, 4]), sb("sel", [NE, 3, T])
        pick = sb("pick", [P, TT, NE, CAP])
        ps, v = g.ps, nc.vector
        act_n, dve_n, pe_n = rms_transposed(g, nc, S, g.x, g.xt, g.scale[:, 2, :], g.shift[:, 2, :])
        block = ctx.enter_context(nc.Block(no_gpsimd_drain=True))

        @block.sync
        def _(sp):
            sp.dma_start(rw[:], I["router_w_2"][0].rearrange("(k p) e -> p k e", p=P)).then_inc(S["consts"], 16)
            sp.dma_start(iota[:], I["k_iota"]).then_inc(S["consts"], 16)

        @block.tensor
        def _(pe):
            pe_n(pe)
            pe.wait_ge(S["consts"], 32)
            for t in range(TT):
                for k in range(KC):
                    mm = nc.tensor.matmul(ps[:, 2, NE * t:NE * t + NE], g.xt[:, k, P * t:P * t + P], rw[:, k], start=k == 0, stop=k == KC - 1)
            mm.then_inc(S["logits"], 1)
            pe.wait_ge(S["aff"], 1)
            for t in range(TT):
                mm = nc.tensor.transpose(ps[0:NE, 3, P * t:P * t + P], aff[:, t], g.ident[:])
            mm.then_inc(S["afft"], 1)
            pe.wait_ge(S["slots"], 1)
            for t in range(TT):
                mm = nc.tensor.transpose(ps[:, 4, NE * t:NE * t + NE], sel[:, 0, P * t:P * t + P], g.ident[0:NE, 0:NE])
            mm.then_inc(S["slott"], 1)
            pe.wait_ge(S["pick"], TT)
            for k in range(KC):
                if k >= 2:
                    pe.wait_ge(S["xet"], k - 1)
                for t in range(TT):
                    mm = nc.tensor.matmul(ps[:, 5 + k % 2, :], g.xn[:, t, P * k:P * k + P], pick[:, t].rearrange("p e s -> p (e s)"),
                                          start=t == 0, stop=t == TT - 1)
                mm.then_inc(S["gathered"], 1)

        @block.scalar
        def _(act):
            act_n(act)
            act.wait_ge(S["max"], 1)
            for t in range(TT):
                nc.scalar.activation(aff[:, t], ps[:, 2, NE * t:NE * t + NE], ACT.Exp, bias=st[:, t, 1:2],
                                     accum_out=st[:, t, 2:3]).then_inc(S["exp"], 1)

        @block.vector
        def _(dve):
            ch = Chain(dve, S["dve"])
            dve_n(dve, ch)
            dve.wait_ge(S["logits"], 1)
            ch(v.tensor_reduce(st[:, :, 0], ps[:, 2, 0:2 * NE].rearrange("p (t e) -> p t e", t=TT), AX_X, ALU.max))
            v.tensor_scalar(st[:, :, 1], st[:, :, 0], -1.0, None, ALU.mult).then_inc(S["max"], 1)
            dve.wait_ge(S["exp"], TT)
            ch(v.reciprocal(st[:, :, 3], st[:, :, 2]))
            v.tensor_tensor(aff[:], aff[:], st[:, :, 3:4].to_broadcast([P, TT, NE]), ALU.mult).then_inc(S["aff"], 1)
            dve.wait_ge(S["afft"], 1)
            ch(v.tensor_copy(at[:], ps[0:NE, 3, 0:T]))
            first_by_rank(nc, ch, at[:], work[:], top, sel, cnt, CAP, g.ones[0:NE, :])
            ch(v.tensor_tensor_scan(sel[:, 2], g.ones[0:NE, :], sel[:, 0], 0.0, ALU.mult, ALU.add))
            v.tensor_tensor(sel[:, 0], sel[:, 0], sel[:, 2], ALU.mult).then_inc(S["slots"], 1)
            dve.wait_ge(S["slott"], 1)
            dve.wait_ge(S["consts"], 32)
            ch(v.tensor_copy(mt[:], ps[:, 4, 0:2 * NE].rearrange("p (t e) -> p t e", t=TT)))
            for t in range(TT):
                v.tensor_tensor(pick[:, t], mt[:, t].unsqueeze(2).to_broadcast([P, NE, CAP]),
                                iota[:].unsqueeze(1).to_broadcast([P, NE, CAP]), ALU.is_equal).then_inc(S["pick"], 1)
            for k in range(KC):
                dve.wait_ge(S["gathered"], k + 1)
                v.tensor_scalar(xet[:, k, :], ps[:, 5 + k % 2, :], g.scale[:, 2, k:k + 1], g.shift[:, 2, k:k + 1],
                                ALU.mult, ALU.add).then_inc(S["xet"], 1)


def expert_phase(nc, g, I, xet, mt, aff, out_dram):
    with ExitStack() as ctx:
        S = Sems(nc, ctx, "ex")

        def sb(name, shape):
            return ctx.enter_context(nc.sbuf_tensor("ex_" + name, shape, F32))
        xe = sb("xe", [P, KC, CAP])
        silu, hid, ht = sb("silu", [P, 512]), sb("hid", [P, 512]), sb("ht", [P, 4, P])
        wsel, wselt = sb("wsel", [P, TT, 4, CAP]), sb("wselt", [P, T])
        iota, ye, zero = sb("iota", [P, CAP]), sb("ye", [P, 512]), sb("zero", [P, 512])
        ss, post, tmp = sb("ss", [P, 8]), sb("post", [P, D]), sb("tmp", [P, TT, D])
        ps, v = g.ps, nc.vector
        e0 = g.stream.first["experts"]
        TPE = 3 * KC
        block = ctx.enter_context(nc.Block(no_gpsimd_drain=True))

        def slot(j):
            return (e0 + j) % R

        def loaded(e, j):
            return 16 * ((e0 + j) // R + 1) + e * (16 * TPE // R)

        ahead = g.issued - e0

        @block.sync
        def _(sp):
            sp.dma_start(iota[:], I["k_iota"]).then_inc(S["consts"], 16)
            sp.dma_start(post[:], g.post_dram[:, 1]).then_inc(S["consts"], 16)
            w1, w3 = I["exp_w1_2"][0], I["exp_w3_2"][0]
            w2 = I["exp_w2_2"][0].rearrange("e (h k p) n -> p k (e h) n", h=2, p=P)

            def load(e, j, static=True):
                if j < 2 * KC:
                    w = (w1, w3)[j // KC].rearrange("e (k p) f -> p (e k) f", p=P)
                    kk = KC * e + j % KC
                    src = w[:, kk, :] if static else w[:, bass.ds(kk, 1), :]
                    dst = g.ring[:, slot(j), :] if static else g.ring[:, slot(j), :].unsqueeze(1)
                else:
                    src = w2[:, j % KC, 2 * e:2 * e + 2, :] if static else w2[:, j % KC, bass.ds(2 * e, 2), :]
                    dst = g.ring[:, slot(j), :].rearrange("p (h n) -> p h n", h=2)
                return sp.dma_start(dst, src).then_inc(g.tile_loaded[slot(j)], 16)

            for j in range(ahead, TPE):
                sp.wait_ge(g.tiles_used, e0 + j - R + 1)
                load(0, j)
            with sp.Fori(1, NE) as e:
                for j in range(TPE):
                    sp.wait_ge(g.tiles_used, e * TPE + (e0 + j - R + 1))
                    load(e, j, False)
            for t in range(TT):
                sp.wait_ge(S["done"], t + 1)
                sp.dma_start(out_dram[P * t:P * t + P, :], g.x[:, t]).then_inc(S["out"], 16)
            sp.wait_ge(S["out"], 16 * TT)

        @block.tensor
        def _(pe):
            mm_ = nc.tensor.matmul
            pe.wait_ge(S["zeroed"], 1)
            for b in range(4):
                mm_(ps[:, b, :], zero[:, 0:P], zero[:], start=True, stop=False, skip_group_check=True)
            with pe.Fori(0, NE) as e:
                pe.wait_ge(S["xe"], e + 1)
                for u in range(2):
                    for k in range(KC):
                        j = KC * u + k
                        pe.wait_ge(g.tile_loaded[slot(j)], loaded(e, j))
                        for q in range(4):
                            mm = mm_(ps[32 * q:32 * q + 32, 4 + u, :], xe[:, k], g.ring[:, slot(j), 512 * q:512 * q + 512],
                                     start=k == 0, stop=k == KC - 1)
                        mm.then_inc(g.tiles_used, 1)
                pe.wait_ge(S["wsel"], e + 1)
                for t in range(TT):
                    mm = nc.tensor.transpose(ps[:, 6, P * t:P * t + P], wsel[:, t].rearrange("p q s -> p (q s)"), g.ident[:])
                mm.then_inc(S["wturn"], 1)
                pe.wait_ge(S["wselt"], e + 1)
                pe.wait_ge(S["hid"], e + 1)
                for c in range(4):
                    mm = nc.tensor.transpose(ps[:, 6, P * c:P * c + P], hid[:, P * c:P * c + P], g.ident[:])
                mm.then_inc(S["hturn"], 1)
                pe.wait_ge(S["ht"], e + 1)
                for k in range(KC):
                    j = 2 * KC + k
                    pe.wait_ge(g.tile_loaded[slot(j)], loaded(e, j))
                    w = g.ring[:, slot(j), :].rearrange("p (h n) -> p h n", h=2)
                    for n in range(2):
                        for h in range(2):
                            q, f = 2 * n + h, 2 * h + k // 4
                            mm = mm_(ps[32 * q:32 * q + 32, 7, :], ht[:, k % 4, CAP * f:CAP * f + CAP], w[:, h, 512 * n:512 * n + 512],
                                     start=k == 0, stop=k == KC - 1)
                    mm.then_inc(g.tiles_used, 1)
                pe.wait_ge(S["ye"], e + 1)
                for t in range(TT):
                    for n in range(2):
                        mm = mm_(ps[:, 2 * t + n, :], wselt[64 * n:64 * n + 64, P * t:P * t + P], ye[64 * n:64 * n + 64, :],
                                 start=False, stop=False, skip_group_check=True)
                mm.then_inc(S["added"], 1)

        @block.scalar
        def _(act):
            with act.Fori(0, NE) as e:
                act.wait_ge(g.tiles_used, e * TPE + (e0 + KC))
                nc.scalar.activation(silu[:], ps[:, 4, :], ACT.Silu).then_inc(S["silu"], 1)
                act.wait_ge(S["wturn"], e + 1)
                nc.scalar.copy(wselt[:], ps[:, 6, 0:T]).then_inc(S["wselt"], 1)
                act.wait_ge(S["hturn"], e + 1)
                nc.scalar.copy(ht[:], ps[:, 6, :].rearrange("p (c q) -> p c q", c=4)).then_inc(S["ht"], 1)
                act.wait_ge(g.tiles_used, e * TPE + (e0 + TPE))
                nc.scalar.copy(ye[:], ps[:, 7, :]).then_inc(S["ye"], 1)
            act.wait_ge(S["added"], NE)
            for t in range(TT):
                nc.scalar.activation(tmp[:, t].rearrange("p (b n) -> p b n", b=2), ps[:, 2 * t:2 * t + 2, :], ACT.Square,
                                     accum_out=ss[:, t:t + 1]).then_inc(S["ss"], 1)
            act.wait_ge(S["mean"], 1)
            nc.scalar.activation(ss[:, 4:6], ss[:, 2:4], ACT.Sqrt).then_inc(S["root"], 1)

        @block.vector
        def _(dve):
            ch = Chain(dve, S["dve"])
            v.memset(zero[:], 0.0).then_inc(S["zeroed"], 1)
            dve.wait_ge(S["consts"], 32)

            def prepare(e, static):
                one = (lambda x, i, n: x[:, :, i:i + n]) if static else (lambda x, i, n: x[:, :, bass.ds(i, n)])
                v.tensor_copy(xe[:], one(xet, e * CAP, CAP)).then_inc(S["xe"], 1)
                for t in range(TT):
                    m = (mt[:, t, e:e + 1] if static else mt[:, t, bass.ds(e, 1)])
                    a = (aff[:, t, e:e + 1] if static else aff[:, t, bass.ds(e, 1)])
                    ins = v.scalar_tensor_tensor(wsel[:, t], iota[:].unsqueeze(1).to_broadcast([P, 4, CAP]), m,
                                                 a.unsqueeze(1).to_broadcast([P, 4, CAP]), ALU.is_equal, ALU.mult)
                ins.then_inc(S["wsel"], 1)

            prepare(0, True)

            def hidden(e):
                dve.wait_ge(S["silu"], e + 1)
                dve.wait_ge(g.tiles_used, e * TPE + (e0 + 2 * KC))
                v.tensor_tensor(hid[:], ps[:, 5, :], silu[:], ALU.mult).then_inc(S["hid"], 1)

            with dve.Fori(0, NE - 1) as e:
                hidden(e)
                dve.wait_ge(S["wturn"], e + 1)
                prepare(e + 1, False)
            hidden(NE - 1)
            dve.wait_ge(S["ss"], TT)
            v.tensor_scalar(ss[:, 2:4], ss[:, 0:2], 1.0 / D, EPS, ALU.mult, ALU.add).then_inc(S["mean"], 1)
            dve.wait_ge(S["root"], 1)
            ch(v.reciprocal(ss[:, 4:6], ss[:, 4:6]))
            for t in range(TT):
                bank = ps[:, 2 * t:2 * t + 2, :].rearrange("p b n -> p (b n)")
                ch(v.scalar_tensor_tensor(tmp[:, t], bank, ss[:, 4 + t:5 + t], post[:], ALU.mult, ALU.mult))
                v.tensor_tensor(g.x[:, t], g.x[:, t], tmp[:, t], ALU.add).then_inc(S["done"], 1)


def second_block(nc, g, I, out_dram, dump=None):
    with ExitStack() as ctx:
        def sb(name, shape):
            return ctx.enter_context(nc.sbuf_tensor(name, shape, F32))
        g.mod, g.scale, g.shift, g.own = sb("mod", [P, 96]), sb("scale", [P, 3, KC]), sb("shift", [P, 3, KC]), sb("own", [P, RWC])
        with ExitStack() as rec:
            def sr(name, shape):
                return rec.enter_context(nc.sbuf_tensor(name, shape, F32))
            g.masks, g.blockones, g.blk16 = sr("masks", [P, 2, 4 * P]), sr("blockones", [P, P]), sr("blk16", [P, P])
            g.restart, g.ident2 = sr("restart", [P, T]), sr("ident2", [P, HD])
            with ExitStack() as c1:
                modulation_phase(nc, g, I)
            z, yh = sr("z", [P, RWC, T]), sr("yh", [P, 4, T])
            store = {"v": sr("vtok", [P, TT, RW_WIDTH]), "kmod": sr("kmod", [P, PAIRS, T]),
                     "carry": sr("carry", [P, 2, PAIRS, HD]), "y": sr("yrw", [P, TT, RW_WIDTH])}
            with ExitStack() as c1:
                g.xn = c1.enter_context(nc.sbuf_tensor("xn_ctx", [P, TT, D], F32))
                context_phase(nc, g, I, z)
            recurrence_phase(nc, g, I, z, store, True, "rc")
            with ExitStack() as c1:
                zh = c1.enter_context(nc.sbuf_tensor("zh", [P, HYC, T], F32))
                with ExitStack() as c2:
                    g.xn = c2.enter_context(nc.sbuf_tensor("xn_lat", [P, TT, D], F32))
                    project_phase(nc, g, I, z, zh)
                with ExitStack() as c2:
                    g.onesq = c2.enter_context(nc.sbuf_tensor("onesq", [P, P], F32))
                    with nc.semaphore("ones_set") as s1, nc.Block(no_gpsimd_drain=True) as block:
                        @block.vector
                        def _(dve):
                            nc.vector.memset(g.onesq[:], 1.0).then_inc(s1, 1)
                    hyena_phase(nc, g, I, zh, yh)
            recurrence_phase(nc, g, I, z, store, False, "rl")
            merge_phase(nc, g, I, z, yh, store)
        if dump:
            dump("d")
        xet, mt, aff = sb("xet", [P, KC, NE * CAP]), sb("mt", [P, TT, NE]), sb("aff", [P, TT, NE])
        with ExitStack() as c1:
            g.xn = c1.enter_context(nc.sbuf_tensor("xn_moe", [P, TT, D], F32))
            router_phase(nc, g, I, xet, mt, aff)
        expert_phase(nc, g, I, xet, mt, aff, out_dram)


def constants_2():
    f32 = np.float32
    sel = np.zeros((P, 2 + P), f32)
    sel[0::32, 0], sel[1::32, 1], sel[0::32, 2:] = 1, 1, 1
    p = np.arange(P)
    same = p[:, None] // CH == p[None, :] // CH
    masks = []
    for d in range(2):
        before = (p[:, None] < p[None, :]) if d == 0 else (p[:, None] > p[None, :])
        strict = same & before
        masks.append(np.concatenate([strict, strict | np.eye(P, dtype=bool), strict.T, strict.T], axis=1))
    blk16 = p[:, None] // 16 == p[None, :] // 16
    blockones = p[:, None] // HD == p[None, :] // HD
    restart = np.ones((P, T), f32)
    restart[:, ::CH] = 0
    ident2 = np.concatenate([np.eye(HD), np.eye(HD)]).astype(f32)
    t = np.arange(T)
    ang = 2 * np.pi * ((t[:, None] * t[None, :]) % FREQ) / FREQ
    sign = (1.0 - 2.0 * (t % 2))
    fz = np.concatenate([np.cos(ang), np.sin(ang), -np.sin(ang), sign[:, None]], axis=1)
    w = np.where(t == 0, 1.0, 2.0)[:, None] / FREQ
    gi = np.concatenate([np.cos(ang) * w, np.sin(ang) * w], axis=0)
    tl = np.linspace(0.0, 1.0, T, dtype=f32)[:, None]
    an = f32(2.0 * math.pi / T) * np.arange(T, dtype=f32)[:, None]
    bands = np.linspace(1e-4, 15, 16, dtype=f32)
    feat = np.concatenate([tl, np.cos(bands * an), -np.sin(bands * an)], axis=-1)
    deltas = np.abs(np.linspace(math.log(1e-2) / 1.5, math.log(1e-2) / 0.3, HY_W, dtype=f32))
    decay = np.exp(-tl * deltas)
    decay = np.concatenate([decay, np.where(t[:, None] == 0, 0, decay)], axis=1)
    headsel = (p[:, None] // HD == np.arange(2)[None, :])
    iota = np.tile(np.arange(1, CAP + 1), (P, 1))
    out = {"k_modsel": sel, "k_masks": np.concatenate(masks, axis=1), "k_blk16": blk16, "k_blockones": blockones,
           "k_restart": restart, "k_ident2": ident2, "k_fz": fz, "k_gi": gi, "k_alt": sign[None, :] / FREQ, "k_feat": feat.T,
           "k_decay": decay, "k_headsel": headsel, "k_iota": iota}
    return {k: np.ascontiguousarray(v.astype(f32)) for k, v in out.items()}


_INS = ["x", "rel_bias", "ffn1_norm", "ffn1_w_gate", "ffn1_w_up", "ffn1_w_down", "mix_norm", "w_in", "qk_gain", "diff_lambda",
        "diff_out_norm", "w_branch_a", "w_branch_b", "w_branch_c", "w_out", "ffn2_norm", "ffn2_w_gate", "ffn2_w_up",
        "ffn2_w_down", "c_2", "ctx_2", "c_ctx_2", "mod_w_2", "mod_b_2", "norm1_pre_2", "norm1_post_2", "norm2_pre_2",
        "norm2_post_2", "w_in_2", "hy_conv_w_2", "hy_conv_b_2", "hy_ffn_w1_2", "hy_ffn_b1_2", "hy_ffn_w2_2", "hy_ffn_b2_2",
        "hy_ffn_w3_2", "hy_freq_2", "hy_bias_2", "hy_proj_2", "rw_mu_2", "rw_w0_2", "rw_w_up_2", "rw_a0_2", "rw_a_up_2",
        "rw_g_up_2", "rw_k_k_2", "rw_k_a_2", "rw_r_k_2", "rw_ln_g_2", "rw_ln_b_2", "rw_proj_2", "w_out_2", "router_w_2",
        "exp_w1_2", "exp_w3_2", "exp_w2_2"]


def two_blocks(nc, I, out):
    g = G()
    g.I = I
    g.stream = Stream()
    first_stream(g.stream, I)
    second_stream(g.stream, I)
    g.bias_dram = nc.dram_tensor("bias_by_distance", [BIAS_HEADS, DIST], F32).ap()
    g.post_dram = nc.dram_tensor("gated_post_norms", [P, 2, D], F32).ap()
    with ExitStack() as ctx:
        allocate(nc, ctx, g)
        with ExitStack() as first:
            first_block(nc, g, I, first)
        second_block(nc, g, I, out.rearrange("b t d -> (b t) d"))


def kernel(**inputs):
    import concourse.bacc as bacc
    from concourse.bass_utils import run_bass_kernel_spmd

    nc = bacc.Bacc("TRN2", target_bir_lowering=False, num_devices=1)
    arrays, I = {}, {}
    for name in _INS:
        a = np.ascontiguousarray(inputs[name])
        arrays[f"in_{name}"] = a
        I[name] = nc.dram_tensor(f"in_{name}", a.shape, mybir.dt.from_np(a.dtype), kind="ExternalInput").ap()
    for name, a in (constants() | constants_2()).items():
        arrays[name] = a
        I[name] = nc.dram_tensor(name, a.shape, mybir.dt.from_np(a.dtype), kind="ExternalInput").ap()
    out = nc.dram_tensor("out_x", (1, T, D), F32, kind="ExternalOutput").ap()
    two_blocks(nc, I, out)
    r = run_bass_kernel_spmd(nc, [arrays], core_ids=[0])
    return r.results[0]["out_x"]
```

```python
import math
from contextlib import ExitStack

import concourse.bass as bass
import numpy as np
from concourse import mybir

P = 128
T = 256
TT = T // P
D = 1024
KC = D // P
D_FF = 2816
FC = D_FF // P
HD = 64
N_IN = 7880
A_COL, BQK_COL, BV_COL, C_COL, IX_COL, GATE_COL = 0, 2304, 3328, 3840, 4224, 4808
A_HEADS, B_HEADS, C_HEADS, IDX_HEADS = 12, 4, 4, 8
BIAS_HEADS = 20
NUM_BUCKETS, MAX_DISTANCE = 32, 2048
TOP_KEYS = 64
LAM_INIT = 0.8 - 0.6 * math.exp(-0.3 * 0)
EPS = 1e-6
MASKED = -1e30
HY_COLS, RW_COLS, GATE2_COLS = 1536, 1792, 2048
IN2_COLS = HY_COLS + RW_COLS + GATE2_COLS
HYC, RWC = HY_COLS // P, RW_COLS // P
RW_WIDTH = 512
STATE_LO, STATE_HI = RW_WIDTH, 3 * RW_WIDTH + 128
HY_W = 512
NE, CAP, D_EXP = 16, 32, 2048
DIST = 383

ALU = mybir.AluOpType
ACT = mybir.ActivationFunctionType
F32 = mybir.dt.float32
F32R = mybir.dt.float32r
AX_X = mybir.AxisListType.X
AX_XY = mybir.AxisListType.XY

WT = 2048
R = 4
H = 3


class Stream:

    def __init__(self):
        self.src, self.first, self.kinds = [], {}, []

    def mark(self, name):
        self.first[name] = len(self.src)

    def add(self, n, src, kind="split"):
        self.src.append((n, src))
        self.kinds.append(kind)

    def count(self, i, kind):
        return self.kinds[:i + 1].count(kind)

    def columns(self, name, w, c0, c1, kind="split"):
        self.mark(name)
        for c in range(c0, c1, 256):
            n = min(256, c1 - c)
            self.add(KC * n, w[:, c:c + n].rearrange("(k p) n -> p k n", p=P), kind)

    def rows(self, name, w):
        self.mark(name)
        chunks = w.rearrange("(k p) n -> p k n", p=P)
        for i in range(chunks.shape[1] // 2):
            self.add(WT, chunks[:, 2 * i:2 * i + 2, :])


VEC_A = ["ffn1_norm", "mix_norm", "ffn2_norm", "norm1_pre_2", "norm2_pre_2", "c_2", "c_ctx_2", "mod_b_2",
         "diff_out_norm", "qk_gain"]
VEC_A_ROWS = [8, 8, 8, 8, 8, 8, 8, 48, 1, 6]
VEC_B = ["hy_conv_w_2", "hy_conv_b_2", "hy_bias_2", "rw_mu_2", "rw_w0_2", "rw_a0_2", "rw_k_k_2", "rw_k_a_2", "rw_r_k_2"]
VEC_B_ROWS = [36, 12, 4, 28, 8, 8, 4, 4, 4]
ROW_A = {n: sum(VEC_A_ROWS[:i]) for i, n in enumerate(VEC_A)}
ROW_B = {n: sum(VEC_B_ROWS[:i]) for i, n in enumerate(VEC_B)}
HY64_ROW = sum(VEC_A_ROWS)
NA, NB = HY64_ROW + 3, sum(VEC_B_ROWS)


class Sems:

    def __init__(self, nc, ctx, phase):
        self.nc, self.ctx, self.phase, self.made = nc, ctx, phase, {}
        ctx.callback(self.clear)

    def clear(self):
        for sem in self.made.values():
            self.nc.gpsimd.sem_clear(sem)
            self.nc.release_semaphore(sem)

    def __getitem__(self, name):
        if name not in self.made:
            self.made[name] = self.nc.alloc_semaphore(f"{self.phase}_{name}")
        return self.made[name]


class Chain:

    def __init__(self, eng, sem):
        self.eng, self.sem, self.n = eng, sem, 0

    def __call__(self, ins):
        self.n += 1
        ins.then_inc(self.sem, 1)
        self.eng.wait_ge(self.sem, self.n)

    def add(self, ins):
        self.n += 1
        ins.then_inc(self.sem, 1)

    def sync(self):
        self.eng.wait_ge(self.sem, self.n)


class G:
    pass


def load_tiles(g, sp, upto):
    st = g.stream
    while g.issued < min(upto, len(st.src)):
        i = g.issued
        if i >= R:
            if st.kinds[i - R] == "raw":
                sp.wait_ge(g.raw_used, st.count(i - R, "raw"))
            else:
                sp.wait_ge(g.tiles_split, st.count(i - R, "split"))
        n, src = st.src[i]
        dst = g.ring[:, i % R, 0:n]
        if len(src.shape) == 3:
            dst = dst.rearrange("p (k n) -> p k n", k=src.shape[1])
        sp.dma_start(dst, src).then_inc(g.tile_loaded[i % R], 16)
        g.issued += 1


def wait_tile(g, eng, i):
    eng.wait_ge(g.tile_loaded[i % R], 16 * (i // R + 1))


def tile3(g, i, k):
    n = g.stream.src[i][0]
    return g.ring[:, i % R, 0:n].rearrange("p (k n) -> p k n", k=k)



def split_buffers(nc, ctx, g, name):
    g.whi = ctx.enter_context(nc.sbuf_tensor(f"{name}_whi", [P, H, WT], F32R))
    g.wlo = ctx.enter_context(nc.sbuf_tensor(f"{name}_wlo", [P, H, WT], F32R))


def split_hi(nc, g, act, i):
    s, n = g.stream.count(i, "split") - 1, g.stream.src[i][0]
    wait_tile(g, act, i)
    if s >= H:
        act.wait_ge(g.split_used, s - H + 1)
    nc.scalar.copy(g.whi[:, s % H, 0:n], g.ring[:, i % R, 0:n]).then_inc(g.hi_done, 1)


def split_lo(nc, g, dve, i):
    s, n = g.stream.count(i, "split") - 1, g.stream.src[i][0]
    dve.wait_ge(g.hi_done, s + 1)
    nc.vector.tensor_tensor(g.wlo[:, s % H, 0:n], g.ring[:, i % R, 0:n], g.whi[:, s % H, 0:n].bitcast(F32),
                            ALU.subtract).then_inc(g.tiles_split, 1)


def split_pair(g, pe, i, k):
    s, n = g.stream.count(i, "split") - 1, g.stream.src[i][0]
    pe.wait_ge(g.tiles_split, s + 1)
    return [w[:, s % H, 0:n].rearrange("p (k n) -> p k n", k=k) for w in (g.whi, g.wlo)]


def wait_used(g, eng, i):
    eng.wait_ge(g.split_used, g.stream.count(i, "split"))


def with_splits(split, tiles, after):
    for k, i in enumerate(tiles):
        split(i)
        if k >= 2:
            after(k - 2)
    for k in range(max(0, len(tiles) - 2), len(tiles)):
        after(k)


def product3(nc, out, lhs, rhs, start, stop):
    nc.tensor.matmul(out, lhs[0], rhs[0], start=start, stop=False)
    nc.tensor.matmul(out, lhs[0], rhs[1], start=False, stop=False)
    return nc.tensor.matmul(out, lhs[1], rhs[0], start=False, stop=stop)


def rms_transposed(g, nc, S, src, dst, gain, shift=None, pair=None):
    xn, ss, ps = g.xn, g.ss, g.ps

    def act(eng):
        for t in range(TT):
            nc.scalar.activation(xn[:, t], src[:, t], ACT.Square, accum_out=ss[:, t:t + 1]).then_inc(S["squares"], 1)
        eng.wait_ge(S["mean"], 1)
        nc.scalar.activation(ss[:, 4:6], ss[:, 2:4], ACT.Sqrt).then_inc(S["root"], 1)

    def dve(eng, ch):
        eng.wait_ge(S["squares"], TT)
        nc.vector.tensor_scalar(ss[:, 2:4], ss[:, 0:2], 1.0 / D, EPS, ALU.mult, ALU.add).then_inc(S["mean"], 1)
        eng.wait_ge(S["root"], 1)
        ch(nc.vector.reciprocal(ss[:, 4:6], ss[:, 4:6]))
        for t in range(TT):
            nc.vector.tensor_scalar(xn[:, t], src[:, t], ss[:, 4 + t:5 + t], None, ALU.mult).then_inc(S["normed"], 1)
        for q in range(4):
            t, half = q // 2, q % 2
            eng.wait_ge(S["turned"], q + 1)
            pq = ps[:, q % 2, :].rearrange("p (k n) -> p k n", k=4)
            where = (slice(None), slice(4 * half, 4 * half + 4), slice(P * t, P * t + P))
            out = dst[:] if pair else dst[where]
            gq = gain[:, 4 * half:4 * half + 4].unsqueeze(2).to_broadcast([P, 4, P])
            ins = nc.vector.tensor_tensor(out, pq, gq, ALU.mult)
            if shift is not None:
                ch(ins)
                sq = shift[:, 4 * half:4 * half + 4].unsqueeze(2).to_broadcast([P, 4, P])
                ins = nc.vector.tensor_tensor(out, out, sq, ALU.add)
            if pair:
                ch(ins)
                ch(nc.vector.tensor_copy(pair[0][where], out))
                ins = nc.vector.tensor_tensor(pair[1][where], out, pair[0][where].bitcast(F32), ALU.subtract)
            ins.then_inc(S["xt"], 1)
            eng.wait_ge(S["xt"], q + 1)

    def pe(eng):
        for q in range(4):
            t, half = q // 2, q % 2
            if half == 0:
                eng.wait_ge(S["normed"], t + 1)
            if q >= 2:
                eng.wait_ge(S["xt"], q - 1)
            for k in range(4):
                kk = 4 * half + k
                mm = nc.tensor.transpose(ps[:, q % 2, k * P:k * P + P], xn[:, t, kk * P:kk * P + P], g.ident[:])
            mm.then_inc(S["turned"], 1)
        eng.wait_ge(S["xt"], 4)

    return act, dve, pe


def setup_phase(nc, g, I):
    with ExitStack() as ctx:
        S = Sems(nc, ctx, "setup")
        rows = ctx.enter_context(nc.sbuf_tensor("vec_rows", [P, 2, P], F32))
        buckets = ctx.enter_context(nc.sbuf_tensor("buckets", [NUM_BUCKETS, BIAS_HEADS + DIST], F32))
        dmask = ctx.enter_context(nc.sbuf_tensor("dist_mask", [BIAS_HEADS, DIST], F32))
        dbias = ctx.enter_context(nc.sbuf_tensor("dist_bias", [BIAS_HEADS, DIST], F32))
        lamv = ctx.enter_context(nc.sbuf_tensor("lam_rows", [P, 4 * HD + 8], F32))
        n_rows = [0]
        block = ctx.enter_context(nc.Block(no_gpsimd_drain=True))

        @block.scalar
        def _(act):
            def put(dst, src):
                act.dma_start(dst, src).then_inc(S["rows"], 16)
                n_rows[0] += 16
            put(g.ident[:], I["k_ident"])
            put(g.causal[:], I["k_causal"])
            put(g.x[:], I["x"].rearrange("b (t p) d -> p (b t) d", p=P))
            for names, counts, start, half in ((VEC_A, VEC_A_ROWS, ROW_A, 0), (VEC_B, VEC_B_ROWS, ROW_B, 1)):
                for n, k in zip(names, counts):
                    r0 = start[n]
                    if n == "qk_gain":
                        flat = I[n].rearrange("l a b e -> (l a b) e")
                        put(rows[r0:r0 + k, half, 0:HD], flat)
                        put(rows[r0:r0 + k, half, HD:P], flat)
                        continue
                    shape = I[n].shape
                    letters = "abcd"[:len(shape)]
                    flat = I[n].rearrange(f"{' '.join(letters)} -> ({' '.join(letters)})")
                    put(rows[r0:r0 + k, half, :], flat.rearrange("(r n) -> r n", n=P))
            for j, n in enumerate(("hy_freq_2", "hy_ffn_b1_2", "hy_ffn_b2_2")):
                put(rows[HY64_ROW + j:HY64_ROW + j + 1, 0, 0:HD], I[n])
                put(rows[HY64_ROW + j:HY64_ROW + j + 1, 0, HD:P], I[n])
            act.wait_ge(S["lamsum"], 1)
            nc.scalar.activation(lamv[:, 258:260], lamv[:, 256:258], ACT.Exp).then_inc(S["lamexp"], 1)

        @block.sync
        def _(sp):
            load_tiles(g, sp, R)
            sp.dma_start(buckets[:, 0:BIAS_HEADS], I["rel_bias"]).then_inc(S["buckets"], 16)
            sp.dma_start(buckets[:, BIAS_HEADS:], I["k_onehot"]).then_inc(S["buckets"], 16)
            sp.dma_start(dmask[:], I["k_dmask"]).then_inc(S["buckets"], 16)
            sp.dma_start(lamv[:, 0:256], I["diff_lambda"].rearrange("l a b -> l (a b)").to_broadcast([P, 256])
                         ).then_inc(S["lam"], 16)
            sp.wait_ge(S["dbias"], 1)
            sp.dma_start(g.bias_dram, dbias[:]).then_inc(S["stored"], 16)
            sp.wait_ge(S["stored"], 16)

        @block.tensor
        def _(pe):
            pe.wait_ge(S["rows"], n_rows[0])
            nc.tensor.transpose(g.ps[:, 0, 0:NA], rows[0:NA, 0, :], g.ident[0:NA, 0:NA])
            nc.tensor.transpose(g.ps[:, 1, 0:NB], rows[0:NB, 1, :], g.ident[0:NB, 0:NB]).then_inc(S["cols"], 1)
            pe.wait_ge(S["buckets"], 48)
            nc.tensor.matmul(g.ps[0:BIAS_HEADS, 2, 0:DIST], buckets[:, 0:BIAS_HEADS], buckets[:, BIAS_HEADS:],
                             start=True, stop=True).then_inc(S["bias_ps"], 1)

        @block.vector
        def _(dve):
            ch = Chain(dve, S["dve"])
            nc.vector.memset(g.ones[:], 1.0)
            dve.wait_ge(S["cols"], 1)
            nc.vector.tensor_copy(g.va[:, 0:NA], g.ps[:, 0, 0:NA])
            nc.vector.tensor_copy(g.vb[:, 0:NB], g.ps[:, 1, 0:NB])
            dve.wait_ge(S["bias_ps"], 1)
            dve.wait_ge(S["buckets"], 48)
            nc.vector.tensor_tensor(dbias[:], g.ps[0:BIAS_HEADS, 2, 0:DIST], dmask[:], ALU.add).then_inc(S["dbias"], 1)
            dve.wait_ge(S["lam"], 16)
            pair = lamv[:, 0:256].rearrange("p (a b e) -> p a b e", a=2, b=2)
            ch(nc.vector.tensor_tensor(pair[:, :, 0, :], pair[:, :, 0, :], pair[:, :, 1, :], ALU.mult))
            nc.vector.tensor_reduce(lamv[:, 256:258], pair[:, :, 0, :], AX_X, ALU.add).then_inc(S["lamsum"], 1)
            dve.wait_ge(S["lamexp"], 1)
            ch(nc.vector.tensor_tensor(lamv[:, 260:261], lamv[:, 258:259], lamv[:, 259:260], ALU.subtract))
            ch(nc.vector.tensor_scalar(g.lam[:], lamv[:, 260:261], LAM_INIT, None, ALU.add))


def ffn_phase(nc, g, name, gain_row):
    with ExitStack() as ctx:
        S = Sems(nc, ctx, name)
        hid = [ctx.enter_context(nc.sbuf_tensor(f"{name}_hid_{part}", [P, FC, T], F32R)) for part in ("hi", "lo")]
        silu = ctx.enter_context(nc.sbuf_tensor(f"{name}_silu", [P, 2, 2 * T], F32))
        tmp = ctx.enter_context(nc.sbuf_tensor(f"{name}_tmp", [P, 2 * T], F32))
        split_buffers(nc, ctx, g, name)
        xt, ps = g.xt2, g.ps
        act_n, dve_n, pe_n = rms_transposed(g, nc, S, g.x, g.xquarter, g.va[:, gain_row:gain_row + KC], pair=xt)
        first = g.stream.first[name]
        down0 = g.stream.first[name + "_down"]
        pairs = FC // 2
        tiles = list(range(first, down0 + pairs))
        block = ctx.enter_context(nc.Block(no_gpsimd_drain=True))

        @block.sync
        def _(sp):
            load_tiles(g, sp, down0 + pairs + R)

        @block.tensor
        def _(pe):
            pe_n(pe)
            for k in range(2 * pairs):
                m, u = k // 2, k % 2
                w = split_pair(g, pe, first + k, KC)
                if m >= 2 and u == 0:
                    pe.wait_ge(S["hid"], m - 1)
                for f in range(2):
                    for c in range(KC):
                        mm = product3(nc, ps[:, 2 * (m % 2) + u, T * f:T * f + T], [x[:, c, P * f:P * f + P] for x in w],
                                      [x[:, c, :] for x in xt], c == 0, c == KC - 1)
                mm.then_inc(g.split_used, 1)
            for m in range(pairs):
                w = split_pair(g, pe, down0 + m, 2)
                pe.wait_ge(S["hid"], m + 1)
                for c in range(2):
                    f = 2 * m + c
                    for t in range(TT):
                        for n in range(2):
                            mm = product3(nc, ps[:, 4 + 2 * t + n, :], [x[:, f, P * t:P * t + P] for x in hid],
                                          [x[:, c, 512 * n:512 * n + 512] for x in w], f == 0, f == FC - 1)
                mm.then_inc(g.split_used, 1)

        @block.scalar
        def _(act):
            act_n(act)

            def gate(k):
                if k >= 2 * pairs or k % 2:
                    return
                m = k // 2
                wait_used(g, act, first + k)
                if m >= 2:
                    act.wait_ge(S["hid"], m - 1)
                nc.scalar.activation(silu[:, m % 2], ps[:, 2 * (m % 2), :], ACT.Silu).then_inc(S["silu"], 1)

            with_splits(lambda i: split_hi(nc, g, act, i), tiles, gate)

        @block.vector
        def _(dve):
            ch = Chain(dve, S["dve"])
            dve_n(dve, ch)

            def up(k):
                if k >= 2 * pairs or k % 2 == 0:
                    return
                m = k // 2
                wait_used(g, dve, first + k)
                dve.wait_ge(S["silu"], m + 1)
                ch(nc.vector.tensor_tensor(tmp[:], ps[:, 2 * (m % 2) + 1, :], silu[:, m % 2], ALU.mult))
                hi, lo = (x[:, 2 * m:2 * m + 2].rearrange("p f t -> p (f t)") for x in hid)
                ch(nc.vector.tensor_copy(hi, tmp[:]))
                nc.vector.tensor_tensor(lo, tmp[:], hi.bitcast(F32), ALU.subtract).then_inc(S["hid"], 1)
                dve.wait_ge(S["hid"], m + 1)

            with_splits(lambda i: split_lo(nc, g, dve, i), tiles, up)
            wait_used(g, dve, down0 + pairs - 1)
            for t in range(TT):
                for n in range(2):
                    xs = g.x[:, t, 512 * n:512 * n + 512]
                    nc.vector.scalar_tensor_tensor(xs, ps[:, 4 + 2 * t + n, :], 0.5, xs, ALU.mult, ALU.add)


QK_HEADS_A, QK_HEADS_B, QK_HEADS_C = 24, 16, 5
QT_CHUNKS = ([(A_COL + P * i, "qk_gain", 0 if i < 6 else 1) for i in range(12)]
             + [(BQK_COL + P * i, "qk_gain", 2 if i < 4 else 3) for i in range(8)]
             + [(C_COL + P * i, "qk_gain", 4) for i in range(2)] + [(C_COL + 256, "qk_gain", 5)]
             + [(IX_COL + P * i, None, 0) for i in range(4)] + [(IX_COL + 512, None, 0)])
QC, QI = 20, 23
UNITS = [("a", i) for i in range(4)] + [("b", i) for i in range(4)] + [("c", 0)]


def mixer_phase(nc, g):
    with ExitStack() as ctx:
        S = Sems(nc, ctx, "mix")

        def sb(name, shape):
            return ctx.enter_context(nc.sbuf_tensor(name, shape, F32))
        pr = sb("proj", [P, TT, N_IN])
        ps = g.ps
        in0 = g.stream.first["w_in"]
        n_in = g.stream.first["w_branch_a"] - in0
        with ExitStack() as inner:
            S1 = Sems(nc, inner, "mixin")
            split_buffers(nc, inner, g, "mixin")
            act_n, dve_n, pe_n = rms_transposed(g, nc, S1, g.x, g.xquarter, g.va[:, ROW_A["mix_norm"]:ROW_A["mix_norm"] + KC],
                                                pair=g.xt2)
            tiles = list(range(in0, in0 + n_in))
            block = inner.enter_context(nc.Block(no_gpsimd_drain=True))

            @block.sync
            def _(sp):
                load_tiles(g, sp, in0 + n_in + R)

            @block.tensor
            def _(pe):
                pe_n(pe)
                for k in range(n_in):
                    if k >= 4:
                        pe.wait_ge(S1["copied"], k - 3)
                    column_product(nc, g, pe, in0 + k, ps[:, k % 4, :])

            def copy_out(k):
                c0 = 256 * k
                n = min(256, N_IN - c0)
                return pr[:, :, c0:c0 + n], ps[:, k % 4, :].rearrange("p (t n) -> p t n", t=TT)[:, :, 0:n]

            @block.scalar
            def _(act):
                act_n(act)

                def copy(k):
                    wait_used(g, act, in0 + k)
                    nc.scalar.copy(*copy_out(k)).then_inc(S1["copied"], 1)

                with_splits(lambda i: split_hi(nc, g, act, i), tiles, copy)

            @block.vector
            def _(dve):
                ch = Chain(dve, S1["dve"])
                dve_n(dve, ch)
                for i in tiles:
                    split_lo(nc, g, dve, i)

        mixer_attention(nc, g, pr)
        mixer_out(nc, g, pr)


def mixer_attention(nc, g, pr):
    with ExitStack() as ctx:
        S = Sems(nc, ctx, "att")

        def sb(name, shape):
            return ctx.enter_context(nc.sbuf_tensor(name, shape, F32))
        ps = g.ps
        qt = sb("qt", [P, len(QT_CHUNKS), T])
        hs = sb("head_sums", [P, TT, 48])
        with ExitStack() as inner:
            sq = inner.enter_context(nc.sbuf_tensor("head_squares", [P, QK_HEADS_A * HD], F32))
            twice = inner.enter_context(nc.sbuf_tensor("keys_twice", [P, TT, 2, P], F32))
            S1 = Sems(nc, inner, "qk")
            block = inner.enter_context(nc.Block(no_gpsimd_drain=True))
            groups = [(A_COL, QK_HEADS_A, 0), (BQK_COL, QK_HEADS_B, 24), (C_COL, QK_HEADS_C, 40)]
            flip = inner.enter_context(nc.sbuf_tensor("flip", [P, P], F32))
            bias_pairs = g.bias[:].rearrange("p (m two) n -> p m (two n)", two=2)

            @block.sync
            def _(sp):
                skew = bass.AP(tensor=g.bias_dram.tensor, offset=0, ap=[[1, P], [DIST, BIAS_HEADS], [1, T]])
                sp.dma_start(g.bias[:], skew).then_inc(S1["skewed"], 16)
                sp.dma_start(flip[:], g.I["k_flip"]).then_inc(S1["skewed"], 16)

            @block.scalar
            def _(act):
                n = 0
                for t in range(TT):
                    for c0, heads, h0 in groups:
                        if n:
                            act.wait_ge(S1["summed"], n)
                        nc.scalar.activation(sq[:, 0:heads * HD], pr[:, t, c0:c0 + heads * HD], ACT.Square).then_inc(S1["squared"], 1)
                        n += 1
                act.wait_ge(S1["mean"], 1)
                nc.scalar.activation(hs[:, :, 0:45], hs[:, :, 0:45], ACT.Sqrt).then_inc(S1["root"], 1)
                for i, (c0, gname, gr) in enumerate(QT_CHUNKS):
                    act.wait_ge(S1["turned"], i + 1)
                    src = ps[:, i % 4, 0:T]
                    if gname:
                        r = ROW_A[gname] + gr
                        nc.scalar.activation(qt[:, i, :], src, ACT.Copy, scale=g.va[:, r:r + 1]).then_inc(S1["evac"], 1)
                    else:
                        nc.scalar.copy(qt[:, i, :], src).then_inc(S1["evac"], 1)
                act.wait_ge(S1["evac"], len(QT_CHUNKS))

            @block.vector
            def _(dve):
                ch = Chain(dve, S1["dve"])
                n = 0
                for t in range(TT):
                    for c0, heads, h0 in groups:
                        dve.wait_ge(S1["squared"], n + 1)
                        s3 = sq[:, 0:heads * HD].rearrange("p (h e) -> p h e", e=HD)
                        nc.vector.tensor_reduce(hs[:, t, h0:h0 + heads], s3, AX_X, ALU.add).then_inc(S1["summed"], 1)
                        n += 1
                dve.wait_ge(S1["summed"], n)
                nc.vector.tensor_scalar(hs[:, :, 0:45], hs[:, :, 0:45], 1.0 / HD, EPS, ALU.mult, ALU.add).then_inc(S1["mean"], 1)
                for n in range(BIAS_HEADS // 2):
                    dve.wait_ge(S1["flip_ps"], n + 1)
                    nc.vector.tensor_copy(bias_pairs[:, n], ps[:, 4 + n % 4, :]).then_inc(S1["flipped"], 1)
                dve.wait_ge(S1["root"], 1)
                ch(nc.vector.reciprocal(hs[:, :, 0:45], hs[:, :, 0:45]))
                for c0, heads, h0 in groups:
                    for t in range(TT):
                        p3 = pr[:, t, c0:c0 + heads * HD].rearrange("p (h e) -> p h e", e=HD)
                        r3 = hs[:, t, h0:h0 + heads].unsqueeze(2).to_broadcast([P, heads, HD])
                        nc.vector.tensor_tensor(p3, p3, r3, ALU.mult).then_inc(S1["unit"], 1)
                dve.wait_ge(S1["unit"], 6)
                for t in range(TT):
                    for j, c0 in enumerate((C_COL + 256, IX_COL + 512)):
                        nc.vector.tensor_copy(twice[:, t, j, :].rearrange("p (a e) -> p a e", a=2),
                                              pr[:, t, c0:c0 + HD].unsqueeze(1).to_broadcast([P, 2, HD])).then_inc(S1["twice"], 1)

            @block.tensor
            def _(pe):
                pe.wait_ge(S1["skewed"], 32)
                for n in range(BIAS_HEADS // 2):
                    if n >= 4:
                        pe.wait_ge(S1["flipped"], n - 3)
                    nc.tensor.matmul(ps[:, 4 + n % 4, :], flip[:], bias_pairs[:, n], start=True, stop=True).then_inc(S1["flip_ps"], 1)
                for i, (c0, gname, gr) in enumerate(QT_CHUNKS):
                    pe.wait_ge(S1["unit"], 2 if i < 12 else 4 if i < 20 else 6)
                    if i >= 4:
                        pe.wait_ge(S1["evac"], i - 3)
                    single = c0 in (C_COL + 256, IX_COL + 512)
                    if single:
                        pe.wait_ge(S1["twice"], 4)
                    for t in range(TT):
                        if single:
                            src = twice[:, t, int(c0 > C_COL + 256), :]
                        else:
                            src = pr[:, t, c0:c0 + P]
                        mm = nc.tensor.transpose(ps[:, i % 4, P * t:P * t + P], src, g.ident[:])
                    mm.then_inc(S1["turned"], 1)

        keep = sb("keep", [P, TT, T])
        score = pr[:, :, 0:T]
        index_scores(nc, g, pr, qt, score)
        softmax_units(nc, g, pr, qt, score, keep)


def causal_keys(t):
    return P * (t + 1), P * (1 - t)


def index_scores(nc, g, pr, qt, score):
    with ExitStack() as ctx:
        S = Sems(nc, ctx, "idx")

        def sb(name, shape):
            return ctx.enter_context(nc.sbuf_tensor(name, shape, F32))
        relu = sb("relu", [P, 2, T])
        wix = sb("wix", [P, TT, IDX_HEADS])
        ps = g.ps
        block = ctx.enter_context(nc.Block(no_gpsimd_drain=True))
        steps = [(t, h) for t in range(TT) for h in range(IDX_HEADS)]

        @block.tensor
        def _(pe):
            for i, (t, h) in enumerate(steps):
                nk = causal_keys(t)[0]
                lo = HD * (h % 2)
                if i >= 4:
                    pe.wait_ge(S["relu"], i - 3)
                nc.tensor.matmul(ps[:, i % 4, 0:nk], qt[lo:lo + HD, QI + h // 2, P * t:P * t + P],
                                 qt[lo:lo + HD, QI + 4, 0:nk], start=True, stop=True).then_inc(S["raw"], 1)

        @block.scalar
        def _(act):
            for i, (t, h) in enumerate(steps):
                nk = causal_keys(t)[0]
                act.wait_ge(S["raw"], i + 1)
                if i >= 2:
                    act.wait_ge(S["added"], i - 1)
                nc.scalar.activation(relu[:, i % 2, 0:nk], ps[:, i % 4, 0:nk], ACT.Relu, scale=HD ** -0.5).then_inc(S["relu"], 1)

        @block.vector
        def _(dve):
            ch = Chain(dve, S["dve"])
            c0 = IX_COL + IDX_HEADS * HD + HD
            ch(nc.vector.tensor_scalar(wix[:], pr[:, :, c0:c0 + IDX_HEADS], IDX_HEADS ** -0.5, None, ALU.mult))
            for i, (t, h) in enumerate(steps):
                nk, b0 = causal_keys(t)
                dve.wait_ge(S["relu"], i + 1)
                if i:
                    dve.wait_ge(S["added"], i)
                sc = score[:, t, 0:nk]
                w = wix[:, t, h:h + 1]
                if h == 0:
                    ins = nc.vector.tensor_scalar(sc, relu[:, i % 2, 0:nk], w, None, ALU.mult)
                else:
                    ins = nc.vector.scalar_tensor_tensor(sc, relu[:, i % 2, 0:nk], w, sc, ALU.mult, ALU.add)
                ins.then_inc(S["added"], 1)


def rank_round(nc, ch, sc, wk, top, r, count):
    src = sc if r == 0 else wk
    ch(nc.vector.max(top[:], src))
    if r < count // 8 - 1:
        ch(nc.vector.match_replace(out=wk, in_to_replace=top[:], in_values=src, imm_value=-3e38))


def mark_ranked(nc, ch, sc, top, sel, cnt, count, ones):
    v = nc.vector
    thr = top[:, 7:8]
    gt, eq, run = sel[:, 0], sel[:, 1], sel[:, 2]
    ch(v.tensor_scalar(gt, sc, thr, None, ALU.is_gt))
    ch(v.tensor_reduce(cnt[:, 0:1], gt, AX_X, ALU.add))
    ch(v.tensor_scalar(cnt[:, 1:2], cnt[:, 0:1], -1.0, float(count), ALU.mult, ALU.add))
    ch(v.tensor_scalar(eq, sc, thr, None, ALU.is_equal))
    ch(v.tensor_tensor_scan(run, ones, eq, 0.0, ALU.mult, ALU.add))
    ch(v.scalar_tensor_tensor(eq, run, cnt[:, 1:2], eq, ALU.is_le, ALU.mult))
    ch(v.tensor_tensor(gt, gt, eq, ALU.add))


def first_by_rank(nc, ch, sc, wk, top, sel, cnt, count, ones):
    for r in range(count // 8):
        rank_round(nc, ch, sc, wk, top, r, count)
    mark_ranked(nc, ch, sc, top, sel, cnt, count, ones)


def softmax_units(nc, g, pr, qt, score, keep):
    with ExitStack() as ctx:
        S = Sems(nc, ctx, "sm")

        def sb(name, shape):
            return ctx.enter_context(nc.sbuf_tensor(name, shape, F32))
        lg = sb("logits", [P, 2, 4, T])
        pt = sb("probs_t", [P, 2, 8, P])
        st = sb("stats", [P, 2, 16])
        rden = sb("rden", [P, 2, 4])
        ps, o = g.ps, g.o
        top, cnt = sb("top", [P, 8]), sb("cnt", [P, 4])
        work, sel = pr[:, 0, T:2 * T], pr[:, 0, 2 * T:5 * T].rearrange("p (k n) -> p k n", k=3)
        steps = [(u, h, t) for u, h in UNITS for t in range(TT)]
        block = ctx.enter_context(nc.Block(no_gpsimd_drain=True))
        n_group = {"a": 3, "b": 2, "c": 4}
        n_turn = {"a": 3, "b": 1, "c": 4}
        bias_head = {"a": lambda h, j: 4 * j + h, "b": lambda h, j: A_HEADS + h, "c": lambda h, j: A_HEADS + B_HEADS + j}

        def heads_of(u, h, j):
            if u == "a":
                n = 4 * j + h
                return (n // 2, 6 + n // 2, HD * (n % 2))
            if u == "b":
                return (12 + 2 * j + h // 2, 16 + 2 * j + h // 2, HD * (h % 2))
            return (QC + j // 2, QC + 2, HD * (j % 2))

        def score_place(i, u, j, nk):
            b, c = (j % 2, j // 2) if u == "c" else (j // 2, j % 2)
            return ps[:, 2 * (i % 2) + b, T * c:T * c + nk]

        def values_of(u, h, j, kt):
            if u == "a":
                c = A_COL + 2 * A_HEADS * HD + HD * (4 * j + h)
                return pr[:, kt, c:c + HD]
            if u == "b":
                return pr[:, kt, BV_COL + P * h:BV_COL + P * h + P]
            return pr[:, kt, C_COL + 320:C_COL + 320 + HD]

        @block.tensor
        def _(pe):
            def scores(i):
                u, h, t = steps[i]
                nk = causal_keys(t)[0]
                if i >= 2:
                    pe.wait_ge(S["logits"], i - 1)
                for j in range(n_group[u]):
                    cq, ck, lo = heads_of(u, h, j)
                    mm = nc.tensor.matmul(score_place(i, u, j, nk),
                                          qt[lo:lo + HD, cq, P * t:P * t + P], qt[lo:lo + HD, ck, 0:nk],
                                          start=True, stop=True)
                mm.then_inc(S["scores"], 1)

            def outputs(i):
                u, h, t = steps[i]
                pe.wait_ge(S["probs"], i + 1)
                if i:
                    pe.wait_ge(S["pt"], i)
                for j in range(n_turn[u]):
                    for kt in range(t + 1):
                        n = (t + 1) * j + kt
                        mm = nc.tensor.transpose(ps[:, 4 + n // 4, P * (n % 4):P * (n % 4) + P],
                                                 lg[:, i % 2, j, P * kt:P * kt + P], g.ident[:])
                mm.then_inc(S["turned"], 1)
                pe.wait_ge(S["pt"], i + 1)
                if i >= 2:
                    pe.wait_ge(S["out"], i - 1)
                for j in range(n_turn[u]):
                    for kt in range(t + 1):
                        n = (t + 1) * j + kt
                        joint = u == "a"
                        v = values_of(u, h, j, kt)
                        w = v.shape[1]
                        c = 0 if joint else w * j
                        first = n == 0 if joint else kt == 0
                        last = n == 3 * (t + 1) - 1 if joint else kt == t
                        mm = nc.tensor.matmul(ps[:, 6 + i % 2, c:c + w], pt[:, i % 2, n, :], v, start=first, stop=last)
                mm.then_inc(S["o_ps"], 1)

            scores(0)
            for i in range(1, len(steps) + 2):
                if i < len(steps):
                    scores(i)
                if i >= 2:
                    outputs(i - 2)

        @block.scalar
        def _(act):
            def copy_turned(i):
                u, h, t = steps[i]
                n = n_turn[u] * (t + 1)
                act.wait_ge(S["turned"], i + 1)
                if i >= 2:
                    act.wait_ge(S["o_ps"], i - 1)
                src = ps[:, 4:6, :].rearrange("p b (n q) -> p (b n) q", n=4)[:, 0:n, :]
                nc.scalar.copy(pt[:, i % 2, 0:n, :], src).then_inc(S["pt"], 1)

            for i, (u, h, t) in enumerate(steps):
                nk = causal_keys(t)[0]
                n = n_group[u]
                act.wait_ge(S["max"], i + 1)
                if u == "a":
                    nc.scalar.activation(lg[:, i % 2, 0:n, 0:nk], lg[:, i % 2, 0:n, 0:nk], ACT.Exp, bias=st[:, i % 2, 0:1],
                                         accum_out=st[:, i % 2, 8:9]).then_inc(S["exp"], 1)
                else:
                    for j in range(n):
                        ins = nc.scalar.activation(lg[:, i % 2, j, 0:nk], lg[:, i % 2, j, 0:nk], ACT.Exp,
                                                   bias=st[:, i % 2, j:j + 1], accum_out=st[:, i % 2, 8 + j:9 + j])
                    ins.then_inc(S["exp"], 1)
                if i:
                    copy_turned(i - 1)
            copy_turned(len(steps) - 1)

        @block.vector
        def _(dve):
            ch = Chain(dve, S["dve"])
            v = nc.vector

            def logits(i):
                u, h, t = steps[i]
                nk, b0 = causal_keys(t)
                n = n_group[u]
                dve.wait_ge(S["scores"], i + 1)
                if i >= 2:
                    dve.wait_ge(S["turned"], i - 1)
                for j in range(n):
                    src = score_place(i, u, j, nk)
                    b = bias_head[u](h, j)
                    ins = v.scalar_tensor_tensor(lg[:, i % 2, j, 0:nk], src, HD ** -0.5, g.bias[:, b, b0:b0 + nk],
                                                 ALU.mult, ALU.add)
                    if j < n - 1:
                        ch.add(ins)
                ins.then_inc(S["logits"], 1)
                dve.wait_ge(S["logits"], i + 1)
                ch.sync()
                l3 = lg[:, i % 2, 0:n, 0:nk]
                if u == "c":
                    k3 = keep[:, t, 0:nk].unsqueeze(1).to_broadcast([P, n, nk])
                    ch(v.tensor_tensor(l3, l3, k3, ALU.add))
                if u == "a":
                    ch(v.tensor_reduce(st[:, i % 2, 4:5], l3, AX_XY, ALU.max))
                    m = 1
                else:
                    ch(v.tensor_reduce(st[:, i % 2, 4:4 + n], l3, AX_X, ALU.max))
                    m = n
                v.tensor_scalar(st[:, i % 2, 0:m], st[:, i % 2, 4:4 + m], -1.0, None, ALU.mult).then_inc(S["max"], 1)

            def weights(i):
                u, h, t = steps[i]
                nk = causal_keys(t)[0]
                m = 1 if u == "a" else n_group[u]
                dve.wait_ge(S["exp"], i + 1)
                if i >= 2:
                    dve.wait_ge(S["out"], i - 1)
                ins = v.reciprocal(rden[:, i % 2, 0:m], st[:, i % 2, 8:8 + m])
                if u != "b":
                    ins.then_inc(S["probs"], 1)
                    return
                ch(ins)
                ch(v.tensor_tensor(rden[:, i % 2, 2:3], rden[:, i % 2, 1:2], g.lam[:], ALU.mult))
                l0, l1 = lg[:, i % 2, 0, 0:nk], lg[:, i % 2, 1, 0:nk]
                ch(v.tensor_scalar(l1, l1, rden[:, i % 2, 2:3], None, ALU.mult))
                v.scalar_tensor_tensor(l0, l0, rden[:, i % 2, 0:1], l1, ALU.mult, ALU.subtract).then_inc(S["probs"], 1)

            def scale_out(i):
                u, h, t = steps[i]
                dve.wait_ge(S["o_ps"], i + 1)
                dve.wait_ge(S["probs"], i + 1)
                src = ps[:, 6 + i % 2, :]
                if u == "a":
                    v.tensor_scalar(o[:, t, HD * h:HD * h + HD], src[:, 0:HD], rden[:, i % 2, 0:1], None,
                                    ALU.mult).then_inc(S["out"], 1)
                elif u == "b":
                    v.tensor_copy(o[:, t, 256 + P * h:256 + P * h + P], src[:, 0:P]).then_inc(S["out"], 1)
                else:
                    dst = o[:, t, 768:1024].rearrange("p (h e) -> p h e", e=HD)
                    r3 = rden[:, i % 2, 0:4].unsqueeze(2).to_broadcast([P, 4, HD])
                    v.tensor_tensor(dst, src[:, 0:256].rearrange("p (h e) -> p h e", e=HD), r3, ALU.mult).then_inc(S["out"], 1)

            rounds = TOP_KEYS // 8

            def rank_keys(i):
                t, r = i // rounds, i % rounds
                if t >= TT:
                    return
                nk, b0 = causal_keys(t)
                sc = score[:, t, 0:nk]
                if r == 0:
                    ch(v.tensor_tensor(sc, sc, g.causal[:, b0:b0 + nk], ALU.add))
                rank_round(nc, ch, sc, work[:, 0:nk], top, r, TOP_KEYS)
                if r == rounds - 1:
                    mark_ranked(nc, ch, sc, top, sel[:, :, 0:nk], cnt, TOP_KEYS, g.ones[:, 0:nk])
                    ch(v.tensor_scalar(keep[:, t, 0:nk], sel[:, 0, 0:nk], -1.0, -MASKED, ALU.add, ALU.mult))

            assert TT * rounds <= steps.index(("c", 0, 0))
            for i in range(len(steps)):
                logits(i)
                if i:
                    weights(i - 1)
                if i >= 2:
                    scale_out(i - 2)
                rank_keys(i)
            weights(len(steps) - 1)
            scale_out(len(steps) - 2)
            scale_out(len(steps) - 1)


def column_product(nc, g, pe, i, bank):
    w = split_pair(g, pe, i, KC)
    n = w[0].shape[2]
    for t in range(TT):
        for c in range(KC):
            mm = product3(nc, bank[:, 256 * t:256 * t + n], [x[:, c, P * t:P * t + P] for x in g.xt2],
                          [x[:, c, :] for x in w], c == 0, c == KC - 1)
    mm.then_inc(g.split_used, 1)


def turn_rows(nc, g, pe, S, src, dst_name, n, bank0=0):
    q = 0
    for t in range(TT):
        for half in range(n // 4):
            if q >= 2:
                pe.wait_ge(S[dst_name], q - 1)
            for k in range(4):
                kk = 4 * half + k
                mm = nc.tensor.transpose(g.ps[:, bank0 + q % 2, P * k:P * k + P], src[:, t, P * kk:P * kk + P], g.ident[:])
            mm.then_inc(S[dst_name + "_turned"], 1)
            q += 1


def turned_place(g, dst, q, n, bank0=0):
    t, half = q // (n // 4), q % (n // 4)
    return (dst[:, 4 * half:4 * half + 4, P * t:P * t + P],
            g.ps[:, bank0 + q % 2, :].rearrange("p (k n) -> p k n", k=4))


def turned_hi(nc, g, act, S, pair, dst_name, n, bank0=0):
    for q in range(TT * n // 4):
        act.wait_ge(S[dst_name + "_turned"], q + 1)
        nc.scalar.copy(*turned_place(g, pair[0], q, n, bank0)).then_inc(S[dst_name + "_hi"], 1)


def turned_lo(nc, g, dve, S, pair, dst_name, n, bank0=0):
    for q in range(TT * n // 4):
        dve.wait_ge(S[dst_name + "_hi"], q + 1)
        lo, src = turned_place(g, pair[1], q, n, bank0)
        hi = turned_place(g, pair[0], q, n, bank0)[0]
        nc.vector.tensor_tensor(lo, src, hi.bitcast(F32), ALU.subtract).then_inc(S[dst_name], 1)


def mixer_out(nc, g, pr):
    with ExitStack() as ctx:
        S = Sems(nc, ctx, "mo")

        def sb(name, shape):
            return ctx.enter_context(nc.sbuf_tensor(name, shape, F32))
        ps, o = g.ps, g.o
        split_buffers(nc, ctx, g, "mixout")
        y, tmp, sq = pr[:, :, 0:D], pr[:, :, D:2 * D], pr[:, :, 2 * D:2 * D + 512]
        st = sb("st", [P, TT, 8])
        dnorm = sb("dnorm", [P, P])
        br0 = g.stream.first["w_branch_a"]
        out0 = g.stream.first["w_out"]
        branch_tiles = [[0], [1, 2], [3]]
        tiles = list(range(br0, out0 + 4))
        block = ctx.enter_context(nc.Block(no_gpsimd_drain=True))

        @block.sync
        def _(sp):
            sp.dma_start(dnorm[:], g.I["diff_out_norm"].to_broadcast([P, P])).then_inc(S["dnorm"], 16)
            load_tiles(g, sp, out0 + 4 + R)

        @block.scalar
        def _(act):
            for t in range(TT):
                nc.scalar.activation(sq[:, t], o[:, t, 256:768], ACT.Square).then_inc(S["sq"], 1)
            act.wait_ge(S["mean"], 1)
            nc.scalar.activation(st[:, :, 4:8], st[:, :, 0:4], ACT.Sqrt).then_inc(S["root"], 1)
            for i in tiles[0:2]:
                split_hi(nc, g, act, i)
            turned_hi(nc, g, act, S, g.xt2, "ot", KC)
            for t in range(TT):
                gt = pr[:, t, GATE_COL:GATE_COL + 3 * D]
                nc.scalar.activation(gt, gt, ACT.Sigmoid).then_inc(S["gates"], 1)
            for i in tiles[2:7]:
                split_hi(nc, g, act, i)
            turned_hi(nc, g, act, S, g.xt2, "yt", KC)
            split_hi(nc, g, act, tiles[7])

        @block.vector
        def _(dve):
            ch = Chain(dve, S["dve"])
            v = nc.vector
            dve.wait_ge(S["sq"], TT)
            ch(v.tensor_reduce(st[:, :, 0:4], sq[:].rearrange("p t (h e) -> p t h e", e=P), AX_X, ALU.add))
            v.tensor_scalar(st[:, :, 0:4], st[:, :, 0:4], 1.0 / P, EPS, ALU.mult, ALU.add).then_inc(S["mean"], 1)
            dve.wait_ge(S["root"], 1)
            ch(v.reciprocal(st[:, :, 4:8], st[:, :, 4:8]))
            ch(v.tensor_scalar(st[:, :, 0:4], st[:, :, 4:8], 1.0 - LAM_INIT, None, ALU.mult))
            dve.wait_ge(S["dnorm"], 16)
            for t in range(TT):
                o3 = o[:, t, 256:768].rearrange("p (h e) -> p h e", e=P)
                ch(v.tensor_tensor(o3, o3, dnorm[:].unsqueeze(1).to_broadcast([P, 4, P]), ALU.mult))
                v.tensor_tensor(o3, o3, st[:, t, 0:4].unsqueeze(2).to_broadcast([P, 4, P]), ALU.mult).then_inc(S["b_normed"], 1)
            for i in tiles[0:2]:
                split_lo(nc, g, dve, i)
            turned_lo(nc, g, dve, S, g.xt2, "ot", KC)
            for i in tiles[2:4]:
                split_lo(nc, g, dve, i)
            dve.wait_ge(S["gates"], TT)
            for b in range(3):
                wait_used(g, dve, br0 + branch_tiles[b][-1])
                for t in range(TT):
                    gt = pr[:, t, GATE_COL + D * b:GATE_COL + D * b + D]
                    src = ps[:, 4 + 2 * t:6 + 2 * t, :].rearrange("p b n -> p (b n)")
                    if b == 0:
                        ins = v.tensor_tensor(y[:, t], src, gt, ALU.mult)
                        ch(ins) if t == 0 else ins.then_inc(S["gated"], 1)
                    else:
                        ins = v.tensor_tensor(tmp[:, t], src, gt, ALU.mult)
                        ch(ins) if t == 0 else ins.then_inc(S["gated"], 1)
                if b:
                    dve.wait_ge(S["gated"], b + 1)
                    for t in range(TT):
                        ins = v.tensor_tensor(y[:, t], y[:, t], tmp[:, t], ALU.add)
                        if b == 2:
                            ins.then_inc(S["y"], 1)
                        else:
                            ch(ins)
            for i in tiles[4:7]:
                split_lo(nc, g, dve, i)
            turned_lo(nc, g, dve, S, g.xt2, "yt", KC)
            split_lo(nc, g, dve, tiles[7])
            wait_used(g, dve, out0 + 3)
            for t in range(TT):
                xs = g.x[:, t]
                v.tensor_tensor(xs, ps[:, 4 + 2 * t:6 + 2 * t, :].rearrange("p b n -> p (b n)"), xs, ALU.add)

        @block.tensor
        def _(pe):
            pe.wait_ge(S["b_normed"], TT)
            turn_rows(nc, g, pe, S, o, "ot", KC)
            pe.wait_ge(S["ot"], 4)
            n_chunk = 0
            for b, own in enumerate(branch_tiles):
                if b:
                    pe.wait_ge(S["gated"], b)
                for i in own:
                    w = split_pair(g, pe, br0 + i, 2)
                    for c in range(2):
                        first, last = i == own[0] and c == 0, i == own[-1] and c == 1
                        for t in range(TT):
                            for n in range(2):
                                mm = product3(nc, ps[:, 4 + 2 * t + n, :], [x[:, n_chunk, P * t:P * t + P] for x in g.xt2],
                                              [x[:, c, 512 * n:512 * n + 512] for x in w], first, last)
                        n_chunk += 1
                    mm.then_inc(g.split_used, 1)
            pe.wait_ge(S["y"], TT)
            turn_rows(nc, g, pe, S, y, "yt", KC)
            pe.wait_ge(S["yt"], 4)
            token_product(nc, g, pe, g.xt2, out0, 4)


def token_product(nc, g, pe, lhs, i0, n_tiles, k0=0):
    for m in range(n_tiles):
        w = split_pair(g, pe, i0 + m, 2)
        for c in range(2):
            k = 2 * m + c
            for t in range(TT):
                for n in range(2):
                    mm = product3(nc, g.ps[:, 4 + 2 * t + n, :], [x[:, k0 + k, P * t:P * t + P] for x in lhs],
                                  [x[:, c, 512 * n:512 * n + 512] for x in w], k == 0, k == 2 * n_tiles - 1)
        mm.then_inc(g.split_used, 1)


def allocate(nc, ctx, g):
    def sb(name, shape):
        return ctx.enter_context(nc.sbuf_tensor(name, shape, F32))
    g.ps = ctx.enter_context(nc.psum_tensor("ps", [P, 8, 512], F32))
    g.ring = sb("ring", [P, R, WT])
    g.ident, g.va, g.vb = sb("ident", [P, P]), sb("va", [P, NA]), sb("vb", [P, NB])
    g.ones = sb("ones", [P, T])
    g.lam, g.ss = sb("lam", [P, 1]), sb("ss", [P, 8])
    g.x, g.xquarter = sb("x", [P, TT, D]), sb("xquarter", [P, 4, P])
    g.xt2 = [ctx.enter_context(nc.sbuf_tensor(f"xt_{part}", [P, KC, T], F32R)) for part in ("hi", "lo")]
    g.tile_loaded = [ctx.enter_context(nc.semaphore(f"tile_loaded_{i}")) for i in range(R)]
    g.raw_used, g.hi_done, g.tiles_split, g.split_used = (
        ctx.enter_context(nc.semaphore(n)) for n in ("raw_used", "hi_done", "tiles_split", "split_used"))
    g.issued = 0


def first_stream(st, I):
    def ffn(name):
        gate, up = I[f"{name}_w_gate"][0], I[f"{name}_w_up"][0]
        st.mark(name)
        for c in range(0, D_FF, 256):
            for w in (gate, up):
                st.add(WT, w[:, c:c + 256].rearrange("(k p) n -> p k n", p=P))
        st.rows(f"{name}_down", I[f"{name}_w_down"][0])
    ffn("ffn1")
    st.columns("w_in", I["w_in"][0], 0, N_IN)
    for b in "abc":
        st.rows(f"w_branch_{b}", I[f"w_branch_{b}"][0])
    st.rows("w_out", I["w_out"][0])
    ffn("ffn2")


def first_block(nc, g, I, ctx, dump=None):
    with ExitStack() as mine:
        def sb(name, shape):
            return mine.enter_context(nc.sbuf_tensor(name, shape, F32))
        g.o, g.bias = sb("o", [P, TT, D]), sb("bias", [P, BIAS_HEADS, T])
        g.xn = g.o
        g.causal = sb("causal", [P, T])
        setup_phase(nc, g, I)
        ffn_phase(nc, g, "ffn1", ROW_A["ffn1_norm"])
        if dump:
            dump("a")
        mixer_phase(nc, g)
        if dump:
            dump("b")
    g.xn = ctx.enter_context(nc.sbuf_tensor("xn", [P, TT, D], F32))
    ffn_phase(nc, g, "ffn2", ROW_A["ffn2_norm"])
    if dump:
        dump("c")


def constants():
    ident = np.eye(P, dtype=np.float32)
    dist = np.arange(-127, T)
    n = np.maximum(dist, 0)
    exact = NUM_BUCKETS // 2
    nf = np.maximum(n, 1).astype(np.float32)
    large = exact + (np.log(nf / np.float32(exact)) / np.float32(math.log(MAX_DISTANCE / exact))
                     * np.float32(NUM_BUCKETS - exact)).astype(np.int32)
    bucket = np.where(n < exact, n, np.minimum(large, NUM_BUCKETS - 1))
    bucket, d = bucket[::-1], dist[::-1]
    onehot = (bucket[None, :] == np.arange(NUM_BUCKETS)[:, None]).astype(np.float32)
    ok = np.zeros((BIAS_HEADS, DIST), bool)
    ok[:] = d >= 0
    ok[0:4] &= d <= 128
    ok[4:8] &= d % 4 == 0
    ok[8:12] &= d % 16 == 0
    dmask = np.where(ok, np.float32(0), np.float32(MASKED))
    q, c = np.arange(P)[:, None], np.arange(T)[None, :]
    causal = np.where(P + q - c >= 0, np.float32(0), np.float32(MASKED))
    return {"k_ident": ident, "k_flip": np.ascontiguousarray(ident[::-1]), "k_onehot": onehot, "k_dmask": dmask.astype(np.float32), "k_causal": causal.astype(np.float32)}


CH = 32
NCH = T // CH
PAIRS = 4
RW_HEADS = 8
DECAY = -math.exp(-0.5)
LN_EPS = 64e-5
FREQ = 2 * T
TPE = 3 * KC
ER = 12
CTX0 = 4


def second_stream(st, I):
    st.columns("mod_w", I["mod_w_2"][0], 0, 6 * D, "raw")
    st.columns("w_state", I["w_in_2"][0], HY_COLS + STATE_LO, HY_COLS + STATE_HI)
    st.columns("w_in_2", I["w_in_2"][0], 0, HY_COLS + RW_COLS)
    st.columns("w_gates", I["w_in_2"][0], HY_COLS + RW_COLS, IN2_COLS)
    st.rows("hy_proj", I["hy_proj_2"][0])
    st.rows("rw_proj", I["rw_proj_2"][0])
    st.rows("w_out_2", I["w_out_2"][0])


def col(g, name, i=0, n=1):
    if name in ROW_A:
        return g.va[:, ROW_A[name] + i:ROW_A[name] + i + n]
    return g.vb[:, ROW_B[name] + i:ROW_B[name] + i + n]


class HyenaFilter:

    def __init__(self, nc, g, I, S, sb):
        self.nc, self.g, self.I, self.S, self.ps = nc, g, I, S, g.ps
        self.fz = sb("fz", [P, TT, 3 * T + 1])
        self.feat, self.w1, self.w2, self.w3 = sb("feat", [33, T]), sb("w1", [33, HD]), sb("w2", [HD, HD]), sb("w3", [HD, 2 * HY_W])
        self.decay, self.filt, self.absf = (sb(n, [P, TT, 2 * HY_W]) for n in ("decay", "filt", "abs"))
        self.arg, self.k2, self.hid = sb("arg", [HD, T]), sb("turns", [HD, T]), sb("hid", [HD, 2, T])
        self.inorm, self.onesq = sb("inorm", [P, HY_W]), sb("onesq", [P, P])

    def load(self, eng):
        I, S = self.I, self.S
        for dst, src in ((self.feat[:], I["k_feat"]), (self.w1[:], I["hy_ffn_w1_2"][0]), (self.w2[:], I["hy_ffn_w2_2"][0]),
                         (self.w3[:], I["hy_ffn_w3_2"][0])):
            eng.dma_start(dst, src).then_inc(S["ffn_in"], 16)
        for dst, src in ((self.fz[:], I["k_fz"].rearrange("(t p) n -> p t n", p=P)),
                         (self.decay[:], I["k_decay"].rearrange("(t p) n -> p t n", p=P))):
            eng.dma_start(dst, src).then_inc(S["hy_consts"], 16)

    def pe(self, pe, i):
        S, ps, mm_ = self.S, self.ps, self.nc.tensor.matmul
        if i == 1:
            pe.wait_ge(S["ffn_in"], 64)
            mm_(ps[0:HD, 4, 0:T], self.w1[:], self.feat[:], start=True, stop=True).then_inc(S["ffn"], 1)
        if i == 3:
            pe.wait_ge(S["sin"], 1)
            mm_(ps[0:HD, 5, 0:T], self.w2[:], self.hid[:, 0], start=True, stop=True).then_inc(S["ffn"], 1)
        if i == 5:
            pe.wait_ge(S["sin"], 2)
            for t in range(TT):
                for n in range(2):
                    mm = mm_(ps[:, 4 + 2 * t + n, :], self.hid[:, 1, P * t:P * t + P], self.w3[:, 512 * n:512 * n + 512],
                             start=True, stop=True)
            mm.then_inc(S["taps"], 1)
        if i == 7:
            pe.wait_ge(S["filt"], 1)
            pe.wait_ge(S["abs"], 1)
            sides = [(t, n) for t in range(TT) for n in range(2)]
            for j, (t, n) in enumerate(sides):
                mm_(ps[:, 4, :], self.onesq[:], self.absf[:, t, HY_W * n:HY_W * n + HY_W], start=j == 0, stop=j == 3)
            for j, (t, n) in enumerate(sides):
                mm = mm_(ps[0:1, 5, :], self.fz[:, t, 3 * T:3 * T + 1], self.filt[:, t, HY_W * n:HY_W * n + HY_W],
                         start=j == 0, stop=j == 3)
            mm.then_inc(S["norms"], 1)
        if 11 <= i < 15:
            k = i - 11
            if k == 0:
                pe.wait_ge(S["norms_read"], 1)
            for t in range(TT):
                for n in range(2):
                    lo = P * k if n == 0 or k < 2 else P * (k + 2)
                    mm = mm_(ps[:, 4 + k, :], self.fz[:, t, lo:lo + P], self.filt[:, t, HY_W * n:HY_W * n + HY_W],
                             start=t == 0 and n == 0, stop=t == TT - 1 and n == 1)
            mm.then_inc(S["hspec"], 1)

    def act(self, act):
        S, nc = self.S, self.nc
        for j in range(2):
            act.wait_ge(S["arg"], j + 1)
            nc.scalar.activation(self.hid[:, j], self.arg[:], ACT.Sin).then_inc(S["sin"], 1)
        act.wait_ge(S["filt"], 1)
        nc.scalar.activation(self.absf[:], self.filt[:], ACT.Abs).then_inc(S["abs"], 1)

    def dve(self, dve, ch, i):
        S, g, ps, v, arg, k2 = self.S, self.g, self.ps, self.nc.vector, self.arg, self.k2
        if i in (1, 3):
            TWO_PI_HI, TWO_PI_LO = 6.28125, 2 * math.pi - 6.28125
            ROUND = 1.5 * 2 ** 23
            f0, j = HY64_ROW, i // 2
            dve.wait_ge(S["ffn"], j + 1)
            if j:
                dve.wait_ge(S["sin"], 1)
            ch(v.tensor_scalar(arg[:], ps[0:HD, 4 + j, 0:T], g.va[0:HD, f0 + 1 + j:f0 + 2 + j], g.va[0:HD, f0:f0 + 1], ALU.add, ALU.mult))
            ch(v.tensor_scalar(k2[:], arg[:], 1 / (2 * math.pi), ROUND, ALU.mult, ALU.add))
            ch(v.tensor_scalar(k2[:], k2[:], -ROUND, None, ALU.add))
            ch(v.scalar_tensor_tensor(arg[:], k2[:], -TWO_PI_HI, arg[:], ALU.mult, ALU.add))
            ch(v.scalar_tensor_tensor(arg[:], k2[:], -TWO_PI_LO, arg[:], ALU.mult, ALU.add))
            v.tensor_scalar(arg[:], arg[:], 3.1415925, -3.1415925, ALU.min, ALU.max).then_inc(S["arg"], 1)
        if i == 5:
            dve.wait_ge(S["taps"], 1)
            dve.wait_ge(S["hy_consts"], 32)
            v.tensor_tensor(self.filt[:].rearrange("p t n -> p (t n)"), ps[:, 4:8, :].rearrange("p b n -> p (b n)"),
                            self.decay[:].rearrange("p t n -> p (t n)"), ALU.mult).then_inc(S["filt"], 1)
        if i == 8:
            dve.wait_ge(S["norms"], 1)
            ch(v.reciprocal(self.inorm[:], ps[:, 4, :]))
            v.tensor_tensor(g.ny[0:1], ps[0:1, 5, :], self.inorm[0:1, :], ALU.mult).then_inc(S["norms_read"], 1)
        if i == 16:
            dve.wait_ge(S["hspec"], 4)
            v.tensor_tensor(g.hs, ps[:, 4:8, :], self.inorm[:].unsqueeze(1).to_broadcast([P, 4, HY_W]), ALU.mult)


def modulation_phase(nc, g, I):
    with ExitStack() as ctx:
        S = Sems(nc, ctx, "mod")

        def sb(name, shape):
            return ctx.enter_context(nc.sbuf_tensor(name, shape, F32))
        csil, rows, sel = sb("csil", [P, KC, 32]), sb("mod_rows", [P, 2, 256]), sb("mod_sel", [P, 2 + P])
        gate_b, post = sb("gate_bias", [P, 2, D]), sb("post", [P, 2, D])
        ps = g.ps
        filt = HyenaFilter(nc, g, I, S, lambda name, shape: sb("hf_" + name, shape))
        i0 = g.stream.first["mod_w"]
        n_tiles = 6 * D // 256
        gate_tiles = {i: (i - 8, 0) if i < 12 else (i - 20, 1) for i in list(range(8, 12)) + list(range(20, 24))}
        block = ctx.enter_context(nc.Block(no_gpsimd_drain=True))

        @block.sync
        def _(sp):
            load_tiles(g, sp, i0 + n_tiles + R)
            sp.wait_ge(S["post"], 8)
            sp.dma_start(g.post_dram, post[:]).then_inc(S["stored"], 16)
            sp.wait_ge(S["stored"], 16)

        @block.scalar
        def _(act):
            act.dma_start(sel[:], I["k_modsel"]).then_inc(S["sel"], 16)
            act.wait_ge(S["zeroed"], 1)
            nc.scalar.activation(csil[:, :, 0], col(g, "c_2", 0, KC), ACT.Silu).then_inc(S["csil"], 1)
            nc.scalar.activation(csil[:, :, 1], col(g, "c_ctx_2", 0, KC), ACT.Silu).then_inc(S["csil"], 1)
            filt.load(act)
            for dst, name in ((g.masks[:].rearrange("p d n -> p (d n)"), "k_masks"), (g.blockones[:], "k_blockones"),
                              (g.blk16[:], "k_blk16"), (g.restart[:], "k_restart"), (g.ident2[:], "k_ident2")):
                act.dma_start(dst, I[name]).then_inc(S["consts"], 16)
            for j, (m, norm) in enumerate(((2, "norm1_post_2"), (5, "norm2_post_2"))):
                act.dma_start(gate_b[:, j], I["mod_b_2"][:, D * m:D * m + D].to_broadcast([P, D])).then_inc(S["gate_b"], 16)
                act.dma_start(post[:, j], I[norm].to_broadcast([P, D])).then_inc(S["gate_b"], 16)
            filt.act(act)
            act.wait_ge(S["consts"], 80)

        @block.tensor
        def _(pe):
            pe.wait_ge(S["csil"], 2)
            pe.wait_ge(S["sel"], 16)

            def turn(i):
                pe.wait_ge(S["rows"], i + 1)
                for s in range(2):
                    m = 2 * i + s
                    mm = nc.tensor.matmul(ps[:, 2, 2 * m:2 * m + 2], rows[:, i % 2, P * s:P * s + P], sel[:, 0:2],
                                          start=True, stop=True)
                if i in gate_tiles:
                    n = list(gate_tiles).index(i)
                    if n:
                        pe.wait_ge(S["gate"], n)
                    mm = nc.tensor.matmul(ps[:, 3, 0:256], sel[:, 2:2 + P], rows[:, i % 2, :], start=True, stop=True)
                mm.then_inc(S["turned"], 1)

            for i in range(n_tiles):
                wait_tile(g, pe, i0 + i)
                w = tile3(g, i0 + i, KC)
                if i >= 2:
                    pe.wait_ge(S["rows"], i - 1)
                for kk in range(2):
                    for j in range(4):
                        mm = nc.tensor.matmul(ps[32 * j:32 * j + 32, i % 2, 0:256], csil[:, 4 * kk + j, :],
                                              w[:, 4 * kk + j, :], start=kk == 0, stop=kk == 1)
                mm.then_inc(g.raw_used, 1)
                if i:
                    turn(i - 1)
                filt.pe(pe, i)
            turn(n_tiles - 1)

        @block.vector
        def _(dve):
            v = nc.vector
            ch = Chain(dve, S["dve"])
            ch(v.scalar_tensor_tensor(g.own[:], col(g, "rw_mu_2", 0, RWC), -1.0, col(g, "rw_mu_2", RWC, RWC), ALU.mult, ALU.subtract))
            ch(v.tensor_scalar(g.own[:], g.own[:], 1.0, None, ALU.add))
            ch(v.memset(filt.onesq[:], 1.0))
            v.memset(csil[:], 0.0).then_inc(S["zeroed"], 1)

            def gate(i):
                c, j = gate_tiles[i]
                dve.wait_ge(S["gate_b"], 64)
                n = list(gate_tiles).index(i)
                dve.wait_ge(S["turned"], i + 1)
                gb = gate_b[:, j, 256 * c:256 * c + 256]
                po = post[:, j, 256 * c:256 * c + 256]
                v.tensor_tensor(gb, ps[:, 3, 0:256], gb, ALU.add).then_inc(S["gate"], 1)
                dve.wait_ge(S["gate"], n + 1)
                v.tensor_tensor(po, po, gb, ALU.mult).then_inc(S["post"], 1)

            for i in range(n_tiles):
                dve.wait_ge(g.raw_used, g.stream.count(i0 + i, "raw"))
                if i >= 2:
                    dve.wait_ge(S["turned"], i - 1)
                v.tensor_copy(rows[:, i % 2, :], ps[:, i % 2, 0:256]).then_inc(S["rows"], 1)
                if i - 1 in gate_tiles:
                    gate(i - 1)
                filt.dve(dve, ch, i)
            gate(n_tiles - 1)
            dve.wait_ge(S["turned"], n_tiles)
            m3 = g.mod[:].rearrange("p (m r) -> p m r", r=2)
            ch(v.tensor_tensor(m3, ps[:, 2, 0:96].rearrange("p (m r) -> p m r", r=2),
                               col(g, "mod_b_2", 0, 48).unsqueeze(2).to_broadcast([P, 48, 2]), ALU.add))
            for j, (m, r, norm) in enumerate(((1, 0, "norm1_pre_2"), (1, 1, "norm1_pre_2"), (4, 0, "norm2_pre_2"))):
                v.scalar_tensor_tensor(g.scale[:, j, :], m3[:, KC * m:KC * m + KC, r], 1.0, col(g, norm, 0, KC), ALU.add, ALU.mult)
            for j, (m, r) in enumerate(((0, 0), (0, 1), (3, 0))):
                v.tensor_copy(g.shift[:, j, :], m3[:, KC * m:KC * m + KC, r])


def feature_product(g, nc, pe, S, i0, n_chunks, x, banks=4):
    for n in range(n_chunks):
        i, s = i0 + n // 2, P * (n % 2)
        if n % 2 == 0:
            w = split_pair(g, pe, i, KC)
        if n >= banks:
            pe.wait_ge(S["fcopied"], n - banks + 1)
        for k in range(KC):
            mm = product3(nc, g.ps[:, n % banks, 0:T], [y[:, k, s:s + P] for y in w], [y[:, k, :] for y in x],
                          k == 0, k == KC - 1)
        if n % 2 or n == n_chunks - 1:
            mm.then_inc(g.split_used, 1)
        else:
            mm.then_inc(S["even_chunk"], 1)


def wait_feature(g, eng, S, i0, n, last):
    if n % 2 or n == last:
        wait_used(g, eng, i0 + n // 2)
    else:
        eng.wait_ge(S["even_chunk"], n // 2 + 1)


def mix_neighbours(v, ch, dst, src, own, prev, nxt, add=None):
    if add is None:
        ch(v.tensor_scalar(dst, src, own, None, ALU.mult))
    else:
        ch(v.tensor_scalar(dst, src, own, add, ALU.mult, ALU.add))
    ch(v.scalar_tensor_tensor(dst[:, 1:T], src[:, 0:T - 1], prev, dst[:, 1:T], ALU.mult, ALU.add))
    return v.scalar_tensor_tensor(dst[:, 0:T - 1], src[:, 1:T], nxt, dst[:, 0:T - 1], ALU.mult, ALU.add)


def context_phase(nc, g, I, z):
    with ExitStack() as ctx:
        S = Sems(nc, ctx, "ctx")

        def sb(name, shape):
            return ctx.enter_context(nc.sbuf_tensor(name, shape, F32))
        cx, raw = sb("cx", [P, TT, D]), sb("ctx_raw", [P, 9, T])
        act_n, dve_n, pe_n = rms_transposed(g, nc, S, cx, g.xquarter, g.scale[:, 1, :], g.shift[:, 1, :], pair=g.xt2)
        split_buffers(nc, ctx, g, "ctx")
        i0 = g.stream.first["w_state"]
        tiles = range(i0, i0 + 5)
        block = ctx.enter_context(nc.Block(no_gpsimd_drain=True))

        @block.sync
        def _(sp):
            sp.dma_start(cx[:], I["ctx_2"].rearrange("b (t p) d -> p (b t) d", p=P)).then_inc(S["cx"], 16)
            load_tiles(g, sp, i0 + 5 + R)

        @block.tensor
        def _(pe):
            pe_n(pe)
            feature_product(g, nc, pe, S, i0, 9, g.xt2)

        @block.scalar
        def _(act):
            act.wait_ge(S["cx"], 16)
            act_n(act)

            def copy_out(k):
                for n in range(2 * k, min(2 * k + 2, 9)):
                    wait_feature(g, act, S, i0, n, 8)
                    nc.scalar.copy(raw[:, n, :], g.ps[:, n % 4, 0:T]).then_inc(S["fcopied"], 1)
            with_splits(lambda i: split_hi(nc, g, act, i), tiles, copy_out)

        @block.vector
        def _(dve):
            ch = Chain(dve, S["dve"])
            dve.wait_ge(S["cx"], 16)
            dve_n(dve, ch)

            def mix(k):
                for n in range(2 * k, min(2 * k + 2, 9)):
                    dve.wait_ge(S["fcopied"], n + 1)
                    c = CTX0 + n
                    mix_neighbours(nc.vector, ch, z[:, c, :], raw[:, n, :], g.own[:, c:c + 1],
                                   col(g, "rw_mu_2", c), col(g, "rw_mu_2", RWC + c))
            with_splits(lambda i: split_lo(nc, g, dve, i), tiles, mix)


def project_phase(nc, g, I, z, zh):
    with ExitStack() as ctx:
        S = Sems(nc, ctx, "proj2")

        def sb(name, shape):
            return ctx.enter_context(nc.sbuf_tensor(name, shape, F32))
        raw = sb("raw", [P, 4, T])
        act_n, dve_n, pe_n = rms_transposed(g, nc, S, g.x, g.xquarter, g.scale[:, 0, :], g.shift[:, 0, :], pair=g.xt2)
        split_buffers(nc, ctx, g, "proj")
        i0 = g.stream.first["w_in_2"]
        nf = HYC + RWC
        tiles = range(i0, i0 + nf // 2)
        block = ctx.enter_context(nc.Block(no_gpsimd_drain=True))

        @block.sync
        def _(sp):
            load_tiles(g, sp, i0 + nf // 2 + R)

        @block.tensor
        def _(pe):
            pe_n(pe)
            feature_product(g, nc, pe, S, i0, nf, g.xt2)

        @block.scalar
        def _(act):
            act_n(act)

            def copy_out(k):
                for n in (2 * k, 2 * k + 1):
                    wait_feature(g, act, S, i0, n, nf - 1)
                    if n >= 4:
                        act.wait_ge(S["mixed"], n - 3)
                    nc.scalar.copy(raw[:, n % 4, :], g.ps[:, n % 4, 0:T]).then_inc(S["fcopied"], 1)
            with_splits(lambda i: split_hi(nc, g, act, i), tiles, copy_out)

        @block.vector
        def _(dve):
            ch = Chain(dve, S["dve"])
            dve_n(dve, ch)

            def mix(n):
                dve.wait_ge(S["fcopied"], n + 1)
                if n < HYC:
                    ins = mix_neighbours(nc.vector, ch, zh[:, n, :], raw[:, n % 4, :], col(g, "hy_conv_w_2", HYC + n),
                                         col(g, "hy_conv_w_2", n), col(g, "hy_conv_w_2", 2 * HYC + n), col(g, "hy_conv_b_2", n))
                else:
                    c = n - HYC
                    ins = mix_neighbours(nc.vector, ch, z[:, c, :], raw[:, n % 4, :], g.own[:, c:c + 1],
                                         col(g, "rw_mu_2", c), col(g, "rw_mu_2", RWC + c))
                ins.then_inc(S["mixed"], 1)
            with_splits(lambda i: split_lo(nc, g, dve, i), tiles, lambda k: (mix(2 * k), mix(2 * k + 1)))


def recurrence_phase(nc, g, I, z, store, ctx_only, name):
    with ExitStack() as ctx:
        def sb(n, shape):
            return ctx.enter_context(nc.sbuf_tensor(f"{name}_{n}", shape, F32))
        kk = sb("kk", [P, PAIRS, T])
        ar, bk = sb("ar", [P, PAIRS, 2, T]), sb("bk", [P, PAIRS, 2, T])
        tok = sb("tok", [P, 3, TT, RW_WIDTH])
        pc = sb("pc", [P, PAIRS, NCH])
        part = {"tm": sb("tm", [P, NCH, PAIRS, HD]), "rm": sb("rm", [P, NCH, PAIRS, HD])}
        if not ctx_only:
            part |= {"g1": sb("g1", [P, PAIRS, T]), "g2": sb("g2", [P, TT, RW_HEADS, P])}
        st = sb("state", [P, NCH, PAIRS, HD])
        for d in range(2):
            recurrence_inputs(nc, g, I, z, kk, ar, bk, tok, pc, store, part, st, ctx_only, f"{name}{d}", d)
            recurrence_chunks(nc, g, ar, bk, tok, pc, store, part, ctx_only, f"{name}{d}", d)
        recurrence_states(nc, g, store, part, st, ctx_only, f"{name}1", 1)


def recurrence_inputs(nc, g, I, z, kk, ar, bk, tok, pc, store, part, st, ctx_only, name, d):
    with ExitStack() as ctx:
        S = Sems(nc, ctx, name + "i")

        def sb(nm, shape):
            return ctx.enter_context(nc.sbuf_tensor(f"{name}i_{nm}", shape, F32))
        tl = sb("tanh", [P, T])
        w1, w2 = sb("w1", [P, PAIRS, T]), sb("w2", [P, PAIRS, T])
        ld, av, cum = sb("ld", [P, PAIRS, T]), sb("av", [P, PAIRS, T]), sb("cum", [P, PAIRS, T])
        ebk = sb("ebk", [P, 2, PAIRS, T])
        tot = sb("tot", [P, PAIRS, NCH])
        ps = g.ps
        turn0 = 2 if d else 6
        before = States(nc, g, S, store, part, st, ctx_only, 0) if d else None
        k, v_, r = z[:, 4:8, :], z[:, 8:12, :], z[:, 0:4, :]
        v = nc.vector
        block = ctx.enter_context(nc.Block(no_gpsimd_drain=True))

        def per(nm, i=0):
            return col(g, nm, i, PAIRS).unsqueeze(2).to_broadcast([P, PAIRS, T])

        def chunked(x):
            return x.rearrange("p c (n s) -> p (c n) s", s=CH)

        def totb():
            return tot[:].rearrange("p c n -> p (c n)").unsqueeze(2).to_broadcast([P, PAIRS * NCH, CH])

        lora = sb("lora", [P, RW_WIDTH])

        @block.sync
        def _(sp):
            sp.dma_start(lora[0:64, :], I["rw_w_up_2"][0, d]).then_inc(S["lora_in"], 16)
            sp.dma_start(lora[64:P, :], I["rw_a_up_2"][0, d]).then_inc(S["lora_in"], 16)

        @block.tensor
        def _(pe):
            if d == 0:
                pe.wait_ge(S["ksq"], 1)
                for c in range(PAIRS):
                    mm = nc.tensor.matmul(ps[:, c // 2, T * (c % 2):T * (c % 2) + T], g.blockones[:], w1[:, c, :], start=True, stop=True)
                mm.then_inc(S["ksum"], 1)
            pe.wait_ge(S["tanh"], 1)
            pe.wait_ge(S["lora_in"], 32)
            for c in range(PAIRS):
                nc.tensor.matmul(ps[:, 2 + c // 2, T * (c % 2):T * (c % 2) + T], lora[0:64, P * c:P * c + P],
                                 tl[0:64, :], start=True, stop=True)
            for c in range(PAIRS):
                mm = nc.tensor.matmul(ps[:, 4 + c // 2, T * (c % 2):T * (c % 2) + T], lora[64:P, P * c:P * c + P],
                                      z[64:P, 12, :], start=True, stop=True)
            mm.then_inc(S["lora"], 1)
            if d:
                for n in range(NCH):
                    before.pe_step(pe, n)
            q = 0
            for j in range(d, 4):
                if j:
                    pe.wait_ge(S["ready"], j)
                for t in range(TT):
                    if q >= 2:
                        pe.wait_ge(S["tokcopy"], q - 1)
                    for c in range(PAIRS):
                        src = (v_[:, c], ar[:, c, 0], ebk[:, 0, c], ebk[:, 1, c])[j][:, P * t:P * t + P]
                        mm = nc.tensor.transpose(ps[:, turn0 + q % 2, P * c:P * c + P], src, g.ident[:])
                    mm.then_inc(S["tokturn"], 1)
                    q += 1

        @block.scalar
        def _(act):
            nc.scalar.activation(tl[0:64, :], z[0:64, 12, :], ACT.Tanh).then_inc(S["tanh"], 1)
            if d == 0:
                act.wait_ge(S["kmax"], 1)
                nc.scalar.activation(w2[:], w2[:], ACT.Sqrt).then_inc(S["kroot"], 1)
            act.wait_ge(S["lora"], 1)
            for c in range(PAIRS):
                nc.scalar.activation(ld[:, c, :], ps[:, 2 + c // 2, T * (c % 2):T * (c % 2) + T], ACT.Sigmoid,
                                     bias=col(g, "rw_w0_2", 4 * d + c))
            for c in range(PAIRS):
                ins = nc.scalar.activation(av[:, c, :], ps[:, 4 + c // 2, T * (c % 2):T * (c % 2) + T], ACT.Sigmoid,
                                           bias=col(g, "rw_a0_2", 4 * d + c))
            ins.then_inc(S["sig"], 1)
            act.wait_ge(S["logs"], 1)
            nc.scalar.activation(w1[:], w1[:], ACT.Exp).then_inc(S["exp"], 1)
            nc.scalar.activation(w2[:], cum[:], ACT.Exp).then_inc(S["exp"], 1)
            nc.scalar.activation(pc[:], tot[:], ACT.Exp).then_inc(S["exp"], 1)
            act.wait_ge(S["exp"], 3)
            nc.scalar.activation(cum[:], cum[:], ACT.Exp, scale=-1.0).then_inc(S["exp"], 1)
            q = 0
            for j in range(d, 4):
                for t in range(TT):
                    act.wait_ge(S["tokturn"], q + 1)
                    dst = store["v"][:, t, :] if j == 0 else tok[:, j - 1, t, :]
                    nc.scalar.copy(dst, ps[:, turn0 + q % 2, :]).then_inc(S["tokcopy"], 1)
                    q += 1

        @block.vector
        def _(dve):
            ch = Chain(dve, S["dve"])
            if d == 0:
                ch(v.tensor_tensor(kk[:], k, per("rw_k_k_2"), ALU.mult))
                v.tensor_tensor(w1[:], kk[:], kk[:], ALU.mult).then_inc(S["ksq"], 1)
                dve.wait_ge(S["ksum"], 1)
                v.tensor_scalar(w2[:].rearrange("p c t -> p (c t)"), ps[:, 0:2, :].rearrange("p b n -> p (b n)"), 1e-24, None,
                                ALU.max).then_inc(S["kmax"], 1)
                dve.wait_ge(S["kroot"], 1)
                ch(v.reciprocal(w2[:], w2[:]))
                ch(v.tensor_tensor(kk[:], kk[:], w2[:], ALU.mult))
            else:
                before.dve_start()
            states_done = [0]

            def move_state():
                n = states_done[0]
                if d and n < before.moves:
                    before.dve_step(dve, n)
                    states_done[0] += 1
            move_state()
            move_state()
            dve.wait_ge(S["sig"], 1)
            ch(v.tensor_scalar(ld[:], ld[:], DECAY, None, ALU.mult))
            for c in range(PAIRS):
                ch.add(v.tensor_tensor_scan(cum[:, c, :], g.restart[:], ld[:, c, :], 0.0, ALU.mult, ALU.add))
                if c == 1:
                    move_state()
            ch.sync()
            ch(v.tensor_copy(tot[:].rearrange("p c n -> p (c n)"), chunked(cum[:])[:, :, CH - 1]))
            if d:
                ch(v.tensor_tensor(cum[:], ld[:], cum[:], ALU.subtract))
                move_state()
                ch(v.tensor_tensor(chunked(cum[:]), chunked(cum[:]), totb(), ALU.add))
            v.tensor_tensor(w1[:], cum[:], ld[:], ALU.subtract).then_inc(S["logs"], 1)
            move_state()
            keys, rated = ebk[:, 1], ebk[:, 0]
            ch(v.tensor_scalar(keys, av[:], -1.0, None, ALU.add))
            ch(v.tensor_tensor(keys, keys, per("rw_k_a_2"), ALU.mult))
            move_state()
            ch(v.scalar_tensor_tensor(keys, keys, 1.0, k, ALU.add, ALU.mult))
            ch.add(v.tensor_tensor(rated, kk[:], av[:], ALU.mult))
            move_state()
            if not ctx_only:
                if d == 0:
                    ch.add(v.tensor_copy(store["kmod"], keys))
                else:
                    ch.add(v.tensor_tensor(store["kmod"], store["kmod"], keys, ALU.add))
            move_state()
            dve.wait_ge(S["exp"], 1)
            v.scalar_tensor_tensor(ar[:, :, 0, :], kk[:], -1.0, w1[:], ALU.mult, ALU.mult).then_inc(S["ready"], 1)
            if not ctx_only:
                dve.wait_ge(S["exp"], 2)
                ch.add(v.tensor_tensor(ar[:, :, 1, :], r, w2[:], ALU.mult))
            dve.wait_ge(S["exp"], 4)
            ch.sync()
            for j, own in enumerate((rated, keys)):
                ch(v.tensor_tensor(bk[:, :, j, :], own, cum[:], ALU.mult))
                for c in range(PAIRS):
                    src = bk[:, c, j, :].rearrange("p (n s) -> p n s", s=CH)
                    dst = ebk[:, j, c, :].rearrange("p (n s) -> p n s", s=CH)
                    ins = v.tensor_tensor(dst, src, pc[:, c, :].unsqueeze(2).to_broadcast([P, NCH, CH]), ALU.mult)
                ins.then_inc(S["ready"], 1)
            if d and not ctx_only:
                before.dve_outputs(dve)


def recurrence_chunks(nc, g, ar, bk, tok, pc, store, part, ctx_only, name, d):
    with ExitStack() as ctx:
        def sb(nm, shape):
            return ctx.enter_context(nc.sbuf_tensor(f"{name}c_{nm}", shape, F32))
        S = Sems(nc, ctx, name + "c")
        ps, v = g.ps, nc.vector
        tm, rm, vtok = part["tm"], part["rm"], store["v"]
        H4 = 4
        prod = sb("prod", [P, 2, H4, 4, P])
        a16, b16, x16, yv = (sb(n, [P, 2, H4, P]) for n in ("a16", "b16", "x16", "y"))
        ftil, km = sb("f", [P, 2, H4, HD]), sb("km", [P, 2, H4, HD])

        def a2(s):
            return prod[:, s, :, 0]

        def b2(s):
            return prod[:, s, :, 2]
        a4, b4 = a16, b16
        its = [(t, h4) for t in range(TT) for h4 in range(2)]
        block = ctx.enter_context(nc.Block(no_gpsimd_drain=True))
        NR = 10

        def order():
            for it in range(0, len(its), 2):
                for r in range(NR):
                    for j in range(2):
                        yield its[it + j], r, it + j

        def half(x, h):
            return x[HD * (h % 2):HD * (h % 2) + HD]

        @block.tensor
        def _(pe):
            mmf = nc.tensor.matmul
            for (t, h4), r, n in order():
                b = 4 * h4
                s = h4
                if r:
                    pe.wait_ge(S[f"rd{h4}"], NR * (n // 2) + r)
                elif n >= 2:
                    pe.wait_ge(S[f"rd{h4}"], NR * (n // 2))
                heads = [4 * h4 + i for i in range(H4)]
                tsl = slice(P * t, P * t + P)
                if r == 0:
                    for i, h in enumerate(heads):
                        ah, bh = half(ar[:, h // 2], h), half(bk[:, h // 2], h)
                        if ctx_only:
                            mmf(ps[:, b + i, 0:P], bh[:, 0, tsl], ah[:, 0, tsl], start=True, stop=True)
                        else:
                            mmf(ps[:, b + i, 0:2 * P], bh[:, 0, tsl], ah[:, :, tsl], start=True, stop=True)
                        mm = mmf(ps[:, b + i, 2 * P:4 * P], ah[:, 0, tsl], bh[:, :, tsl], start=True, stop=True)
                elif r == 1:
                    for i, h in enumerate(heads):
                        mmf(ps[:, b, P * i:P * i + P], b16[:, s, i], a16[:, s, i], start=True, stop=True)
                        mm = mmf(ps[:, b + 1, P * i:P * i + P], a16[:, s, i], b16[:, s, i], start=True, stop=True)
                    if not ctx_only:
                        for i, h in enumerate(heads):
                            ah, bh = half(ar[:, h // 2], h), half(bk[:, h // 2], h)
                            mm = mmf(ps[:, b + 2 + h % 2, P * (i // 2):P * (i // 2) + P], bh[:, 1, tsl], ah[:, 1, tsl],
                                     start=True, stop=True)
                elif r == 2:
                    for i in range(H4):
                        mmf(ps[:, b, P * i:P * i + P], b2(s)[:, i], a2(s)[:, i], start=True, stop=True)
                        mmf(ps[:, b + 1, P * i:P * i + P], a2(s)[:, i], b2(s)[:, i], start=True, stop=True)
                        mm = mmf(ps[:, b + 2, P * i:P * i + P], b2(s)[:, i], yv[:, s, i], start=True, stop=True)
                elif r == 3:
                    for i in range(H4):
                        mmf(ps[:, b, P * i:P * i + P], a4[:, s, i], b4[:, s, i], start=True, stop=True)
                        mm = mmf(ps[:, b + 1, P * i:P * i + P], b4[:, s, i], yv[:, s, i], start=True, stop=True)
                elif r == 4:
                    for i in range(H4):
                        mm = mmf(ps[:, b, P * i:P * i + P], b2(s)[:, i], yv[:, s, i], start=True, stop=True)
                elif r == 5:
                    for i in range(H4):
                        mmf(ps[:, b, P * i:P * i + P], x16[:, s, i], yv[:, s, i], start=True, stop=True)
                        mm = nc.tensor.transpose(ps[:, b + 1, P * i:P * i + P], yv[:, s, i], g.ident[:])
                elif r == 6:
                    for i in range(H4):
                        mm = mmf(ps[:, b, P * i:P * i + P], b2(s)[:, i], a2(s)[:, i], start=True, stop=True)
                elif r == 7:
                    for i, h in enumerate(heads):
                        if not ctx_only:
                            mmf(ps[:, b, P * i:P * i + P], yv[:, s, i], prod[:, s, i, 1], start=True, stop=True)
                        mm = mmf(ps[:, b + 1, HD * i:HD * i + HD], yv[:, s, i], tok[:, 1, t, HD * h:HD * h + HD],
                                 start=True, stop=True)
                elif r == 8:
                    for i, h in enumerate(heads):
                        mm = mmf(ps[:, b + 1, HD * i:HD * i + HD], prod[:, s, i, 3], ftil[:, s, i], start=True, stop=True)
                        if not ctx_only:
                            mmf(ps[:, b, P * i:P * i + P], prod[:, s, i, 3], a4[:, s, i], start=True, stop=True)
                            mm = mmf(half(ps[:, b + 2, P * (i // 2):P * (i // 2) + P], h), tok[:, 0, t, HD * h:HD * h + HD],
                                     a4[:, s, i], start=True, stop=True)
                else:
                    for i, h in enumerate(heads):
                        for c in range(4):
                            rows = slice(CH * c, CH * c + CH)
                            o0 = HD * (i // 2)
                            mmf(half(ps[:, b + c, o0:o0 + HD], h), tok[rows, 0, t, HD * h:HD * h + HD], ftil[rows, s, i],
                                start=True, stop=True)
                            mm = mmf(half(ps[:, b + c, P + o0:P + o0 + HD], h), km[rows, s, i], vtok[rows, t, HD * h:HD * h + HD],
                                     start=True, stop=True)
                mm.then_inc(S[f"pe{h4}"], 1)

        copy_rounds = (1, 2, 3, 5) if ctx_only else (1, 2, 3, 5, 7)

        def rows4(x):
            return x.rearrange("p (h q) -> p h q", h=H4)

        @block.scalar
        def _(act):
            for (t, h4), r, n in order():
                if r not in copy_rounds:
                    continue
                b, s = 4 * h4, h4
                act.wait_ge(S[f"pe{h4}"], NR * (n // 2) + r + 1)
                dst = b4[:, s] if r == 2 else a4[:, s] if r == 7 else b2(s)
                src = ps[:, b + (r in (1, 2, 5)), :]
                nc.scalar.copy(dst, rows4(src)).then_inc(S[f"cp{h4}"], 1)

        @block.vector
        def _(dve):
            ch = Chain(dve, S["dve"])
            flat = lambda x: x.rearrange("p h q -> p (h q)")
            copies = [0, 0]
            for (t, h4), r, n in order():
                b, s = 4 * h4, h4
                dve.wait_ge(S[f"pe{h4}"], NR * (n // 2) + r + 1)
                if r in copy_rounds:
                    copies[h4] += 1
                    dve.wait_ge(S[f"cp{h4}"], copies[h4])
                if r == 0:
                    m4 = g.masks[:, d].rearrange("p (k q) -> p k q", k=4)
                    for i in range(H4):
                        if ctx_only:
                            for k in (0, 2, 3):
                                ch.add(v.tensor_tensor(prod[:, s, i, k], ps[:, b + i, P * k:P * k + P], m4[:, k], ALU.mult))
                        else:
                            ch.add(v.tensor_tensor(prod[:, s, i], ps[:, b + i, :].rearrange("p (k q) -> p k q", k=4), m4, ALU.mult))
                    ch.sync()
                    blk = g.blk16[:].unsqueeze(1).to_broadcast([P, H4, P])
                    idb = g.ident[:].unsqueeze(1).to_broadcast([P, H4, P])
                    ch(v.tensor_tensor(a16[:, s], prod[:, s, :, 2], blk, ALU.mult))
                    ch.add(v.tensor_tensor(yv[:, s], a16[:, s], idb, ALU.add))
                    ch(v.tensor_tensor(b16[:, s], prod[:, s, :, 0], blk, ALU.mult))
                    ins = v.tensor_tensor(x16[:, s], prod[:, s, :, 0], b16[:, s], ALU.subtract)
                elif r == 1:
                    if not ctx_only:
                        incl = g.masks[:, d, P:2 * P].unsqueeze(1).to_broadcast([P, 2, P])
                        for e in range(2):
                            ch.add(v.tensor_tensor(part["g2"][:, t, 4 * h4 + e:4 * h4 + 4:2],
                                                   ps[:, b + 2 + e, 0:256].rearrange("p (k q) -> p k q", k=2), incl, ALU.mult))
                    ins = v.tensor_copy(a2(s), rows4(ps[:, b, :]))
                elif r == 2:
                    ch.add(v.tensor_copy(flat(a4[:, s]), ps[:, b, :]))
                    ins = v.tensor_tensor(flat(yv[:, s]), flat(yv[:, s]), ps[:, b + 2, :], ALU.add)
                elif r == 3:
                    ins = v.tensor_tensor(flat(yv[:, s]), flat(yv[:, s]), ps[:, b + 1, :], ALU.add)
                elif r == 4:
                    ins = v.tensor_tensor(flat(yv[:, s]), flat(yv[:, s]), ps[:, b, :], ALU.add)
                elif r == 5:
                    ins = v.tensor_copy(a2(s), rows4(ps[:, b, :]))
                elif r == 6:
                    ins = v.tensor_tensor(flat(yv[:, s]), flat(yv[:, s]), ps[:, b, :], ALU.add)
                elif r == 7:
                    ins = v.tensor_copy(flat(ftil[:, s]), ps[:, b + 1, 0:256])
                elif r == 8:
                    kt = tok[:, 2, t, 256 * h4:256 * h4 + 256]
                    ins = v.tensor_tensor(flat(km[:, s]), ps[:, b + 1, 0:256], kt, ALU.add)
                    if not ctx_only:
                        ch.add(ins)
                        g2 = part["g2"][:, t, 4 * h4:4 * h4 + 4]
                        ch.add(v.tensor_tensor(g2, rows4(ps[:, b, :]), g2, ALU.add))
                        ins = v.tensor_tensor(part["g1"][:, 2 * h4:2 * h4 + 2, P * t:P * t + P],
                                              ps[:, b + 2, 0:256].rearrange("p (k q) -> p k q", k=2),
                                              ar[:, 2 * h4:2 * h4 + 2, 1, P * t:P * t + P], ALU.add)
                else:
                    for c in range(4):
                        for k in range(2):
                            pr = 2 * h4 + k
                            ch.add(v.scalar_tensor_tensor(tm[:, 4 * t + c, pr], g.ident2[:], pc[:, pr, 4 * t + c:4 * t + c + 1],
                                                          ps[:, b + c, HD * k:HD * k + HD], ALU.mult, ALU.add))
                        ins = v.tensor_copy(rm[:, 4 * t + c, 2 * h4:2 * h4 + 2],
                                            ps[:, b + c, P:2 * P].rearrange("p (k e) -> p k e", k=2))
                        if c < 3:
                            ch.add(ins)
                ch.sync()
                ins.then_inc(S[f"rd{h4}"], 1)


class States:

    def __init__(self, nc, g, S, store, part, st, ctx_only, d):
        self.nc, self.g, self.S, self.store, self.part, self.st, self.ctx_only, self.d = nc, g, S, store, part, st, ctx_only, d
        self.moves = NCH if ctx_only else NCH - 1

    def chunk(self, n):
        return NCH - 1 - n if self.d else n

    def pe_step(self, pe, n):
        nc, S, st, ps, part = self.nc, self.S, self.st, self.g.ps, self.part
        k = self.chunk(n)
        pe.wait_ge(S["state"], n + 1)
        if n < self.moves:
            for par in range(2):
                lo = HD * par
                for pr in range(PAIRS):
                    o0 = 256 * (n % 2) + pr * HD
                    mm = nc.tensor.matmul(ps[lo:lo + HD, 6, o0:o0 + HD], part["tm"][lo:lo + HD, k, pr],
                                          st[lo:lo + HD, n, pr], start=True, stop=True)
            mm.then_inc(S["moved"], 1)
        if self.ctx_only:
            return
        t, c = k // 4, k % 4
        for par in range(2):
            lo = HD * par
            bank = ps[:, par, 256 * t:256 * t + 256]
            if n % 4 == 0:
                for pr in range(PAIRS):
                    h = 2 * pr + par
                    nc.tensor.matmul(bank[:, HD * pr:HD * pr + HD], part["g2"][:, t, h], self.store["v"][:, t, HD * h:HD * h + HD],
                                     start=n == 0 and pr == 0, stop=False, skip_group_check=True)
            for pr in range(PAIRS):
                mm = nc.tensor.matmul(bank[CH * c:CH * c + CH, HD * pr:HD * pr + HD], part["g1"][lo:lo + HD, pr, CH * k:CH * k + CH],
                                      st[lo:lo + HD, n, pr], start=False, stop=True, skip_group_check=True)
        if n == NCH - 1:
            mm.then_inc(S["y"], 1)

    def dve_start(self):
        if self.ctx_only:
            self.nc.vector.memset(self.st[:, 0], 0.0).then_inc(self.S["state"], 1)
        else:
            self.nc.vector.tensor_copy(self.st[:, 0], self.store["carry"][:, self.d]).then_inc(self.S["state"], 1)

    def dve_step(self, dve, n):
        dve.wait_ge(self.S["moved"], n + 1)
        dst = self.store["carry"][:, self.d] if n == NCH - 1 else self.st[:, n + 1]
        o0 = 256 * (n % 2)
        self.nc.vector.tensor_tensor(dst, self.g.ps[:, 6, o0:o0 + 256].rearrange("p (c e) -> p c e", e=HD),
                                     self.part["rm"][:, self.chunk(n)], ALU.add).then_inc(self.S["state"], 1)

    def dve_outputs(self, dve):
        dve.wait_ge(self.S["y"], 1)
        for t in range(TT):
            for par in range(2):
                dst = self.store["y"][:, t, :].rearrange("p (c two e) -> p two c e", two=2, e=HD)[:, par]
                src = self.g.ps[:, par, 256 * t:256 * t + 256].rearrange("p (c e) -> p c e", e=HD)
                if self.d:
                    self.nc.vector.tensor_tensor(dst, src, dst, ALU.add)
                else:
                    self.nc.vector.tensor_copy(dst, src)


def recurrence_states(nc, g, store, part, st, ctx_only, name, d):
    with ExitStack() as ctx:
        S = Sems(nc, ctx, name + "s")
        states = States(nc, g, S, store, part, st, ctx_only, d)
        block = ctx.enter_context(nc.Block(no_gpsimd_drain=True))

        @block.tensor
        def _(pe):
            for n in range(NCH):
                states.pe_step(pe, n)

        @block.vector
        def _(dve):
            states.dve_start()
            for n in range(states.moves):
                states.dve_step(dve, n)
            if not ctx_only:
                states.dve_outputs(dve)


def hyena_phase(nc, g, I, zh, yh):
    with ExitStack() as ctx:
        S = Sems(nc, ctx, "hy")

        def sb(name, shape):
            return ctx.enter_context(nc.sbuf_tensor("hy_" + name, shape, F32))
        fz = sb("fz", [P, TT, 3 * T + 1])
        gi = sb("gi", [P, 4, T])
        alt = sb("alt", [1, T])
        zt = sb("zt", [P, TT, HY_W])
        zs, hs, ys = sb("zs", [P, 4, HY_W]), g.hs, sb("ys", [P, 4, HY_W])
        ny, cross = sb("ny", [1, HY_W]), sb("cross", [P, 4, HY_W])
        ps, v = g.ps, nc.vector
        block = ctx.enter_context(nc.Block(no_gpsimd_drain=True))

        @block.sync
        def _(sp):
            for dst, src in ((fz[:], I["k_fz"].rearrange("(t p) n -> p t n", p=P)), (gi[:], I["k_gi"].rearrange("(k p) n -> p k n", p=P)),
                             (alt[:], I["k_alt"])):
                sp.dma_start(dst, src).then_inc(S["consts"], 16)

        @block.tensor
        def _(pe):
            mm_ = nc.tensor.matmul
            pe.wait_ge(S["z"], 1)
            for t in range(TT):
                for c in range(4):
                    mm = nc.tensor.transpose(ps[:, 2 + t, P * c:P * c + P], zh[:, 4 + c, P * t:P * t + P], g.ident[:])
            mm.then_inc(S["zturn"], 1)
            pe.wait_ge(S["zt"], 2)
            pe.wait_ge(S["consts"], 48)
            for k in range(4):
                for t in range(TT):
                    mm = mm_(ps[:, 4 + k, :], fz[:, t, P * k:P * k + P], zt[:, t], start=t == 0, stop=t == TT - 1)
            mm.then_inc(S["zspec"], 1)
            for t in range(TT):
                mm = mm_(ps[0:1, 0, :], fz[:, t, 3 * T:3 * T + 1], zt[:, t], start=t == 0, stop=t == TT - 1)
            mm.then_inc(S["zlast"], 1)
            pe.wait_ge(S["ys"], 1)
            for c in range(4):
                for k in range(4):
                    mm_(ps[:, c, 0:T], ys[:, k, P * c:P * c + P], gi[:, k, :], start=k == 0, stop=False)
                mm = mm_(ps[:, c, 0:T], ny[0:1, P * c:P * c + P], alt[0:1, :], start=False, stop=True)
            mm.then_inc(S["conv"], 1)

        @block.scalar
        def _(act):
            act.wait_ge(S["zturn"], 1)
            for t in range(TT):
                nc.scalar.copy(zt[:, t], ps[:, 2 + t, :]).then_inc(S["zt"], 1)
            act.wait_ge(S["zspec"], 1)
            nc.scalar.copy(zs[:], ps[:, 4:8, :]).then_inc(S["zs"], 1)

        @block.vector
        def _(dve):
            ch = Chain(dve, S["dve"])
            v.tensor_tensor(zh[:, 4:8], zh[:, 4:8], zh[:, 8:12], ALU.mult).then_inc(S["z"], 1)
            dve.wait_ge(S["zlast"], 1)
            ch(v.tensor_tensor(ny[:], ps[0:1, 0, :], g.ny[0:1], ALU.mult))
            dve.wait_ge(S["zs"], 1)
            ch.add(v.tensor_tensor(ys[:, 0:2], zs[:, 0:2], hs[:, 0:2], ALU.mult))
            ch.add(v.tensor_tensor(ys[:, 2:4], zs[:, 0:2], hs[:, 2:4], ALU.mult))
            ch.sync()
            ch.add(v.tensor_tensor(cross[:, 0:2], zs[:, 2:4], hs[:, 2:4], ALU.mult))
            ch.add(v.tensor_tensor(cross[:, 2:4], zs[:, 2:4], hs[:, 0:2], ALU.mult))
            ch.sync()
            ch(v.tensor_tensor(ys[:, 0:2], ys[:, 0:2], cross[:, 0:2], ALU.subtract))
            v.tensor_tensor(ys[:, 2:4], ys[:, 2:4], cross[:, 2:4], ALU.add).then_inc(S["ys"], 1)
            dve.wait_ge(S["conv"], 1)
            for c in range(4):
                ch(v.scalar_tensor_tensor(yh[:, c], zh[:, 4 + c], col(g, "hy_bias_2", c), ps[:, c, 0:T], ALU.mult, ALU.add))
            ch(v.tensor_tensor(yh[:], yh[:], zh[:, 0:4], ALU.mult))


def merge_phase(nc, g, I, z, yh, store):
    with ExitStack() as ctx:
        S = Sems(nc, ctx, "mg")

        def sb(name, shape):
            return ctx.enter_context(nc.sbuf_tensor("mg_" + name, shape, F32))
        gates, post = sb("gates", [P, TT, 2 * D]), sb("post", [P, D])
        lng, lnb, gup = sb("lng", [P, RW_WIDTH]), sb("lnb", [P, RW_WIDTH]), sb("gup", [P, RW_WIDTH])
        hsel = sb("hsel", [P, 2])
        slg, q = sb("slg", [P, T]), sb("q", [P, PAIRS, T])
        cen, st = sb("cen", [P, TT, RW_WIDTH]), sb("st", [P, TT, 4, RW_HEADS])
        sq = z[:, 4:8, :].rearrange("p c n -> p (c n)").rearrange("p (t f) -> p t f", t=TT)
        split_buffers(nc, ctx, g, "merge")
        mixed, tmp = sb("mixed", [P, TT, D]), sb("tmp", [P, TT, D])
        ss = sb("ss", [P, 8])
        y, vt = store["y"], store["v"]
        ps, v = g.ps, nc.vector
        i0, hy0, rw0, out0 = (g.stream.first[n] for n in ("w_gates", "hy_proj", "rw_proj", "w_out_2"))
        block = ctx.enter_context(nc.Block(no_gpsimd_drain=True))

        def heads(x):
            return x.rearrange("p t (h e) -> p t h e", e=HD)

        def branch_rows(part, t):
            return (g.xt2[part][:, PAIRS:2 * PAIRS, P * t:P * t + P], ps[:, 1 + t, :].rearrange("p (c n) -> p c n", c=PAIRS))

        @block.sync
        def _(sp):
            for dst, src in ((lng[:], I["rw_ln_g_2"].to_broadcast([P, RW_WIDTH])), (lnb[:], I["rw_ln_b_2"].to_broadcast([P, RW_WIDTH])),
                             (gup[:], I["rw_g_up_2"][0]), (hsel[:], I["k_headsel"]), (post[:], g.post_dram[:, 0])):
                sp.dma_start(dst, src).then_inc(S["consts"], 16)
            load_tiles(g, sp, out0 + 4 + R)

        @block.tensor
        def _(pe):
            mm_ = nc.tensor.matmul
            for i in range(8):
                if i >= 2:
                    pe.wait_ge(S["gates"], i - 1)
                column_product(nc, g, pe, i0 + i, ps[:, i % 2, :])
            pe.wait_ge(S["consts"], 80)
            pe.wait_ge(S["slg"], 1)
            pe.wait_ge(S["q"], 1)
            pe.wait_ge(S["gates"], 8)
            for t in range(TT):
                mm_(ps[:, 2 + t, :], slg[:, P * t:P * t + P], gup[:], start=True, stop=True)
                for c in range(PAIRS):
                    mm = mm_(ps[:, 0, 8 * t + 2 * c:8 * t + 2 * c + 2], q[:, c, P * t:P * t + P], hsel[:], start=True, stop=True)
            mm.then_inc(S["rwgate"], 1)
            pe.wait_ge(S["yh"], 1)
            token_product(nc, g, pe, g.xt2, hy0, 2)
            pe.wait_ge(S["yrw"], 1)
            for t in range(TT):
                for c in range(PAIRS):
                    mm = nc.tensor.transpose(ps[:, 1 + t, P * c:P * c + P], y[:, t, P * c:P * c + P], g.ident[:])
            mm.then_inc(S["yturn"], 1)
            pe.wait_ge(S["yt"], 2)
            pe.wait_ge(S["hy_read"], 2)
            token_product(nc, g, pe, g.xt2, rw0, 2, PAIRS)
            pe.wait_ge(S["mixed"], TT)
            turn_rows(nc, g, pe, S, mixed, "mt", KC)
            pe.wait_ge(S["mt"], 4)
            token_product(nc, g, pe, g.xt2, out0, 4)

        @block.scalar
        def _(act):
            nc.scalar.activation(slg[:], z[:, 13, :], ACT.Sigmoid).then_inc(S["slg"], 1)

            def gate(i):
                wait_used(g, act, i0 + i)
                nc.scalar.activation(gates[:, :, 256 * i:256 * i + 256],
                                     ps[:, i % 2, :].rearrange("p (t n) -> p t n", t=TT), ACT.Sigmoid).then_inc(S["gates"], 1)
            for k in range(10):
                split_hi(nc, g, act, i0 + k)
                if k == 4:
                    act.wait_ge(S["var"], 1)
                    nc.scalar.activation(st[:, :, 2], st[:, :, 1], ACT.Sqrt).then_inc(S["root"], 1)
                if k >= 2:
                    gate(k - 2)
            nc.scalar.copy(g.xt2[0][:, 0:4], yh[:]).then_inc(S["yh_hi"], 1)
            for i in (hy0 + 2, hy0 + 3, hy0 + 4):
                split_hi(nc, g, act, i)
            act.wait_ge(S["yturn"], 1)
            for t in range(TT):
                nc.scalar.copy(*branch_rows(0, t)).then_inc(S["yt_hi"], 1)
            for i in (out0 + 1, out0 + 2):
                split_hi(nc, g, act, i)
            turned_hi(nc, g, act, S, g.xt2, "mt", KC)
            split_hi(nc, g, act, out0 + 3)
            wait_used(g, act, out0 + 3)
            for t in range(TT):
                nc.scalar.activation(tmp[:, t].rearrange("p (b n) -> p b n", b=2), ps[:, 4 + 2 * t:6 + 2 * t, :], ACT.Square,
                                     accum_out=ss[:, t:t + 1]).then_inc(S["ss"], 1)
            act.wait_ge(S["mean"], 1)
            nc.scalar.activation(ss[:, 4:6], ss[:, 2:4], ACT.Sqrt).then_inc(S["root2"], 1)

        @block.vector
        def _(dve):
            ch = Chain(dve, S["dve"])
            for i in range(3):
                split_lo(nc, g, dve, i0 + i)
            for c in range(PAIRS):
                ch(v.scalar_tensor_tensor(q[:, c], z[:, c], col(g, "rw_r_k_2", c), store["kmod"][:, c], ALU.mult, ALU.mult))
            v.memset(ss[:, 6:8], 0.0).then_inc(S["q"], 1)
            ch(v.tensor_reduce(st[:, :, 0], heads(y), AX_X, ALU.add))
            ch(v.tensor_scalar(st[:, :, 0], st[:, :, 0], 1.0 / HD, None, ALU.mult))
            for t in range(TT):
                m3 = st[:, t, 0].unsqueeze(2).to_broadcast([P, RW_HEADS, HD])
                ch(v.tensor_tensor(cen[:, t].rearrange("p (h e) -> p h e", e=HD), y[:, t].rearrange("p (h e) -> p h e", e=HD), m3, ALU.subtract))
            ch(v.tensor_tensor(sq, cen[:], cen[:], ALU.mult))
            ch(v.tensor_reduce(st[:, :, 1], heads(sq), AX_X, ALU.add))
            v.tensor_scalar(st[:, :, 1], st[:, :, 1], 1.0 / HD, LN_EPS, ALU.mult, ALU.add).then_inc(S["var"], 1)
            for i in (3, 4):
                split_lo(nc, g, dve, i0 + i)
            dve.wait_ge(S["root"], 1)
            ch(v.reciprocal(st[:, :, 2], st[:, :, 2]))
            dve.wait_ge(S["consts"], 80)
            for t in range(TT):
                c3 = cen[:, t].rearrange("p (h e) -> p h e", e=HD)
                ch(v.tensor_tensor(c3, c3, st[:, t, 2].unsqueeze(2).to_broadcast([P, RW_HEADS, HD]), ALU.mult))
                ch(v.tensor_tensor(cen[:, t], cen[:, t], lng[:], ALU.mult))
                ch(v.tensor_tensor(cen[:, t], cen[:, t], lnb[:], ALU.add))
            for i in range(5, 10):
                split_lo(nc, g, dve, i0 + i)
            dve.wait_ge(S["yh_hi"], 1)
            v.tensor_tensor(g.xt2[1][:, 0:4], yh[:], g.xt2[0][:, 0:4].bitcast(F32), ALU.subtract).then_inc(S["yh"], 1)
            split_lo(nc, g, dve, hy0 + 2)
            dve.wait_ge(S["rwgate"], 1)
            ch(v.tensor_copy(st[:, :, 3], ps[:, 0, 0:16].rearrange("p (t h) -> p t h", t=TT)))
            for t in range(TT):
                y3 = y[:, t].rearrange("p (h e) -> p h e", e=HD)
                ch(v.tensor_tensor(y3, vt[:, t].rearrange("p (h e) -> p h e", e=HD), st[:, t, 3].unsqueeze(2).to_broadcast([P, RW_HEADS, HD]), ALU.mult))
                ch(v.tensor_tensor(y[:, t], y[:, t], cen[:, t], ALU.add))
                ins = v.tensor_tensor(y[:, t], y[:, t], ps[:, 2 + t, :], ALU.mult)
                ins.then_inc(S["yrw"], 1) if t else ch(ins)
            split_lo(nc, g, dve, hy0 + 3)
            wait_used(g, dve, hy0 + 1)
            for t in range(TT):
                bank = ps[:, 4 + 2 * t:6 + 2 * t, :].rearrange("p b n -> p (b n)")
                v.tensor_tensor(mixed[:, t], bank, gates[:, t, 0:D], ALU.mult).then_inc(S["hy_read"], 1)
            for t in range(TT):
                dve.wait_ge(S["yt_hi"], t + 1)
                lo, src = branch_rows(1, t)
                v.tensor_tensor(lo, src, branch_rows(0, t)[0].bitcast(F32), ALU.subtract).then_inc(S["yt"], 1)
            split_lo(nc, g, dve, out0)
            wait_used(g, dve, rw0 + 1)
            for t in range(TT):
                bank = ps[:, 4 + 2 * t:6 + 2 * t, :].rearrange("p b n -> p (b n)")
                ch(v.tensor_tensor(tmp[:, t], bank, gates[:, t, D:2 * D], ALU.mult))
                v.tensor_tensor(mixed[:, t], mixed[:, t], tmp[:, t], ALU.add).then_inc(S["mixed"], 1)
            for i in (out0 + 1, out0 + 2):
                split_lo(nc, g, dve, i)
            turned_lo(nc, g, dve, S, g.xt2, "mt", KC)
            split_lo(nc, g, dve, out0 + 3)
            dve.wait_ge(S["ss"], TT)
            v.tensor_scalar(ss[:, 2:4], ss[:, 0:2], 1.0 / D, EPS, ALU.mult, ALU.add).then_inc(S["mean"], 1)
            dve.wait_ge(S["root2"], 1)
            ch(v.reciprocal(ss[:, 4:6], ss[:, 4:6]))
            for t in range(TT):
                bank = ps[:, 4 + 2 * t:6 + 2 * t, :].rearrange("p b n -> p (b n)")
                ch(v.scalar_tensor_tensor(tmp[:, t], bank, ss[:, 4 + t:5 + t], post[:], ALU.mult, ALU.mult))
                ch(v.tensor_tensor(g.x[:, t], g.x[:, t], tmp[:, t], ALU.add))


def load_expert_tile(nc, g, sp, I, e, j, static=True):
    slot = g.ex_ring[:, j % ER, :]
    if j < 2 * KC:
        w = I[("exp_w1_2", "exp_w3_2")[j // KC]][0].rearrange("e (k p) f -> p (e k) f", p=P)
        src = w[:, bass.ds(KC * e + j % KC, 1), :]
        dst = slot.unsqueeze(1)
    else:
        src = I["exp_w2_2"][0].rearrange("e (h k p) n -> p k (e h) n", h=2, p=P)[:, j % KC, bass.ds(2 * e, 2), :]
        dst = slot.rearrange("p (h n) -> p h n", h=2)
    sp.dma_start(dst, src).then_inc(g.ex_loaded[j % ER], 16)


def router_phase(nc, g, I, xet, mt, aff):
    with ExitStack() as ctx:
        S = Sems(nc, ctx, "rt")

        def sb(name, shape):
            return ctx.enter_context(nc.sbuf_tensor("rt_" + name, shape, F32))
        rw, iota = sb("w", [P, KC, NE]), sb("iota", [P, CAP])
        st, at = sb("st", [P, TT, 4]), sb("at", [NE, T])
        work, top, cnt, sel = sb("work", [NE, T]), sb("top", [NE, 8]), sb("cnt", [NE, 4]), sb("sel", [NE, 3, T])
        pick, xt = sb("pick", [P, TT, NE, CAP]), sb("xt", [P, KC, T])
        ps, v = g.ps, nc.vector
        act_n, dve_n, pe_n = rms_transposed(g, nc, S, g.x, xt, g.scale[:, 2, :], g.shift[:, 2, :])
        block = ctx.enter_context(nc.Block(no_gpsimd_drain=True))

        @block.sync
        def _(sp):
            sp.dma_start(rw[:], I["router_w_2"][0].rearrange("(k p) e -> p k e", p=P)).then_inc(S["consts"], 16)
            sp.dma_start(iota[:], I["k_iota"]).then_inc(S["consts"], 16)
            for j in range(ER):
                load_expert_tile(nc, g, sp, I, 0, j)

        @block.tensor
        def _(pe):
            pe_n(pe)
            pe.wait_ge(S["consts"], 32)
            for t in range(TT):
                for k in range(KC):
                    mm = nc.tensor.matmul(ps[:, 2, NE * t:NE * t + NE], xt[:, k, P * t:P * t + P], rw[:, k], start=k == 0, stop=k == KC - 1)
            mm.then_inc(S["logits"], 1)
            pe.wait_ge(S["aff"], 1)
            for t in range(TT):
                mm = nc.tensor.transpose(ps[0:NE, 3, P * t:P * t + P], aff[:, t], g.ident[:])
            mm.then_inc(S["afft"], 1)
            pe.wait_ge(S["slots"], 1)
            for t in range(TT):
                mm = nc.tensor.transpose(ps[:, 4, NE * t:NE * t + NE], sel[:, 0, P * t:P * t + P], g.ident[0:NE, 0:NE])
            mm.then_inc(S["slott"], 1)
            pe.wait_ge(S["pick"], TT)
            for k in range(KC):
                if k >= 2:
                    pe.wait_ge(S["xet"], k - 1)
                for t in range(TT):
                    mm = nc.tensor.matmul(ps[:, 5 + k % 2, :], g.xn[:, t, P * k:P * k + P], pick[:, t].rearrange("p e s -> p (e s)"),
                                          start=t == 0, stop=t == TT - 1)
                mm.then_inc(S["gathered"], 1)

        @block.scalar
        def _(act):
            act_n(act)
            act.wait_ge(S["max"], 1)
            for t in range(TT):
                nc.scalar.activation(aff[:, t], ps[:, 2, NE * t:NE * t + NE], ACT.Exp, bias=st[:, t, 1:2],
                                     accum_out=st[:, t, 2:3]).then_inc(S["exp"], 1)

        @block.vector
        def _(dve):
            ch = Chain(dve, S["dve"])
            dve_n(dve, ch)
            dve.wait_ge(S["logits"], 1)
            ch(v.tensor_reduce(st[:, :, 0], ps[:, 2, 0:2 * NE].rearrange("p (t e) -> p t e", t=TT), AX_X, ALU.max))
            v.tensor_scalar(st[:, :, 1], st[:, :, 0], -1.0, None, ALU.mult).then_inc(S["max"], 1)
            dve.wait_ge(S["exp"], TT)
            ch(v.reciprocal(st[:, :, 3], st[:, :, 2]))
            v.tensor_tensor(aff[:], aff[:], st[:, :, 3:4].to_broadcast([P, TT, NE]), ALU.mult).then_inc(S["aff"], 1)
            dve.wait_ge(S["afft"], 1)
            ch(v.tensor_copy(at[:], ps[0:NE, 3, 0:T]))
            first_by_rank(nc, ch, at[:], work[:], top, sel, cnt, CAP, g.ones[0:NE, :])
            ch(v.tensor_tensor_scan(sel[:, 2], g.ones[0:NE, :], sel[:, 0], 0.0, ALU.mult, ALU.add))
            v.tensor_tensor(sel[:, 0], sel[:, 0], sel[:, 2], ALU.mult).then_inc(S["slots"], 1)
            dve.wait_ge(S["slott"], 1)
            dve.wait_ge(S["consts"], 32)
            ch(v.tensor_copy(mt[:], ps[:, 4, 0:2 * NE].rearrange("p (t e) -> p t e", t=TT)))
            for t in range(TT):
                v.tensor_tensor(pick[:, t], mt[:, t].unsqueeze(2).to_broadcast([P, NE, CAP]),
                                iota[:].unsqueeze(1).to_broadcast([P, NE, CAP]), ALU.is_equal).then_inc(S["pick"], 1)
            for k in range(KC):
                dve.wait_ge(S["gathered"], k + 1)
                v.tensor_scalar(xet[:, k, :], ps[:, 5 + k % 2, :], g.scale[:, 2, k:k + 1], g.shift[:, 2, k:k + 1],
                                ALU.mult, ALU.add).then_inc(S["xet"], 1)


def expert_phase(nc, g, I, xet, mt, aff, out_dram):
    with ExitStack() as ctx:
        S = Sems(nc, ctx, "ex")

        def sb(name, shape):
            return ctx.enter_context(nc.sbuf_tensor("ex_" + name, shape, F32))
        xe = sb("xe", [P, KC, CAP])
        silu, hid, ht = sb("silu", [P, 512]), sb("hid", [P, 512]), sb("ht", [P, 4, P])
        wsel, wselt = sb("wsel", [P, TT, 4, CAP]), sb("wselt", [P, T])
        iota, ye, zero = sb("iota", [P, CAP]), sb("ye", [P, 512]), sb("zero", [P, 512])
        ss, post, tmp = sb("ss", [P, 8]), sb("post", [P, D]), sb("tmp", [P, TT, D])
        ps, v = g.ps, nc.vector
        used = g.ex_used
        block = ctx.enter_context(nc.Block(no_gpsimd_drain=True))

        def loaded(e, j):
            return e * (16 * TPE // ER) + 16 * (j // ER + 1)

        @block.sync
        def _(sp):
            sp.dma_start(iota[:], I["k_iota"]).then_inc(S["consts"], 16)
            sp.dma_start(post[:], g.post_dram[:, 1]).then_inc(S["consts"], 16)
            for j in range(ER, TPE):
                sp.wait_ge(used, j - ER + 1)
                load_expert_tile(nc, g, sp, I, 0, j)
            with sp.Fori(1, NE) as e:
                for j in range(TPE):
                    sp.wait_ge(used, e * TPE + (j - ER + 1))
                    load_expert_tile(nc, g, sp, I, e, j, False)
            for t in range(TT):
                sp.wait_ge(S["done"], t + 1)
                sp.dma_start(out_dram[P * t:P * t + P, :], g.x[:, t]).then_inc(S["out"], 16)
            sp.wait_ge(S["out"], 16 * TT)

        @block.tensor
        def _(pe):
            mm_ = nc.tensor.matmul
            pe.wait_ge(S["zeroed"], 1)
            for b in range(4):
                mm_(ps[:, b, :], zero[:, 0:P], zero[:], start=True, stop=False, skip_group_check=True)
            with pe.Fori(0, NE) as e:
                pe.wait_ge(S["xe"], e + 1)
                for u in range(2):
                    for k in range(KC):
                        j = KC * u + k
                        pe.wait_ge(g.ex_loaded[j % ER], loaded(e, j))
                        for q in range(4):
                            mm = mm_(ps[32 * q:32 * q + 32, 4 + u, :], xe[:, k], g.ex_ring[:, j % ER, 512 * q:512 * q + 512],
                                     start=k == 0, stop=k == KC - 1)
                        mm.then_inc(used, 1)
                pe.wait_ge(S["wsel"], e + 1)
                for t in range(TT):
                    mm = nc.tensor.transpose(ps[:, 6, P * t:P * t + P], wsel[:, t].rearrange("p q s -> p (q s)"), g.ident[:])
                mm.then_inc(S["wturn"], 1)
                pe.wait_ge(S["wselt"], e + 1)
                pe.wait_ge(S["hid"], e + 1)
                for c in range(4):
                    mm = nc.tensor.transpose(ps[:, 6, P * c:P * c + P], hid[:, P * c:P * c + P], g.ident[:])
                mm.then_inc(S["hturn"], 1)
                pe.wait_ge(S["ht"], e + 1)
                for k in range(KC):
                    j = 2 * KC + k
                    pe.wait_ge(g.ex_loaded[j % ER], loaded(e, j))
                    w = g.ex_ring[:, j % ER, :].rearrange("p (h n) -> p h n", h=2)
                    for n in range(2):
                        for h in range(2):
                            q, f = 2 * n + h, 2 * h + k // 4
                            mm = mm_(ps[32 * q:32 * q + 32, 7, :], ht[:, k % 4, CAP * f:CAP * f + CAP], w[:, h, 512 * n:512 * n + 512],
                                     start=k == 0, stop=k == KC - 1)
                    mm.then_inc(used, 1)
                pe.wait_ge(S["ye"], e + 1)
                for t in range(TT):
                    for n in range(2):
                        mm = mm_(ps[:, 2 * t + n, :], wselt[64 * n:64 * n + 64, P * t:P * t + P], ye[64 * n:64 * n + 64, :],
                                 start=False, stop=False, skip_group_check=True)
                mm.then_inc(S["added"], 1)

        @block.scalar
        def _(act):
            with act.Fori(0, NE) as e:
                act.wait_ge(used, e * TPE + KC)
                nc.scalar.activation(silu[:], ps[:, 4, :], ACT.Silu).then_inc(S["silu"], 1)
                act.wait_ge(S["wturn"], e + 1)
                nc.scalar.copy(wselt[:], ps[:, 6, 0:T]).then_inc(S["wselt"], 1)
                act.wait_ge(S["hturn"], e + 1)
                nc.scalar.copy(ht[:], ps[:, 6, :].rearrange("p (c q) -> p c q", c=4)).then_inc(S["ht"], 1)
                act.wait_ge(used, e * TPE + TPE)
                nc.scalar.copy(ye[:], ps[:, 7, :]).then_inc(S["ye"], 1)
            act.wait_ge(S["added"], NE)
            for t in range(TT):
                nc.scalar.activation(tmp[:, t].rearrange("p (b n) -> p b n", b=2), ps[:, 2 * t:2 * t + 2, :], ACT.Square,
                                     accum_out=ss[:, t:t + 1]).then_inc(S["ss"], 1)
            act.wait_ge(S["mean"], 1)
            nc.scalar.activation(ss[:, 4:6], ss[:, 2:4], ACT.Sqrt).then_inc(S["root"], 1)

        @block.vector
        def _(dve):
            ch = Chain(dve, S["dve"])
            v.memset(zero[:], 0.0).then_inc(S["zeroed"], 1)
            dve.wait_ge(S["consts"], 32)

            def prepare(e, static):
                one = (lambda x, i, n: x[:, :, i:i + n]) if static else (lambda x, i, n: x[:, :, bass.ds(i, n)])
                v.tensor_copy(xe[:], one(xet, e * CAP, CAP)).then_inc(S["xe"], 1)
                for t in range(TT):
                    m = (mt[:, t, e:e + 1] if static else mt[:, t, bass.ds(e, 1)])
                    a = (aff[:, t, e:e + 1] if static else aff[:, t, bass.ds(e, 1)])
                    ins = v.scalar_tensor_tensor(wsel[:, t], iota[:].unsqueeze(1).to_broadcast([P, 4, CAP]), m,
                                                 a.unsqueeze(1).to_broadcast([P, 4, CAP]), ALU.is_equal, ALU.mult)
                ins.then_inc(S["wsel"], 1)

            prepare(0, True)

            def hidden(e):
                dve.wait_ge(S["silu"], e + 1)
                dve.wait_ge(used, e * TPE + 2 * KC)
                v.tensor_tensor(hid[:], ps[:, 5, :], silu[:], ALU.mult).then_inc(S["hid"], 1)

            with dve.Fori(0, NE - 1) as e:
                hidden(e)
                dve.wait_ge(S["wturn"], e + 1)
                prepare(e + 1, False)
            hidden(NE - 1)
            dve.wait_ge(S["ss"], TT)
            v.tensor_scalar(ss[:, 2:4], ss[:, 0:2], 1.0 / D, EPS, ALU.mult, ALU.add).then_inc(S["mean"], 1)
            dve.wait_ge(S["root"], 1)
            ch(v.reciprocal(ss[:, 4:6], ss[:, 4:6]))
            for t in range(TT):
                bank = ps[:, 2 * t:2 * t + 2, :].rearrange("p b n -> p (b n)")
                ch(v.scalar_tensor_tensor(tmp[:, t], bank, ss[:, 4 + t:5 + t], post[:], ALU.mult, ALU.mult))
                v.tensor_tensor(g.x[:, t], g.x[:, t], tmp[:, t], ALU.add).then_inc(S["done"], 1)


def second_block(nc, g, I, out_dram, dump=None):
    with ExitStack() as ctx:
        def sb(name, shape):
            return ctx.enter_context(nc.sbuf_tensor(name, shape, F32))
        g.mod, g.scale, g.shift, g.own = sb("mod", [P, 96]), sb("scale", [P, 3, KC]), sb("shift", [P, 3, KC]), sb("own", [P, RWC])
        with ExitStack() as rec:
            def sr(name, shape):
                return rec.enter_context(nc.sbuf_tensor(name, shape, F32))
            g.masks, g.blockones, g.blk16 = sr("masks", [P, 2, 4 * P]), sr("blockones", [P, P]), sr("blk16", [P, P])
            g.restart, g.ident2 = sr("restart", [P, T]), sr("ident2", [P, HD])
            z, yh = sr("z", [P, RWC, T]), sr("yh", [P, 4, T])
            late = sr("kmod_y", [P, 2, PAIRS * T])
            store = {"v": sr("vtok", [P, TT, RW_WIDTH]), "carry": sr("carry", [P, 2, PAIRS, HD]),
                     "kmod": late[:, 0].rearrange("p (c n) -> p c n", c=PAIRS), "y": late[:, 1].rearrange("p (t f) -> p t f", t=TT)}
            g.hs = late[:].rearrange("p a n -> p (a n)").rearrange("p (k n) -> p k n", k=4)
            g.ny = yh[:, 0:2].rearrange("p c n -> p (c n)")
            modulation_phase(nc, g, I)
            with ExitStack() as c1:
                g.xn = c1.enter_context(nc.sbuf_tensor("xn_ctx", [P, TT, D], F32))
                context_phase(nc, g, I, z)
            recurrence_phase(nc, g, I, z, store, True, "rc")
            with ExitStack() as c1:
                zh = c1.enter_context(nc.sbuf_tensor("zh", [P, HYC, T], F32))
                with ExitStack() as c2:
                    g.xn = c2.enter_context(nc.sbuf_tensor("xn_lat", [P, TT, D], F32))
                    project_phase(nc, g, I, z, zh)
                hyena_phase(nc, g, I, zh, yh)
            recurrence_phase(nc, g, I, z, store, False, "rl")
            merge_phase(nc, g, I, z, yh, store)
        if dump:
            dump("d")
        g.ex_ring = sb("ex_ring", [P, ER, WT])
        g.ex_loaded = [ctx.enter_context(nc.semaphore(f"ex_loaded_{i}")) for i in range(ER)]
        g.ex_used = ctx.enter_context(nc.semaphore("ex_used"))
        xet, mt, aff = sb("xet", [P, KC, NE * CAP]), sb("mt", [P, TT, NE]), sb("aff", [P, TT, NE])
        with ExitStack() as c1:
            g.xn = c1.enter_context(nc.sbuf_tensor("xn_moe", [P, TT, D], F32))
            router_phase(nc, g, I, xet, mt, aff)
        expert_phase(nc, g, I, xet, mt, aff, out_dram)


def constants_2():
    f32 = np.float32
    sel = np.zeros((P, 2 + P), f32)
    sel[0::32, 0], sel[1::32, 1], sel[0::32, 2:] = 1, 1, 1
    p = np.arange(P)
    same = p[:, None] // CH == p[None, :] // CH
    masks = []
    for d in range(2):
        before = (p[:, None] < p[None, :]) if d == 0 else (p[:, None] > p[None, :])
        strict = same & before
        masks.append(np.concatenate([strict, strict | np.eye(P, dtype=bool), strict.T, strict.T], axis=1))
    blk16 = p[:, None] // 16 == p[None, :] // 16
    blockones = p[:, None] // HD == p[None, :] // HD
    restart = np.ones((P, T), f32)
    restart[:, ::CH] = 0
    ident2 = np.concatenate([np.eye(HD), np.eye(HD)]).astype(f32)
    t = np.arange(T)
    ang = 2 * np.pi * ((t[:, None] * t[None, :]) % FREQ) / FREQ
    sign = (1.0 - 2.0 * (t % 2))
    fz = np.concatenate([np.cos(ang), np.sin(ang), -np.sin(ang), sign[:, None]], axis=1)
    w = np.where(t == 0, 1.0, 2.0)[:, None] / FREQ
    gi = np.concatenate([np.cos(ang) * w, np.sin(ang) * w], axis=0)
    tl = np.linspace(0.0, 1.0, T, dtype=f32)[:, None]
    an = f32(2.0 * math.pi / T) * np.arange(T, dtype=f32)[:, None]
    bands = np.linspace(1e-4, 15, 16, dtype=f32)
    feat = np.concatenate([tl, np.cos(bands * an), -np.sin(bands * an)], axis=-1)
    deltas = np.abs(np.linspace(math.log(1e-2) / 1.5, math.log(1e-2) / 0.3, HY_W, dtype=f32))
    decay = np.exp(-tl * deltas)
    decay = np.concatenate([decay, np.where(t[:, None] == 0, 0, decay)], axis=1)
    headsel = (p[:, None] // HD == np.arange(2)[None, :])
    iota = np.tile(np.arange(1, CAP + 1), (P, 1))
    out = {"k_modsel": sel, "k_masks": np.concatenate(masks, axis=1), "k_blk16": blk16, "k_blockones": blockones,
           "k_restart": restart, "k_ident2": ident2, "k_fz": fz, "k_gi": gi, "k_alt": sign[None, :] / FREQ, "k_feat": feat.T,
           "k_decay": decay, "k_headsel": headsel, "k_iota": iota}
    return {k: np.ascontiguousarray(v.astype(f32)) for k, v in out.items()}


_INS = ["x", "rel_bias", "ffn1_norm", "ffn1_w_gate", "ffn1_w_up", "ffn1_w_down", "mix_norm", "w_in", "qk_gain", "diff_lambda",
        "diff_out_norm", "w_branch_a", "w_branch_b", "w_branch_c", "w_out", "ffn2_norm", "ffn2_w_gate", "ffn2_w_up",
        "ffn2_w_down", "c_2", "ctx_2", "c_ctx_2", "mod_w_2", "mod_b_2", "norm1_pre_2", "norm1_post_2", "norm2_pre_2",
        "norm2_post_2", "w_in_2", "hy_conv_w_2", "hy_conv_b_2", "hy_ffn_w1_2", "hy_ffn_b1_2", "hy_ffn_w2_2", "hy_ffn_b2_2",
        "hy_ffn_w3_2", "hy_freq_2", "hy_bias_2", "hy_proj_2", "rw_mu_2", "rw_w0_2", "rw_w_up_2", "rw_a0_2", "rw_a_up_2",
        "rw_g_up_2", "rw_k_k_2", "rw_k_a_2", "rw_r_k_2", "rw_ln_g_2", "rw_ln_b_2", "rw_proj_2", "w_out_2", "router_w_2",
        "exp_w1_2", "exp_w3_2", "exp_w2_2"]


def two_blocks(nc, I, out):
    g = G()
    g.I = I
    g.stream = Stream()
    first_stream(g.stream, I)
    second_stream(g.stream, I)
    g.bias_dram = nc.dram_tensor("bias_by_distance", [BIAS_HEADS, DIST], F32).ap()
    g.post_dram = nc.dram_tensor("gated_post_norms", [P, 2, D], F32).ap()
    with ExitStack() as ctx:
        allocate(nc, ctx, g)
        with ExitStack() as first:
            first_block(nc, g, I, first)
        second_block(nc, g, I, out.rearrange("b t d -> (b t) d"))


def kernel(**inputs):
    import concourse.bacc as bacc
    from concourse.bass_utils import run_bass_kernel_spmd

    nc = bacc.Bacc("TRN2", target_bir_lowering=False, num_devices=1)
    arrays, I = {}, {}
    for name in _INS:
        a = np.ascontiguousarray(inputs[name])
        arrays[f"in_{name}"] = a
        I[name] = nc.dram_tensor(f"in_{name}", a.shape, mybir.dt.from_np(a.dtype), kind="ExternalInput").ap()
    for name, a in (constants() | constants_2()).items():
        arrays[name] = a
        I[name] = nc.dram_tensor(name, a.shape, mybir.dt.from_np(a.dtype), kind="ExternalInput").ap()
    out = nc.dram_tensor("out_x", (1, T, D), F32, kind="ExternalOutput").ap()
    two_blocks(nc, I, out)
    r = run_bass_kernel_spmd(nc, [arrays], core_ids=[0])
    return r.results[0]["out_x"]
```
